# Optimizing a Trainium2 kernel written in Bass

```python
import jax, jax.numpy as jnp
from jax import lax
import numpy as np
import math

D_MODEL = 1024
BATCH = 1
SEQ = 256
DEPTH = 2

CTX_LEN = 256
GRID_W = 64
HEAD_DIM = 64
AXIS_DIM = HEAD_DIM // 2
ATTN_WIDTH = D_MODEL // 2
N_Q_HEADS = ATTN_WIDTH // HEAD_DIM
N_KV_HEADS = N_Q_HEADS // 4
KV_WIDTH = N_KV_HEADS * HEAD_DIM
FOURIER_WIDTH = D_MODEL // 4
FOURIER_GROUP = 64
N_FOURIER_GROUPS = FOURIER_WIDTH // FOURIER_GROUP
GMLP_WIDTH = D_MODEL // 4
GMLP_HEAD = 64
N_GMLP_HEADS = GMLP_WIDTH // GMLP_HEAD
CHUNK = 128
Q_BLOCK = 128
MIX_WIDTH = ATTN_WIDTH + FOURIER_WIDTH + GMLP_WIDTH
IN_WIDTH = ATTN_WIDTH + 2 * KV_WIDTH + FOURIER_WIDTH + 2 * GMLP_WIDTH
SPLITS = [ATTN_WIDTH, ATTN_WIDTH + KV_WIDTH, ATTN_WIDTH + 2 * KV_WIDTH,
          ATTN_WIDTH + 2 * KV_WIDTH + FOURIER_WIDTH,
          ATTN_WIDTH + 2 * KV_WIDTH + FOURIER_WIDTH + GMLP_WIDTH]
D_FF = 4 * D_MODEL
ROPE_THETA = 10000.0
EPS = 1e-6


def rms_norm(x, g):
    xf = x.astype(jnp.float32)
    y = xf * lax.rsqrt(jnp.mean(xf * xf, axis=-1, keepdims=True) + EPS)
    return (y * g.astype(jnp.float32)).astype(x.dtype)

def modulate(h, shift, scale):
    return h * (1 + scale) + shift

def adaln(cond, w, b):
    return jnp.split(jax.nn.silu(cond) @ w + b, 6, axis=-1)

def axial_rope_tables(n, dtype):
    rows = n // GRID_W
    row = jnp.repeat(jnp.arange(rows, dtype=jnp.float32), GRID_W)
    col = jnp.tile(jnp.arange(GRID_W, dtype=jnp.float32), rows)
    inv = ROPE_THETA ** (-jnp.arange(0, AXIS_DIM, 2, dtype=jnp.float32) / AXIS_DIM)
    ar = (row[:, None] * inv)[:, None, :]
    ac = (col[:, None] * inv)[:, None, :]
    return tuple(t.astype(dtype) for t in (jnp.cos(ar), jnp.sin(ar), jnp.cos(ac), jnp.sin(ac)))

def rope_1d(x, cos, sin):
    x1, x2 = jnp.split(x, 2, axis=-1)
    return jnp.concatenate([x1 * cos - x2 * sin, x1 * sin + x2 * cos], axis=-1)

def apply_axial_rope(x, tabs):
    cr, sr, cc, sc = tabs
    xr, xc = jnp.split(x, 2, axis=-1)
    return jnp.concatenate([rope_1d(xr, cr, sr), rope_1d(xc, cc, sc)], axis=-1)

def heads(t, h):
    return t.reshape(t.shape[0], t.shape[1], h, HEAD_DIM)

def attend(q, k, v):
    s = jnp.einsum('bqkgd,btkd->bkgqt', q, k).astype(jnp.float32) * (HEAD_DIM ** -0.5)
    p = jax.nn.softmax(s, axis=-1).astype(v.dtype)
    return jnp.einsum('bkgqt,btkd->bqkgd', p, v)

def latent_attention(q, k, v):
    b, s, hq, d = q.shape
    g = hq // N_KV_HEADS
    nblk = s // Q_BLOCK
    qb = q.reshape(b, nblk, Q_BLOCK, N_KV_HEADS, g, d).transpose(1, 0, 2, 3, 4, 5)
    out = lax.map(lambda qblk: attend(qblk, k, v), qb)
    return out.transpose(1, 0, 2, 3, 4, 5).reshape(b, s, hq * d)

def context_attention(q, k, v):
    b, n, hq, d = q.shape
    g = hq // N_KV_HEADS
    return attend(q.reshape(b, n, N_KV_HEADS, g, d), k, v).reshape(b, n, hq * d)

def fourier_mix(f):
    b, n, _ = f.shape
    fg = f.astype(jnp.float32).reshape(b, n, N_FOURIER_GROUPS, FOURIER_GROUP)
    y = jnp.fft.fft2(fg, axes=(1, 3), norm='ortho').real
    return y.reshape(b, n, FOURIER_WIDTH).astype(f.dtype)

def chunk_spatial_gate(u, v, v_g, w_s, b_s):
    b, n, _ = u.shape
    u = jax.nn.gelu(u)
    vh = jax.nn.gelu(v).reshape(b, n // CHUNK, CHUNK, N_GMLP_HEADS, GMLP_HEAD)
    vh = rms_norm(vh, v_g.reshape(N_GMLP_HEADS, GMLP_HEAD))
    sp = jnp.einsum('hpq,bcqhd->bcphd', w_s, vh) + b_s.T[None, None, :, :, None]
    return u * sp.reshape(b, n, GMLP_WIDTH)

def squared_relu_mlp(h, w1, w2):
    return jnp.square(jax.nn.relu(h @ w1)) @ w2

def layer(x, ctx, c, c_ctx, w_ada, b_ada, g1, g2, w_in, q_g, k_g, v_g, w_s, b_s, w_out, w1, w2, update_ctx):
    sh1, sc1, gt1, sh2, sc2, gt2 = [m[:, None, :] for m in adaln(c, w_ada, b_ada)]
    csh1, csc1, cgt1, csh2, csc2, cgt2 = adaln(c_ctx, w_ada, b_ada)

    px = modulate(rms_norm(x, g1), sh1, sc1) @ w_in
    pc = modulate(rms_norm(ctx, g1), csh1, csc1) @ w_in
    qx, kx, vx, fx, ux, gvx = jnp.split(px, SPLITS, axis=-1)
    qc, kc, vc, fc, uc, gvc = jnp.split(pc, SPLITS, axis=-1)

    tabs = axial_rope_tables(x.shape[1], x.dtype)
    qx = apply_axial_rope(rms_norm(heads(qx, N_Q_HEADS), q_g), tabs)
    kx = apply_axial_rope(rms_norm(heads(kx, N_KV_HEADS), k_g), tabs)
    kc = rms_norm(heads(kc, N_KV_HEADS), k_g)
    vx = heads(vx, N_KV_HEADS)
    vc = heads(vc, N_KV_HEADS)
    k_all = jnp.concatenate([kc, kx], axis=1)
    v_all = jnp.concatenate([vc, vx], axis=1)

    mix_x = jnp.concatenate([latent_attention(qx, k_all, v_all),
                             fourier_mix(fx),
                             chunk_spatial_gate(ux, gvx, v_g, w_s, b_s)], axis=-1) @ w_out
    x = x + gt1 * mix_x
    x = x + gt2 * squared_relu_mlp(modulate(rms_norm(x, g2), sh2, sc2), w1, w2)

    if update_ctx:
        qc = rms_norm(heads(qc, N_Q_HEADS), q_g)
        mix_c = jnp.concatenate([context_attention(qc, kc, vc),
                                 fourier_mix(fc),
                                 chunk_spatial_gate(uc, gvc, v_g, w_s, b_s)], axis=-1) @ w_out
        ctx = ctx + cgt1 * mix_c
        ctx = ctx + cgt2 * squared_relu_mlp(modulate(rms_norm(ctx, g2), csh2, csc2), w1, w2)
    return x, ctx

def first_inputs(seed: int = 0) -> dict:
    key = jax.random.key(seed)
    ks = jax.random.split(key, 17)
    f32 = jnp.float32
    n = lambda k, s: jax.random.normal(k, s, dtype=f32)
    return {
        'x': n(ks[0], (BATCH, SEQ, D_MODEL)),
        'c': n(ks[1], (BATCH, D_MODEL)),
        'ctx': n(ks[2], (BATCH, CTX_LEN, D_MODEL)),
        'c_ctx': n(ks[3], (D_MODEL,)),
        'w_ada': n(ks[4], (DEPTH, D_MODEL, 6 * D_MODEL)) * (0.5 * D_MODEL ** -0.5),
        'b_ada': n(ks[5], (DEPTH, 6 * D_MODEL)) * 0.01,
        'norm1_g': 1.0 + 0.02 * n(ks[6], (DEPTH, D_MODEL)),
        'norm2_g': 1.0 + 0.02 * n(ks[7], (DEPTH, D_MODEL)),
        'w_in': n(ks[8], (DEPTH, D_MODEL, IN_WIDTH)) * D_MODEL ** -0.5,
        'q_norm_g': 1.0 + 0.02 * n(ks[9], (DEPTH, HEAD_DIM)),
        'k_norm_g': 1.0 + 0.02 * n(ks[10], (DEPTH, HEAD_DIM)),
        'gmlp_v_g': 1.0 + 0.02 * n(ks[11], (DEPTH, GMLP_WIDTH)),
        'w_spatial': n(ks[12], (DEPTH, N_GMLP_HEADS, CHUNK, CHUNK)) * CHUNK ** -0.5,
        'b_spatial': n(ks[13], (DEPTH, N_GMLP_HEADS, CHUNK)) * 0.02,
        'w_out': n(ks[14], (DEPTH, MIX_WIDTH, D_MODEL)) * MIX_WIDTH ** -0.5,
        'w_mlp1': n(ks[15], (DEPTH, D_MODEL, D_FF)) * D_MODEL ** -0.5,
        'w_mlp2': n(ks[16], (DEPTH, D_FF, D_MODEL)) * D_FF ** -0.5,
    }

def first_block(x, c, ctx, c_ctx, w_ada, b_ada, norm1_g, norm2_g, w_in, q_norm_g, k_norm_g, gmlp_v_g,
              w_spatial, b_spatial, w_out, w_mlp1, w_mlp2):
    for l in range(DEPTH):
        x, ctx = layer(x, ctx, c, c_ctx, w_ada[l], b_ada[l], norm1_g[l], norm2_g[l], w_in[l],
                       q_norm_g[l], k_norm_g[l], gmlp_v_g[l], w_spatial[l], b_spatial[l], w_out[l],
                       w_mlp1[l], w_mlp2[l], l < DEPTH - 1)
    return x


MOBA_HEADS = 4
DIFF_HEADS = 4
DSA_HEADS = 4
DIFF_V_DIM = 2 * HEAD_DIM
IDX_HEADS = 8
IDX_DIM = 64
MOBA_BLOCK = 256
MOBA_TOPK = 3
DSA_TOPK_MAX = 256
MOBA_Q_CHUNK = 32
D_FF_2 = -(-8 * D_MODEL // (3 * 256)) * 256

MOBA_W = MOBA_HEADS * HEAD_DIM
DIFF_QK_W = DIFF_HEADS * 2 * HEAD_DIM
DIFF_V_W = DIFF_HEADS * DIFF_V_DIM
DSA_W = DSA_HEADS * HEAD_DIM
IDX_Q_W = IDX_HEADS * IDX_DIM
MIX_W = MOBA_W + DIFF_V_W + DSA_W
IN_COLS = 3 * MOBA_W + 2 * DIFF_QK_W + DIFF_V_W + 3 * DSA_W + IDX_Q_W + IDX_DIM + IDX_HEADS


def rms_norm_2(x, g):
    xf = x.astype(jnp.float32)
    y = xf * lax.rsqrt(jnp.mean(xf * xf, axis=-1, keepdims=True) + EPS)
    return (y * g.astype(jnp.float32)).astype(x.dtype)

def rope_tables(seq, dim):
    inv = 1.0 / (ROPE_THETA ** (jnp.arange(0, dim, 2, dtype=jnp.float32) / dim))
    ang = jnp.arange(seq, dtype=jnp.float32)[:, None] * inv[None, :]
    return jnp.cos(ang), jnp.sin(ang)

def apply_rope(x, cos, sin):
    x1, x2 = jnp.split(x, 2, axis=-1)
    c = cos.astype(x.dtype)
    s = sin.astype(x.dtype)
    return jnp.concatenate([x1 * c - x2 * s, x1 * s + x2 * c], axis=-1)

def split_heads(t, n_heads):
    b, s, _ = t.shape
    return t.reshape(b, s, n_heads, -1).transpose(0, 2, 1, 3)

def merge_heads(t):
    b, h, s, d = t.shape
    return t.transpose(0, 2, 1, 3).reshape(b, s, h * d)

def moba_attention(q, k, v):
    B, H, S, D = q.shape
    nb = -(-S // MOBA_BLOCK)
    pad = nb * MOBA_BLOCK - S
    kb = jnp.pad(k, ((0, 0), (0, 0), (0, pad), (0, 0))).reshape(B, H, nb, MOBA_BLOCK, D)
    vb = jnp.pad(v, ((0, 0), (0, 0), (0, pad), (0, 0))).reshape(B, H, nb, MOBA_BLOCK, D)
    k_mean = jnp.mean(kb.astype(jnp.float32), axis=3).astype(k.dtype)
    n_sel = min(MOBA_TOPK, nb - 1)
    scale = D ** -0.5
    blk_ids = jnp.arange(nb)
    own_off = jnp.arange(MOBA_BLOCK)
    gather = jax.vmap(jax.vmap(lambda t, i: t[i]))

    def chunk(i):
        start = i * MOBA_Q_CHUNK
        qc = lax.dynamic_slice_in_dim(q, start, MOBA_Q_CHUNK, axis=2)
        qpos = start + jnp.arange(MOBA_Q_CHUNK)
        cur = start // MOBA_BLOCK
        k_own = lax.dynamic_index_in_dim(kb, cur, axis=2, keepdims=False)
        v_own = lax.dynamic_index_in_dim(vb, cur, axis=2, keepdims=False)
        own_pos = cur * MOBA_BLOCK + own_off
        s_own = jnp.einsum('bhcd,bhkd->bhck', qc, k_own).astype(jnp.float32) * scale
        s_own = jnp.where(own_pos[None, :] <= qpos[:, None], s_own, -jnp.inf)
        if n_sel == 0:
            p_own = jax.nn.softmax(s_own, axis=-1).astype(v.dtype)
            return jnp.einsum('bhck,bhkd->bhcd', p_own, v_own)
        gate = jnp.einsum('bhcd,bhnd->bhcn', qc, k_mean).astype(jnp.float32)
        gate = jnp.where(blk_ids < cur, gate, -jnp.inf)
        _, sel = lax.top_k(gate, n_sel)
        sel_ok = jnp.arange(n_sel) < cur
        k_sel = gather(kb, sel)
        v_sel = gather(vb, sel)
        s_sel = jnp.einsum('bhcd,bhcnkd->bhcnk', qc, k_sel).astype(jnp.float32) * scale
        s_sel = jnp.where(sel_ok[:, None], s_sel, -jnp.inf).reshape(B, H, MOBA_Q_CHUNK, n_sel * MOBA_BLOCK)
        p = jax.nn.softmax(jnp.concatenate([s_sel, s_own], axis=-1), axis=-1).astype(v.dtype)
        p_sel = p[..., :n_sel * MOBA_BLOCK].reshape(B, H, MOBA_Q_CHUNK, n_sel, MOBA_BLOCK)
        p_own = p[..., n_sel * MOBA_BLOCK:]
        return (jnp.einsum('bhcnk,bhcnkd->bhcd', p_sel, v_sel)
                + jnp.einsum('bhck,bhkd->bhcd', p_own, v_own))

    out = lax.map(chunk, jnp.arange(S // MOBA_Q_CHUNK))
    return out.transpose(1, 2, 0, 3, 4).reshape(B, H, S, D)

def diff_attention(q1, q2, k1, k2, v, lam):
    B, H, S, D = q1.shape
    scale = D ** -0.5
    kpos = jnp.arange(S)

    def block(i):
        start = i * Q_BLOCK
        qpos = start + jnp.arange(Q_BLOCK)
        mask = kpos[None, :] <= qpos[:, None]

        def probs(qf, kf):
            qb = lax.dynamic_slice_in_dim(qf, start, Q_BLOCK, axis=2)
            s = jnp.einsum('bhqd,bhkd->bhqk', qb, kf).astype(jnp.float32) * scale
            return jax.nn.softmax(jnp.where(mask, s, -jnp.inf), axis=-1)

        a = probs(q1, k1) - lam * probs(q2, k2)
        return jnp.einsum('bhqk,bhkv->bhqv', a.astype(v.dtype), v)

    out = lax.map(block, jnp.arange(S // Q_BLOCK))
    return out.transpose(1, 2, 0, 3, 4).reshape(B, H, S, v.shape[-1])

def dsa_attention(q, k, v, iq, ik, iw):
    B, H, S, D = q.shape
    n_top = min(DSA_TOPK_MAX, S // 4)
    scale = D ** -0.5
    kpos = jnp.arange(S)
    gather = jax.vmap(lambda t, i: t[:, i])

    def chunk(i):
        start = i * Q_BLOCK
        qpos = start + jnp.arange(Q_BLOCK)
        iqc = lax.dynamic_slice_in_dim(iq, start, Q_BLOCK, axis=2)
        iwc = lax.dynamic_slice_in_dim(iw, start, Q_BLOCK, axis=1)
        logits = jnp.einsum('bhcd,bsd->bhcs', iqc, ik).astype(jnp.float32) * (IDX_DIM ** -0.5)
        score = jnp.einsum('bch,bhcs->bcs', iwc.astype(jnp.float32), jax.nn.relu(logits))
        score = jnp.where(kpos[None, :] <= qpos[:, None], score, -jnp.inf)
        _, sel = lax.top_k(score, n_top)
        sel_ok = sel <= qpos[None, :, None]
        qc = lax.dynamic_slice_in_dim(q, start, Q_BLOCK, axis=2)
        k_sel = gather(k, sel)
        v_sel = gather(v, sel)
        s = jnp.einsum('bhcd,bhcnd->bhcn', qc, k_sel).astype(jnp.float32) * scale
        s = jnp.where(sel_ok[:, None], s, -jnp.inf)
        p = jax.nn.softmax(s, axis=-1).astype(v.dtype)
        return jnp.einsum('bhcn,bhcnd->bhcd', p, v_sel)

    out = lax.map(chunk, jnp.arange(S // Q_BLOCK))
    return out.transpose(1, 2, 0, 3, 4).reshape(B, H, S, D)

def second_inputs(seed: int = 0) -> dict:
    key = jax.random.key(seed)
    ks = jax.random.split(key, 12)
    f32 = jnp.float32

    def nrm(k, shape, scale):
        return jax.random.normal(k, shape, f32) * scale

    return {
        "x": nrm(ks[0], (BATCH, SEQ, D_MODEL), 1.0),
        "attn_norm_g": 1.0 + nrm(ks[1], (DEPTH, D_MODEL), 0.05),
        "w_in": nrm(ks[2], (DEPTH, D_MODEL, IN_COLS), D_MODEL ** -0.5),
        "q_norm_g": 1.0 + nrm(ks[3], (DEPTH, 3, HEAD_DIM), 0.05),
        "k_norm_g": 1.0 + nrm(ks[4], (DEPTH, 3, HEAD_DIM), 0.05),
        "diff_lambda": nrm(ks[5], (DEPTH, 4, HEAD_DIM), 0.1),
        "diff_subln_g": 1.0 + nrm(ks[6], (DEPTH, DIFF_V_DIM), 0.05),
        "w_out": nrm(ks[7], (DEPTH, MIX_W, D_MODEL), MIX_W ** -0.5),
        "ffn_norm_g": 1.0 + nrm(ks[8], (DEPTH, D_MODEL), 0.05),
        "w_gate": nrm(ks[9], (DEPTH, D_MODEL, D_FF_2), D_MODEL ** -0.5),
        "w_up": nrm(ks[10], (DEPTH, D_MODEL, D_FF_2), D_MODEL ** -0.5),
        "w_down": nrm(ks[11], (DEPTH, D_FF_2, D_MODEL), D_FF_2 ** -0.5),
    }

def second_block(x, attn_norm_g, w_in, q_norm_g, k_norm_g, diff_lambda, diff_subln_g,
              w_out, ffn_norm_g, w_gate, w_up, w_down):
    S = x.shape[1]
    cos, sin = rope_tables(S, HEAD_DIM)
    sizes = [MOBA_W] * 3 + [DIFF_QK_W, DIFF_QK_W, DIFF_V_W] + [DSA_W] * 3 + [IDX_Q_W, IDX_DIM, IDX_HEADS]
    offsets = []
    acc = 0
    for sz in sizes[:-1]:
        acc += sz
        offsets.append(acc)

    for l in range(DEPTH):
        h = rms_norm_2(x, attn_norm_g[l])
        proj = h @ w_in[l]
        (mq, mk, mv, dq, dk, dv, sq, sk, sv, iq, ik, iw) = jnp.split(proj, offsets, axis=-1)
        qg, kg = q_norm_g[l], k_norm_g[l]

        def qk(t, nh, g):
            return apply_rope(rms_norm_2(split_heads(t, nh), g), cos, sin)

        moba = moba_attention(qk(mq, MOBA_HEADS, qg[0]), qk(mk, MOBA_HEADS, kg[0]),
                              split_heads(mv, MOBA_HEADS))

        dq_h = qk(dq, 2 * DIFF_HEADS, qg[1])
        dk_h = qk(dk, 2 * DIFF_HEADS, kg[1])
        lam_init = 0.8 - 0.6 * math.exp(-0.3 * l)
        lp = diff_lambda[l].astype(jnp.float32)
        lam = jnp.exp(jnp.sum(lp[0] * lp[1])) - jnp.exp(jnp.sum(lp[2] * lp[3])) + lam_init
        diff = diff_attention(dq_h[:, 0::2], dq_h[:, 1::2], dk_h[:, 0::2], dk_h[:, 1::2],
                              split_heads(dv, DIFF_HEADS), lam)
        diff = rms_norm_2(diff, diff_subln_g[l]) * (1.0 - lam_init)

        iq_h = apply_rope(split_heads(iq, IDX_HEADS), cos, sin)
        ik_r = apply_rope(ik, cos, sin)
        dsa = dsa_attention(qk(sq, DSA_HEADS, qg[2]), qk(sk, DSA_HEADS, kg[2]),
                            split_heads(sv, DSA_HEADS), iq_h, ik_r,
                            iw * (IDX_HEADS ** -0.5))

        mix = jnp.concatenate([merge_heads(moba), merge_heads(diff), merge_heads(dsa)], axis=-1)
        x = x + mix @ w_out[l]

        h2 = rms_norm_2(x, ffn_norm_g[l])
        x = x + (jax.nn.silu(h2 @ w_gate[l]) * (h2 @ w_up[l])) @ w_down[l]
    return x


def setup_inputs(seed=0):
    out = dict(first_inputs(seed))
    for name, value in second_inputs(seed + 1).items():
        if name != "x":
            out[name + "_2"] = value
    return out


def reference(
    x, c, ctx, c_ctx, w_ada, b_ada, norm1_g, norm2_g, w_in, q_norm_g, k_norm_g, gmlp_v_g,
    w_spatial, b_spatial, w_out, w_mlp1, w_mlp2, attn_norm_g_2, w_in_2, q_norm_g_2, k_norm_g_2,
    diff_lambda_2, diff_subln_g_2, w_out_2, ffn_norm_g_2, w_gate_2, w_up_2, w_down_2,
):
    x = first_block(
        x, c, ctx, c_ctx, w_ada, b_ada, norm1_g, norm2_g, w_in, q_norm_g, k_norm_g, gmlp_v_g,
        w_spatial, b_spatial, w_out, w_mlp1, w_mlp2,
    )
    return second_block(
        x, attn_norm_g_2, w_in_2, q_norm_g_2, k_norm_g_2, diff_lambda_2, diff_subln_g_2,
        w_out_2, ffn_norm_g_2, w_gate_2, w_up_2, w_down_2,
    )


_drawn_inputs = setup_inputs


def setup_inputs(seed=0):
    import zlib

    import numpy as np

    out = dict(_drawn_inputs(seed))
    spreads = {}
    factors = {'norm1_g': 5.821,
     'norm2_g': 3.144,
     'q_norm_g': 8.0,
     'k_norm_g': 8.0,
     'gmlp_v_g': 8.0,
     'b_spatial': 8.0,
     'q_norm_g_2': 11.096,
     'k_norm_g_2': 10.555,
     'diff_lambda_2': 3.998,
     'diff_subln_g_2': 8.0,
     'ffn_norm_g_2': 7.93}
    for name, (base, spread) in spreads.items():
        noise = np.random.default_rng([zlib.crc32(name.encode()), seed]).standard_normal(out[name].shape)
        drawn = base * np.exp(spread * noise) if base else spread * noise
        out[name] = __import__('jax').numpy.asarray(drawn.astype(out[name].dtype))
    for name, factor in factors.items():
        out[name] = (out[name] * factor).astype(out[name].dtype)
    return out
```

```python
from contextlib import ExitStack

import numpy as np

import concourse.bass as bass
from concourse import mybir

F32 = mybir.dt.float32
F32R = mybir.dt.float32r
BF16 = mybir.dt.bfloat16
ALU = mybir.AluOpType
ACT = mybir.ActivationFunctionType
AX = mybir.AxisListType

P = 128
D = 1024
KT = D // P
NT = 256
TT = NT // P
DH = 64
EPS = 1e-6
DEPTH = 2
MASKED = -1.0e30
TAKEN = -3.0e38
RAW, SPLIT = 4, 4
BODY = 4
CW = 256

Q1, K1, V1, F1, U1, G1, IN1 = 0, 512, 640, 768, 1024, 1280, 1536
NQ1, NKV1 = 8, 2
FF1 = 4096
MQ, MK, MV, DQ, DK, DV, SQ, SK, SV, IQ, IK, IW, IN2 = (
    0, 256, 512, 768, 1280, 1792, 2304, 2560, 2816, 3072, 3584, 3648, 3656)
FF2 = 2816
IH = 8
TOPK = NT // 4

CONSTS = dict(ident=P, dft_n=TT * 2 * NT, dft_c=P, dft_s=P, cos1=TT * DH, sin1=TT * DH, cos2=TT * DH, sin2=TT * DH,
              mask=NT, sel=2)


def constant_table():
    t = {k: np.zeros((P, w), np.float32) for k, w in CONSTS.items()}
    t["ident"][:] = np.eye(P)
    n = np.arange(NT)
    ang = 2 * np.pi * ((n[:, None] * n[None, :]) % NT) / NT
    cs = np.concatenate([np.cos(ang), np.sin(ang)], 1)
    t["dft_n"][:] = cs.reshape(TT, P, 2 * NT).transpose(1, 0, 2).reshape(P, -1)
    d = np.arange(DH)
    ang = 2 * np.pi * ((d[:, None] * d[None, :]) % DH) / DH
    norm = 1.0 / np.sqrt(NT * DH)
    t["dft_c"][:] = np.kron(np.eye(2), np.cos(ang)) * norm
    t["dft_s"][:] = np.kron(np.eye(2), -np.sin(ang)) * norm
    pos = np.arange(NT, dtype=np.float32)
    inv = (np.float32(10000.0) ** (-np.arange(0, 32, 2, dtype=np.float32) / np.float32(32))).astype(np.float32)
    row, col = np.floor(pos / 64)[:, None] * inv, (pos % 64)[:, None] * inv
    inv2 = (np.float32(1.0) / (np.float32(10000.0) ** (np.arange(0, 64, 2, dtype=np.float32) / np.float32(64))))
    ang2 = pos[:, None] * inv2.astype(np.float32)
    for name, f, a in (("cos1", np.cos, 0), ("sin1", np.sin, 1), ("cos2", np.cos, 0), ("sin2", np.sin, 1)):
        parts = [row, row, col, col] if name[-1] == "1" else [ang2, ang2]
        v = [f(x) * (-1 if a and i % 2 == 0 else 1) for i, x in enumerate(parts)]
        t[name][:] = np.concatenate(v, 1).reshape(TT, P, DH).transpose(1, 0, 2).reshape(P, -1)
    t["mask"][:, P:] = np.where(np.arange(P)[None, :] <= np.arange(P)[:, None], 0, MASKED)
    t["sel"][0:5] = [[1, 0], [0, 1], [1, 0], [0, 1], [1, 1]]
    return np.concatenate([t[k] for k in CONSTS], 1).astype(np.float32)


class Tally:

    def __init__(self):
        self.n, self.it, self.step, self.last = {}, None, {}, {}

    def __call__(self, name, k=0):
        v = self.n.get(name, 0) + k
        s = self.step.get(name, 0)
        return v + self.it * s if self.it is not None and s else v

    def static(self, name):
        return self.n.get(name, 0)

    def add(self, name, k=1):
        self.n[name] = self.n.get(name, 0) + k

    def begin(self, it, step):
        self.it, self.step, self.last = it, step, dict(self.n)

    def end(self, times):
        for name, v in list(self.n.items()):
            d = v - self.last.get(name, 0)
            assert d == self.step.get(name, 0), (name, d, self.step.get(name, 0))
            self.n[name] = v + d * (times - 1)
        self.it, self.step = None, {}


def run_chunks(eng, n, count, per_chunk, body, tail=0, least=1):
    m = count - tail
    head = (m - 1) % BODY + 1 if m else 0
    while head < min(least, m):
        head += BODY
    times = (m - head) // BODY
    for j in range(head):
        body(j, j)
    if times == 1:
        for j in range(head, m):
            body(j, j)
    elif times > 1:
        with eng.Fori(0, times) as it:
            n.begin(it, {k: v * BODY for k, v in per_chunk.items()})
            for j in range(BODY):
                body(head + j, it * BODY + (head + j))
            n.end(times)
    for j in range(m, count):
        body(j, j)


def build(nc, A, consts, out, debug=None):
    top = ExitStack()
    with top:
        def sb(name, shape, dt=F32, stack=top):
            return stack.enter_context(nc.sbuf_tensor(name, shape, dt))

        def sem(name):
            return top.enter_context(nc.semaphore(name))

        residual = sb("residual", [P, KT, 2 * NT])
        act_hi = sb("act_hi", [P, KT, NT], F32R)
        act_lo = sb("act_lo", [P, KT, NT], F32R)
        raw = sb("raw", [P, RAW, 2048])
        w_hi = sb("w_hi", [P, SPLIT, 1024], F32R)
        w_lo = sb("w_lo", [P, SPLIT, 1024], F32R)
        const = sb("const", [P, sum(CONSTS.values())])
        cols, at = {}, 0
        for name, w in CONSTS.items():
            cols[name] = const[:, at:at + w]
            at += w
        ident, sel, mask = cols["ident"], cols["sel"], cols["mask"]
        dft_n = cols["dft_n"].rearrange("p (t n) -> p t n", t=TT)
        rope = {b: [cols[f"{f}{b}"].rearrange("p (t d) -> p t d", t=TT) for f in ("cos", "sin")] for b in (1, 2)}
        ones = sb("ones", [P, P])
        neg_half = sb("neg_half", [P, DH])
        cond = sb("cond", [P, KT, P], F32R)
        k_t = sb("k_t", [P, NKV1, 2 * NT])
        v_rows = sb("v_rows", [P, 2 * TT, NKV1 * DH])
        mod = sb("mod", [P, 48, 2])
        mscale = sb("mscale", [P, 2, KT, 2])
        norm_g = sb("norm_g", [P, 2, KT])
        gains1 = sb("gains1", [P, 2 * DH + 256])
        w_sp = sb("w_sp", [P, 4, P])
        b_sp = sb("b_sp", [P, 4])
        norm2_g = sb("norm2_g", [P, 2, KT])
        gains2 = sb("gains2", [P, 3, 2, DH])
        lam_in = sb("lam_in", [P, 4 * DH])
        sub_g = sb("sub_g", [P, 2 * DH])
        variance = sb("variance", [P, DH])
        rstd = sb("rstd", [P, DH])
        diag = sb("diag", [P, TT, P])
        ident_b = sb("ident_b", [P, P], BF16)
        mask_b = sb("mask_b", [P, P], BF16)
        neg_max = sb("neg_max", [P, 64])
        total = sb("total", [P, 64])
        lam = sb("lam", [P, 8])
        best = sb("best", [P, 8])

        with ExitStack() as s:
            wide = sb("wide", [P, KT, NT], stack=s)
            rows_in = sb("rows_in", [P, 2 * TT, D], stack=s)
            cond_raw = sb("cond_raw", [P, 4, KT, 2], stack=s)
            mod_rows = sb("mod_rows", [5, 6 * D], stack=s)
        with ExitStack() as s:
            proj1 = sb("proj1", [P, TT, IN1], stack=s)
            q_t = sb("q_t", [P, NQ1 // 2, NT], stack=s)
            kdup = sb("kdup", [P, TT, 2 * NKV1, DH], stack=s)
            probs1 = sb("probs1", [P, 4, 2 * NT], stack=s)
            probs_t1 = sb("probs_t1", [P, 2, 2 * TT, P], stack=s)
            four = sb("four", [P, 2, 2 * NT], stack=s)
            w_sp_t = sb("w_sp_t", [P, 4, P], stack=s)
            gates = sb("gates", [P, TT, 512], stack=s)
            gtmp = sb("gtmp", [P, TT, 512], stack=s)
            tmp1 = [sb(f"tmp1{i}", [P, 512], stack=s) for i in range(3)]
        with ExitStack() as s:
            proj2 = sb("proj2", [P, TT, IN2], stack=s)
            pairs_t = sb("pairs_t", [P, 21, NT], stack=s)
            ikdup = sb("ikdup", [P, TT, 2, DH], stack=s)
            seen = sb("seen", [P, TT, NT], BF16, stack=s)
            scratch = sb("scratch", [P, 3, 1024], stack=s)
        tmp2 = [scratch[:, i, :] for i in range(3)]
        probs2 = scratch[:, 0, :].rearrange("p (s n) -> p s n", s=4)
        probs_t2 = scratch[:, 1, 0:512].rearrange("p (s k n) -> p s k n", s=2, k=TT)
        relu_t = scratch[:, 1, 512:1024].rearrange("p (s n) -> p s n", s=2)
        diff_rows = scratch[:, 2, :].rearrange("p (t n) -> p t n", t=TT)
        score = scratch[:, 2, 0:NT]
        with ExitStack() as s:
            hid_hi = sb("hid_hi", [P, FF1 // P, NT], F32R, stack=s)
            hid_lo = sb("hid_lo", [P, FF1 // P, NT], F32R, stack=s)
            fa = sb("fa", [P, 2, 2 * NT], stack=s)
            fb = sb("fb", [P, 2, 2 * NT], stack=s)

        bank = [top.enter_context(nc.psum_tensor(f"bank{i}", [P, 512], F32)) for i in range(8)]

        raw_loaded = [sem(f"raw_loaded{i}") for i in range(RAW)]
        hi_ready = sem("hi_ready")
        lo_ready = sem("lo_ready")
        multiplied = sem("multiplied")
        drained_act = sem("drained_act")
        squared = sem("squared")
        relued = sem("relued")
        gate_exp = sem("gate_exp")
        gated = sem("gated")
        gate_hi = sem("gate_hi")
        hidden = sem("hidden")
        residual_new = sem("residual_new")
        squares = sem("squares")
        sums = sem("sums")
        rstd_diag = sem("rstd_diag")
        rstd_wide = sem("rstd_wide")
        var_ready = sem("var_ready")
        rstd_ready = sem("rstd_ready")
        modulated = sem("modulated")
        norm_hi = sem("norm_hi")
        norm_lo = sem("norm_lo")
        consts_in = sem("consts_in")
        inputs_in = sem("inputs_in")
        cond_in = sem("cond_in")
        params_in = sem("params_in")
        preset = sem("preset")
        cond_exp = sem("cond_exp")
        cond_hi = sem("cond_hi")
        cond_ready = sem("cond_ready")
        mod_full = sem("mod_full")
        mod_ready = sem("mod_ready")
        turned = sem("turned")
        turned_out = sem("turned_out")
        rows_ready = sem("rows_ready")
        v_kept = sem("v_kept")
        scored = sem("scored")
        max_ready = sem("max_ready")
        exped = sem("exped")
        prob_ready = sem("prob_ready")
        prob_turned = sem("prob_turned")
        prob_t = sem("prob_t")
        mixed = sem("mixed")
        mix_hi = sem("mix_hi")
        mix_lo = sem("mix_lo")
        dft_full = sem("dft_full")
        dft_out = sem("dft_out")
        mix_full = sem("mix_full")
        gelu_in = sem("gelu_in")
        gelu_tanh = sem("gelu_tanh")
        spatial = sem("spatial")
        logit_full = sem("logit_full")
        logit_relu = sem("logit_relu")
        logit_used = sem("logit_used")
        seen_ready = sem("seen_ready")
        lam_exp = sem("lam_exp")
        lam_sums = sem("lam_sums")
        diff_drained = sem("diff_drained")
        final_rows = sem("final_rows")
        stored = sem("stored")
        act_order = sem("act_order")
        dve_order = sem("dve_order")
        block = top.enter_context(nc.Block())

        A_ = A
        TOTAL = [0]

        def program(ph):
            ph.load()
            ph.params(0)
            for l in range(DEPTH):
                ph.ada(l)
                ph.modulation(l)
                for s in (1, 0):
                    kv_only = s == 1 and l == DEPTH - 1
                    ph.norm(s, 1, 0)
                    if kv_only:
                        ph.up("rows1", 1, dict(w=A_["w_in"], l=l, base=K1))
                    else:
                        ph.up("rows1", IN1 // CW, dict(w=A_["w_in"], l=l, base=0))
                    ph.heads1(s, kv_only)
                    if kv_only:
                        continue
                    ph.attend1(s)
                    ph.fourier()
                    ph.spatial_gate()
                    ph.down("mix", D // P // 2, dict(w=A_["w_out"], l=l), s, 16)
                    if debug == ("wout", l, s): return ph.finish()
                    ph.norm(s, 1, 1)
                    ph.up("relu2", FF1 // CW, dict(w=A_["w_mlp1"], l=l, base=0))
                    ph.down("hidden", FF1 // P // 2, dict(w=A_["w_mlp2"], l=l), s, 40)
                    if debug == ("layer", l, s): return ph.finish()
                if l + 1 < DEPTH:
                    ph.params(l + 1)
            for l in range(DEPTH):
                ph.params2(l)
                ph.norm(0, 2, 0)
                ph.up("rows2", -(-IN2 // CW), dict(w=A_["w_in_2"], l=l, base=0))
                ph.heads2(l)
                ph.index2()
                ph.attend2(l)
                ph.down("mix", D // P // 2, dict(w=A_["w_out_2"], l=l), 0, None)
                ph.norm(0, 2, 1)
                ph.up("silu", FF2 // P, dict(w=A_["w_gate_2"], w2=A_["w_up_2"], l=l, base=0))
                ph.down("hidden", FF2 // P // 2, dict(w=A_["w_down_2"], l=l), 0, None, last=l == DEPTH - 1)
                if debug == ("layer2", l, 0): return ph.finish()
            ph.finish()

        PER_CHUNK = {}

        def tiles(ap, k):
            return ap.rearrange("p (k n) -> p k n", k=k)

        class Phases:

            def __init__(self, eng):
                self.e, self.n = eng, Tally()
                self.behind = False

            def tail(self, count):
                return BODY if self.n.static("chunks") + count == TOTAL[0] else 0

            def load(self): self.n.add("turned", 8)
            def params(self, l): self.n.add("params", 1)
            params2 = params
            def ada(self, l): self.chunks("ada", 24)
            def up(self, kind, count, w): self.chunks(kind, count)
            def down(self, kind, count, w, s, gate, last=False):
                self.chunks("down", count)
                self.n.add("residual", KT)

            def chunks(self, kind, count):
                self.n.add("chunks", count)
                if kind in ("rows1", "rows2", "ada"):
                    self.n.add("drained_act", count)
                if kind == "relu2":
                    self.n.add("drained_act", count)
                    self.n.add("hidden", count)
                if kind == "silu":
                    self.n.add("gated", count)
                    self.n.add("hidden", count)

            def modulation(self, l): self.n.add("mod", 1)
            def norm(self, s, b, which):
                self.n.add("norm", 1)
                self.n.add("pow", 1)
            def heads1(self, s, kv_only):
                self.n.add("heads", 1)
                self.n.add("pow", TT * (1 if kv_only else 2))
                self.n.add("turned", 1 if kv_only else 3)
            def attend1(self, s):
                self.n.add("scores", 16)
                self.n.add("items", 16)
                self.n.add("mix", 2)
            def fourier(self):
                self.n.add("fourier", 1)
                self.n.add("mix", 1)
            def spatial_gate(self):
                self.n.add("gmlp", 1)
                self.n.add("pow", 1)
                self.n.add("turned", 1)
                self.n.add("mix", 1)
            def heads2(self, l):
                self.n.add("heads", 1)
                self.n.add("pow", 3 * TT)
                self.n.add("turned", 11)
            def index2(self): self.n.add("logits", IH * TT)
            def attend2(self, l):
                self.n.add("scores", 32)
                self.n.add("items", 24)
                self.n.add("mix", 4)
                self.n.add("pow", TT)
            def finish(self): pass

        def items1(s):
            keys = TT if s == 1 else 2 * TT
            out = []
            for h in range(NQ1):
                kv, half = h // (NQ1 // NKV1), DH * (h % 2)
                for qt in range(TT):
                    q = q_t[half:half + DH, h // 2, qt * P:(qt + 1) * P]
                    k = k_t[half:half + DH, kv, 0:keys * P]
                    v = [v_rows[:, i, kv * DH:(kv + 1) * DH] for i in range(keys)]
                    o = bank[6 + h // 4][half:half + DH, (h // 2 % 2) * NT + qt * P:(h // 2 % 2) * NT + (qt + 1) * P]
                    out.append(dict(scores=[(q, k, None)], keys=keys, v=v, o=o,
                                    done=(6 + h // 4, 2 * (h // 4)) if h % 4 == 3 and qt == TT - 1 else None))
            return out

        PAIR = dict(mq=0, mk=2, dq=4, dk=8, sq=12, sk=14, iq=16, ik=20)

        def pair(name, h, lo, hi):
            half = DH * (h % 2)
            return pairs_t[half:half + DH, PAIR[name] + h // 2, lo:hi]

        def causal(qt):
            return mask[:, P:2 * P] if qt == 0 else mask[:, :]

        def items2():
            out = []
            for h in range(4):
                for qt in range(TT):
                    n = (qt + 1) * P
                    half = DH * (h % 2)
                    o = bank[6][half:half + DH, h // 2 * NT + qt * P:h // 2 * NT + (qt + 1) * P]
                    out.append(dict(scores=[(pair("mq", h, qt * P, n), pair("mk", h, 0, n), mask_b[:])], keys=qt + 1,
                                    v=[proj2[:, i, MV + h * DH:MV + (h + 1) * DH] for i in range(qt + 1)], o=o,
                                    done=(6, 0) if h == 3 and qt == TT - 1 else None))
            for h in range(4):
                for qt in range(TT):
                    n = (qt + 1) * P
                    half = DH * (h % 2)
                    o = bank[7][half:half + DH, h // 2 * NT + qt * P:h // 2 * NT + (qt + 1) * P]
                    out.append(dict(scores=[(pair("sq", h, qt * P, n), pair("sk", h, 0, n), seen[:, qt, 0:n])],
                                    keys=qt + 1, o=o, done=(7, 6) if h == 3 and qt == TT - 1 else None,
                                    v=[proj2[:, i, SV + h * DH:SV + (h + 1) * DH] for i in range(qt + 1)]))
            for qt in range(TT):
                for h in range(4):
                    n = (qt + 1) * P
                    o = bank[6 + qt][:, h * P:(h + 1) * P]
                    out.append(dict(scores=[(pair("dq", 2 * h + i, qt * P, n), pair("dk", 2 * h + i, 0, n), mask_b[:])
                                            for i in range(2)],
                                    keys=qt + 1, o=o, diff=True, done=(6 + qt, ("rows", qt)) if h == 3 else None,
                                    v=[proj2[:, i, DV + h * P:DV + (h + 1) * P] for i in range(qt + 1)]))
            return out

        class Sync(Phases):
            def load(self):
                super().load()
                self.e.dma_start(rows_in[:, 0:TT, :], A_["x"][0].rearrange("(t p) n -> p t n", p=P)).then_inc(inputs_in, 16)
                self.e.dma_start(rows_in[:, TT:, :], A_["ctx"][0].rearrange("(t p) n -> p t n", p=P)).then_inc(inputs_in, 16)
                self.e.dma_start(const[:], consts).then_inc(consts_in, 16)

            def chunk_loads(self, count, pieces, tail=0):
                e, n = self.e, self.n
                base = n.static("chunks")

                def body(j, at):
                    slot = (base + j) % RAW
                    if n.static("chunks") >= RAW:
                        e.wait_ge(lo_ready, n("halves", -2 * (RAW - 1)))
                    for dst, src in pieces(slot, j, at):
                        e.dma_start(dst, src).then_inc(raw_loaded[slot], 16)
                    n.add("chunks", 1)
                    n.add("halves", 2)

                run_chunks(e, n, count, dict(chunks=1, halves=2), body, tail)

            def kslices(self, w, l, base, width):
                src = w[l].rearrange("(k p) n -> p k n", p=P)

                def pieces(slot, j, at):
                    dst = tiles(raw[:, slot, :], KT)
                    wd = min(CW, width - j * CW)
                    for h in range(2):
                        yield (dst[:, 4 * h:4 * h + 4, 0:wd], src[:, 4 * h:4 * h + 4, bass.ds(at * CW + base, wd)])
                return pieces

            def ada(self, l):
                self.chunk_loads(24, self.kslices(A_["w_ada"], l, 0, 6 * D))

            def up(self, kind, count, w):
                if kind != "silu":
                    width = {"rows1": count * CW, "rows2": IN2, "relu2": FF1}[kind]
                    self.chunk_loads(count, self.kslices(w["w"], w["l"], w["base"], width), 1 if kind == "rows2" else 0)
                    return
                gate, up_ = (w[k][w["l"]].rearrange("(k p) n -> p k n", p=P) for k in ("w", "w2"))

                def pieces(slot, j, at):
                    dst = tiles(raw[:, slot, :], KT)
                    yield dst[:, :, 0:P], gate[:, :, bass.ds(at * P, P)]
                    yield dst[:, :, P:2 * P], up_[:, :, bass.ds(at * P, P)]
                self.chunk_loads(count, pieces)

            def down(self, kind, count, w, s, gate, last=False):
                src = w["w"][w["l"]].rearrange("(c k p) n -> p c k n", p=P, k=2)

                def pieces(slot, j, at):
                    for k in range(2):
                        yield tiles(raw[:, slot, :], 2)[:, k, :], src[:, at, k, :]
                self.chunk_loads(count, pieces, self.tail(count))
                self.n.add("residual", KT)

            def modulation(self, l):
                super().modulation(l)

            def finish(self):
                rows = rows_in[:, 0:TT, :]
                for t in range(TT):
                    self.e.wait_ge(final_rows, KT // 2 * (t + 1))
                    self.e.dma_start(out[0].rearrange("(t p) n -> p t n", p=P)[:, t, :], rows[:, t, :]).then_inc(stored, 16)
                self.e.wait_ge(stored, 16 * TT)

        class Pool(Phases):
            def load(self):
                super().load()
                nc.gpsimd.memset(ones[:], 1.0).then_inc(preset, 1)
                nc.gpsimd.memset(neg_half[:], -0.5).then_inc(preset, 1)
                for i, name in enumerate(("c", "c_ctx")):
                    src = A_["c"][0] if name == "c" else A_["c_ctx"]
                    self.e.dma_start(cond_raw[:, 0, :, i], src.rearrange("(k p) -> p k", p=P), allow_slow_non_contiguous=True).then_inc(cond_in, 16)
                self.e.wait_ge(preset, 2)

            def ada(self, l):
                if l == 0:
                    self.e.wait_ge(turned_out, 8)
                else:
                    self.e.wait_ge(residual_new, self.n("residual"))
                self.e.dma_start(mod_rows[4:5, :], A_["b_ada"][l:l + 1, :]).then_inc(params_in, 16)
                super().ada(l)

            def params(self, l):
                e = self.e
                if l:
                    e.wait_ge(residual_new, self.n("residual"))
                for i, k in enumerate(("norm1_g", "norm2_g")):
                    e.dma_start(norm_g[:, i, :], A_[k][l].rearrange("(k p) -> p k", p=P), allow_slow_non_contiguous=True).then_inc(params_in, 16)
                at = 0
                for k, w in (("q_norm_g", DH), ("k_norm_g", DH), ("gmlp_v_g", 256)):
                    e.dma_start(gains1[:, at:at + w], A_[k][l:l + 1, :].broadcast_to([P, w])).then_inc(params_in, 16)
                    at += w
                e.dma_start(w_sp[:], A_["w_spatial"][l].rearrange("h p q -> p h q")).then_inc(params_in, 16)
                e.dma_start(b_sp[:], A_["b_spatial"][l].rearrange("h p -> p h"), allow_slow_non_contiguous=True).then_inc(params_in, 16)
                super().params(l)

            def params2(self, l):
                e = self.e
                if l:
                    e.wait_ge(residual_new, self.n("residual"))
                for i, k in enumerate(("attn_norm_g_2", "ffn_norm_g_2")):
                    e.dma_start(norm2_g[:, i, :], A_[k][l].rearrange("(k p) -> p k", p=P), allow_slow_non_contiguous=True).then_inc(params_in, 16)
                for i, k in enumerate(("q_norm_g_2", "k_norm_g_2")):
                    e.dma_start(gains2[:, :, i, :], A_[k][l:l + 1].broadcast_to([P, 3, DH])).then_inc(params_in, 16)
                e.dma_start(tiles(lam_in[:], 4), A_["diff_lambda_2"][l:l + 1].broadcast_to([P, 4, DH])).then_inc(params_in, 16)
                e.dma_start(sub_g[:], A_["diff_subln_g_2"][l:l + 1, :].broadcast_to([P, P])).then_inc(params_in, 16)
                self.n.add("params", 1)

            def power(self, w):
                self.e.wait_ge(var_ready, self.n("pow", 1))
                nc.gpsimd.tensor_tensor(rstd[:, 0:w], variance[:, 0:w], neg_half[:, 0:w], ALU.pow).then_inc(rstd_ready, 1)
                self.n.add("pow", 1)

            def norm(self, s, b, which):
                self.power(TT)
                self.n.add("norm", 1)

            def heads1(self, s, kv_only):
                for t in range(TT):
                    for h in ([] if kv_only else [NQ1]) + [NKV1]:
                        self.power(h)
                self.n.add("heads", 1)

            def spatial_gate(self):
                self.power(4 * TT)
                self.n.add("gmlp", 1)

            def heads2(self, l):
                for t in range(TT):
                    for h in (8, 16, 8):
                        self.power(h)

            def attend2(self, l):
                for t in range(TT):
                    self.power(4)

        PARAM_DMAS = [0]

        def params_until(phase, l):
            if phase == "params":
                return 16 * (8 * l + 7)
            if phase == "bias":
                return 16 * (8 * l + 8)
            return 16 * (8 * DEPTH + 6 * (l + 1))

        class Scalar(Phases):
            def __init__(self, eng):
                super().__init__(eng)
                self.split_done = 0

            def order(self, ins):
                ins.then_inc(act_order, 1)
                self.n.add("act_order", 1)
                self.e.wait_ge(act_order, self.n("act_order"))

            def split(self, k):
                n, e = self.n, self.e
                c = n.static("chunks") + k
                e.wait_ge(raw_loaded[c % RAW], self.loaded(c, k))
                for h in range(2):
                    if 2 * c + h >= SPLIT:
                        e.wait_ge(multiplied, n("halves", 2 * k + h + 1 - SPLIT))
                    nc.scalar.copy(w_hi[:, (2 * c + h) % SPLIT, :], raw[:, c % RAW, h * 1024:(h + 1) * 1024]).then_inc(hi_ready, 1)

            def loaded(self, c, k):
                v = 32 * (c // RAW + 1)
                s = self.n.step.get("chunks", 0)
                return v + self.n.it * (32 * (s // RAW)) if self.n.it is not None and s else v

            def stream(self, count, kind, drain, extra=None, tail=0, finish=None):
                n = self.n
                self.catch_up()

                def body(j, at):
                    if drain:
                        self.e.wait_ge(multiplied, n("halves", 2))
                        drain(j, at)
                    if j < count - 1 and n.static("chunks") + 2 < TOTAL[0]:
                        self.split(2)
                    if finish:
                        finish(j, at)
                    n.add("chunks", 1)
                    n.add("halves", 2)

                run_chunks(self.e, n, count, dict(chunks=1, halves=2, **(extra or {})), body, max(tail, 1))
                self.behind = n.static("chunks") + 1 < TOTAL[0]

            def catch_up(self):
                if self.behind:
                    self.behind = False
                    self.split(1)

            def load(self):
                super().load()
                e = self.e
                e.wait_ge(cond_in, 32)
                nc.scalar.activation(cond_raw[:, 1, :, :], cond_raw[:, 0, :, :], ACT.Exp, scale=-1.0).then_inc(cond_exp, 1)
                self.split(0)
                self.split(1)

            def ada(self, l):
                def drain(j, at):
                    b = bank[j % 4]
                    self.e.wait_ge(preset, 2)
                    nc.scalar.copy(mod_rows[0:4, bass.ds(at * CW, CW)], b[0:4, 0:CW]).then_inc(drained_act, 1)
                    self.n.add("drained_act", 1)
                if l == 0:
                    self.e.wait_ge(turned_out, 8)
                self.stream(24, "ada", drain, dict(drained_act=1))

            def up(self, kind, count, w):
                n, e = self.n, self.e
                if kind in ("rows1", "rows2"):
                    dst = proj1 if kind == "rows1" else proj2
                    width = IN2 if kind == "rows2" else IN1

                    def drain(j, at):
                        wd = min(CW, width - j * CW - w["base"])
                        src = tiles(bank[j % 4][:], TT)[:, :, 0:wd]
                        e.wait_ge(preset, 2)
                        nc.scalar.copy(dst[:, :, bass.ds(at * CW + w["base"], wd)], src).then_inc(drained_act, 1)
                        n.add("drained_act", 1)
                    self.stream(count, kind, drain, dict(drained_act=1), 1 if kind == "rows2" else 0)
                elif kind == "relu2":
                    def drain(j, at):
                        if j >= 2:
                            e.wait_ge(hidden, n("hidden", -1))
                        nc.scalar.activation(fa[:, j % 2, :], bank[j % 4][:], ACT.Relu).then_inc(drained_act, 1)
                        n.add("drained_act", 1)
                        n.add("hidden", 1)
                        e.wait_ge(drained_act, n("drained_act"))
                        e.wait_ge(preset, 2)
                        nc.scalar.activation(hid_hi[:, bass.ds(at * 2, 2), :], tiles(fa[:, j % 2, :], 2),
                                             ACT.Square).then_inc(squared, 1)
                    self.stream(count, kind, drain, dict(drained_act=1, hidden=1))
                else:
                    def drain(j, at):
                        if j >= 2:
                            e.wait_ge(hidden, n("hidden", -1))
                        ex = fa[:, j % 2, 0:NT]
                        self.order(nc.scalar.activation(ex, bank[j % 4][:, 0:NT], ACT.Exp, scale=-1.0))
                        nc.scalar.add(ex, ex, 1.0).then_inc(gate_exp, 1)

                    def finish(j, at):
                        n.add("hidden", 1)
                        n.add("gated", 1)
                        e.wait_ge(gated, n("gated"))
                        e.wait_ge(preset, 2)
                        nc.scalar.copy(hid_hi[:, bass.ds(at, 1), :], tiles(fb[:, j % 2, 0:NT], 1)).then_inc(gate_hi, 1)
                    self.stream(count, kind, drain, dict(hidden=1, gated=1, act_order=1), finish=finish)

            def down(self, kind, count, w, s, gate, last=False):
                self.stream(count, kind, None, tail=self.tail(count))
                self.n.add("residual", KT)

            def norm(self, s, b, which):
                n, e = self.n, self.e
                e.wait_ge(residual_new, n("residual"))
                if n.static("v_kept"):
                    e.wait_ge(v_kept, n("v_kept"))
                for h in range(2):
                    nc.scalar.activation(wide[:, 4 * h:4 * h + 4, :], residual[:, 4 * h:4 * h + 4, s * NT:(s + 1) * NT],
                                         ACT.Square).then_inc(squares, 1)
                self.catch_up()
                for h in range(2):
                    e.wait_ge(modulated, 2 * n("norm") + h + 1)
                    nc.scalar.copy(act_hi[:, 4 * h:4 * h + 4, :], wide[:, 4 * h:4 * h + 4, :]).then_inc(norm_hi, 1)
                n.add("norm", 1)
                n.add("pow", 1)

            def turn_out(self, dst, src, scale=None):
                n, e = self.n, self.e
                e.wait_ge(turned, n("turned", 1))
                if scale is None:
                    nc.scalar.copy(dst, src).then_inc(turned_out, 1)
                else:
                    nc.scalar.mul(dst, src, scale).then_inc(turned_out, 1)
                n.add("turned", 1)

            def mix_out(self, b, k):
                nc.scalar.copy(act_hi[:, k:k + 2, :], tiles(b, 2)).then_inc(mix_hi, 1)

            def heads1(self, s, kv_only):
                kt0 = 0 if s == 1 else TT
                self.e.wait_ge(drained_act, self.n("drained_act"))
                nc.scalar.copy(v_rows[:, kt0:kt0 + TT, :], proj1[:, :, V1:V1 + 2 * DH]).then_inc(v_kept, 1)
                self.n.add("v_kept", 1)
                if not kv_only:
                    for i in range(2):
                        self.turn_out(q_t[:, 2 * i:2 * i + 2, :], tiles(bank[self.n.static("turned") % 4][:], 2), DH ** -0.5)
                self.turn_out(k_t[:, :, kt0 * P:(kt0 + TT) * P], tiles(bank[self.n.static("turned") % 4][:], 2))
                self.n.add("heads", 1)
                self.n.add("pow", TT * (1 if kv_only else 2))

            def attention(self, items, probs, probs_t):
                n, e = self.n, self.e
                s0, i0 = n.static("scores"), n.static("items")
                first = [0]
                for it in items:
                    first.append(first[-1] + len(it["scores"]))

                def exps(j):
                    for s in range(first[j], first[j + 1]):
                        width = items[j]["keys"] * P
                        e.wait_ge(max_ready, s0 + s + 1)
                        if s >= 4:
                            prev = next(x for x in range(len(items)) if first[x] <= s - 4 < first[x + 1])
                            e.wait_ge(prob_turned, i0 + prev + 1)
                        nc.scalar.activation(probs[:, s % 4, 0:width], bank[s % 4][:, 0:width], ACT.Exp,
                                             bias=neg_max[:, s:s + 1], accum_out=total[:, s:s + 1]).then_inc(exped, 1)

                def out_(j):
                    done = items[j]["done"]
                    if done and not isinstance(done[1], tuple):
                        e.wait_ge(mixed, i0 + j + 1)
                        self.mix_out(bank[done[0]][:], done[1])
                exps(0)
                for j, it in enumerate(items):
                    if j + 1 < len(items):
                        exps(j + 1)
                    e.wait_ge(prob_turned, i0 + j + 1)
                    if j >= 2:
                        e.wait_ge(mixed, i0 + j - 1)
                    w = it["keys"]
                    nc.scalar.copy(probs_t[:, j % 2, 0:w, :], tiles(bank[4 + j % 2][:, 0:w * P], w)).then_inc(prob_t, 1)
                    if j:
                        out_(j - 1)
                out_(len(items) - 1)
                n.add("scores", first[-1])
                n.add("items", len(items))

            def attend1(self, s):
                self.attention(items1(s), probs1, probs_t1)
                self.n.add("mix", 2)

            def fourier(self):
                n, e = self.n, self.e
                for i in range(2):
                    e.wait_ge(dft_full, 2 * n("fourier") + i + 1)
                    nc.scalar.copy(four[:, i, :], bank[i][:]).then_inc(dft_out, 1)
                e.wait_ge(mix_full, 2 * n("fourier") + 1)
                self.mix_out(bank[2][:], 4)
                n.add("fourier", 1)
                n.add("mix", 1)

            def spatial_gate(self):
                n, e = self.n, self.e
                self.turn_out(w_sp_t[:], tiles(bank[3][:], 4))
                e.wait_ge(gelu_in, n("gmlp", 1))
                nc.scalar.activation(gtmp[:], gtmp[:], ACT.Tanh, scale=float(np.sqrt(2 / np.pi))).then_inc(gelu_tanh, 1)
                e.wait_ge(mix_full, 2 * n("gmlp") + 2)
                self.mix_out(bank[5][:], 6)
                n.add("gmlp", 1)
                n.add("pow", 1)
                n.add("mix", 1)

            def heads2(self, l):
                n, e = self.n, self.e
                for i in range(11):
                    b = bank[n.static("turned") % 4]
                    k = 2 * i
                    query = k < 2 or 4 <= k < 8 or k == 12 or 16 <= k < 20
                    w = 2 if k < 20 else 1
                    self.turn_out(pairs_t[:, k:k + w, :], tiles(b[:, 0:w * NT], w), DH ** -0.5 if query else None)
                n.add("heads", 1)
                n.add("pow", 3 * TT)

            def index2(self):
                n, e = self.n, self.e
                for i in range(IH * TT):
                    w = (i // IH + 1) * P
                    e.wait_ge(logit_full, n("logits", i + 1))
                    if i >= 2:
                        e.wait_ge(logit_used, n("logits", i - 1))
                    nc.scalar.activation(relu_t[:, i % 2, 0:w], bank[i % 4][:, 0:w], ACT.Relu).then_inc(logit_relu, 1)
                n.add("logits", IH * TT)

            def attend2(self, l):
                n, e = self.n, self.e
                e.wait_ge(lam_sums, l + 1)
                nc.scalar.activation(lam[:, 2:4], lam[:, 0:2], ACT.Exp).then_inc(lam_exp, 1)
                self.attention(items2(), probs2, probs_t2)
                for t in range(TT):
                    e.wait_ge(mix_full, 2 * n("gmlp") + 2 * l + t + 1)
                    self.mix_out(bank[4 + t][:], 2 + 2 * t)
                n.add("pow", TT)
                n.add("mix", 4)

            def finish(self):
                n, e = self.n, self.e
                for t in range(TT):
                    for i in range(2):
                        e.wait_ge(turned, n("turned", 1))
                        for q in range(2):
                            nc.scalar.copy(rows_in[:, t, i * 512 + q * 256:i * 512 + (q + 1) * 256],
                                           bank[i + 2 * t][:, q * 256:(q + 1) * 256]).then_inc(final_rows, 1)
                        n.add("turned", 1)

        class Vector(Phases):
            def order(self, ins):
                ins.then_inc(dve_order, 1)
                self.n.add("dve_order", 1)
                self.e.wait_ge(dve_order, self.n("dve_order"))

            def split(self, k):
                n, e = self.n, self.e
                c = n.static("chunks") + k
                for h in range(2):
                    e.wait_ge(hi_ready, n("halves", 2 * k + h + 1))
                    slot = (2 * c + h) % SPLIT
                    nc.vector.tensor_tensor(w_lo[:, slot, :], raw[:, c % RAW, h * 1024:(h + 1) * 1024],
                                            w_hi[:, slot, :].bitcast(F32), ALU.subtract).then_inc(lo_ready, 1)

            def stream(self, count, drain, extra=None, tail=0, finish=None):
                n = self.n
                self.catch_up()

                def body(j, at):
                    if drain:
                        drain(j, at)
                    if j < count - 1 and n.static("chunks") + 2 < TOTAL[0]:
                        self.split(2)
                    if finish:
                        finish(j, at)
                    n.add("chunks", 1)
                    n.add("halves", 2)

                run_chunks(self.e, n, count, dict(chunks=1, halves=2, **(extra or {})), body, max(tail, 1))
                self.behind = n.static("chunks") + 1 < TOTAL[0]

            def catch_up(self):
                if self.behind:
                    self.behind = False
                    self.split(1)

            def load(self):
                n, e = self.n, self.e
                for k in range(KT):
                    e.wait_ge(turned, k + 1)
                    nc.vector.tensor_copy(residual[:, k, :], bank[k][:]).then_inc(turned_out, 1)
                n.add("turned", 8)
                nc.vector.tensor_copy(ident_b[:], ident)
                nc.vector.tensor_copy(mask_b[:], causal(0))
                self.order(nc.vector.memset(cond[:].bitcast(mybir.dt.uint32), 0))
                e.wait_ge(cond_exp, 1)
                self.order(nc.vector.tensor_scalar(cond_raw[:, 1], cond_raw[:, 1], 1.0, None, ALU.add))
                self.order(nc.vector.reciprocal(cond_raw[:, 1], cond_raw[:, 1]))
                e.wait_ge(cond_in, 32)
                self.order(nc.vector.tensor_tensor(cond_raw[:, 2], cond_raw[:, 0], cond_raw[:, 1], ALU.mult))
                self.order(nc.vector.tensor_copy(cond[:, :, 0:2], cond_raw[:, 2]))
                nc.vector.tensor_tensor(cond[:, :, 2:4], cond_raw[:, 2], cond[:, :, 0:2].bitcast(F32),
                                        ALU.subtract).then_inc(cond_ready, 1)
                self.split(0)
                self.split(1)

            def ada(self, l):
                self.stream(24, None)
                self.n.add("drained_act", 24)

            def modulation(self, l):
                n, e = self.n, self.e
                e.wait_ge(mod_full, l + 1)
                self.order(nc.vector.tensor_copy(mod[:], bank[4][:, 0:96].rearrange("p (j s) -> p j s", s=2)))
                e.wait_ge(params_in, params_until("params", l))
                for i in range(2):
                    sc = mod[:, 8 + 24 * i:16 + 24 * i, :]
                    self.order(nc.vector.tensor_scalar(mscale[:, i], sc, 1.0, None, ALU.add))
                    self.order(nc.vector.tensor_tensor(mscale[:, i], mscale[:, i],
                                                       norm_g[:, i, :].unsqueeze(2).broadcast_to([P, KT, 2]), ALU.mult))
                n.add("mod", 1)

            def up(self, kind, count, w):
                n, e = self.n, self.e
                if kind in ("rows1", "rows2"):
                    self.stream(count, None, None, 1 if kind == "rows2" else 0)
                    n.add("drained_act", count)
                elif kind == "relu2":
                    def drain(j, at):
                        e.wait_ge(drained_act, n("drained_act", 1))
                        self.order(nc.vector.tensor_tensor(fb[:, j % 2, :], fa[:, j % 2, :], fa[:, j % 2, :], ALU.mult))

                    def finish(j, at):
                        n.add("drained_act", 1)
                        n.add("hidden", 1)
                        e.wait_ge(squared, n("squared", 1))
                        n.add("squared", 1)
                        nc.vector.tensor_tensor(hid_lo[:, bass.ds(at * 2, 2), :], tiles(fb[:, j % 2, :], 2),
                                                hid_hi[:, bass.ds(at * 2, 2), :].bitcast(F32), ALU.subtract).then_inc(hidden, 1)
                    self.stream(count, drain, dict(drained_act=1, hidden=1, squared=1, dve_order=1), finish=finish)
                else:
                    def drain(j, at):
                        ex, b, f = fa[:, j % 2, 0:NT], bank[j % 4], fb[:, j % 2, 0:NT]
                        e.wait_ge(gate_exp, n("silus", 1))
                        self.order(nc.vector.reciprocal(ex, ex))
                        self.order(nc.vector.tensor_tensor(ex, b[:, 0:NT], ex, ALU.mult))
                        nc.vector.tensor_tensor(f, b[:, NT:2 * NT], ex, ALU.mult).then_inc(gated, 1)

                    def finish(j, at):
                        f = fb[:, j % 2, 0:NT]
                        n.add("silus", 1)
                        n.add("hidden", 1)
                        n.add("gated", 1)
                        e.wait_ge(gate_hi, n("silus"))
                        nc.vector.tensor_tensor(hid_lo[:, bass.ds(at, 1), :], tiles(f, 1),
                                                hid_hi[:, bass.ds(at, 1), :].bitcast(F32), ALU.subtract).then_inc(hidden, 1)
                    self.stream(count, drain, dict(silus=1, hidden=1, gated=1, dve_order=2), finish=finish)

            def down(self, kind, count, w, s, gate, last=False):
                n, e = self.n, self.e
                self.stream(count, None, None, self.tail(count))
                e.wait_ge(multiplied, n("halves"))
                for d in range(KT):
                    x = residual[:, d, s * NT:(s + 1) * NT]
                    src = tiles(bank[4 + d // 2][:], 2)[:, d % 2, :]
                    if gate is None:
                        nc.vector.tensor_tensor(x, src, x, ALU.add).then_inc(residual_new, 1)
                    else:
                        nc.vector.scalar_tensor_tensor(x, src, mod[:, gate + d, s:s + 1], x, ALU.mult, ALU.add).then_inc(residual_new, 1)
                n.add("residual", KT)

            def norm(self, s, b, which):
                n, e = self.n, self.e
                if b == 2:
                    e.wait_ge(params_in, params_until("params2", self.layer2))
                e.wait_ge(sums, n("norm", 1))
                nc.vector.tensor_scalar(variance[:, 0:TT], bank[0][:, 0:TT], 1.0 / D, EPS, ALU.mult, ALU.add).then_inc(var_ready, 1)
                n.add("pow", 1)
                e.wait_ge(rstd_ready, n("pow"))
                for t in range(TT):
                    ins = nc.vector.tensor_scalar(diag[:, t, :], ident, rstd[:, t:t + 1], None, ALU.mult)
                ins.then_inc(rstd_diag, 1)
                self.catch_up()
                e.wait_ge(rstd_wide, n("norm", 1))
                x = residual[:, :, s * NT:(s + 1) * NT]
                for h in range(2):
                    self.order(nc.vector.tensor_tensor(wide[:, 4 * h:4 * h + 4, :], x[:, 4 * h:4 * h + 4, :],
                                                       bank[1][:, 0:NT].unsqueeze(1).broadcast_to([P, 4, NT]), ALU.mult))
                    for k in range(4 * h, 4 * h + 4):
                        if b == 1:
                            ins = nc.vector.tensor_scalar(wide[:, k, :], wide[:, k, :], mscale[:, which, k, s:s + 1],
                                                          mod[:, 24 * which + k, s:s + 1], ALU.mult, ALU.add)
                        else:
                            ins = nc.vector.tensor_scalar(wide[:, k, :], wide[:, k, :], norm2_g[:, which, k:k + 1], None, ALU.mult)
                    ins.then_inc(modulated, 1)
                for h in range(2):
                    e.wait_ge(norm_hi, 2 * n("norm") + h + 1)
                    nc.vector.tensor_tensor(act_lo[:, 4 * h:4 * h + 4, :], wide[:, 4 * h:4 * h + 4, :],
                                            act_hi[:, 4 * h:4 * h + 4, :].bitcast(F32), ALU.subtract).then_inc(norm_lo, 1)
                n.add("norm", 1)

            def params2(self, l):
                super().params2(l)
                self.layer2 = l

            def mix_out(self, b, k):
                n, e = self.n, self.e
                n.add("mix", 1)
                e.wait_ge(mix_hi, n("mix"))
                nc.vector.tensor_tensor(act_lo[:, k:k + 2, :], tiles(b, 2), act_hi[:, k:k + 2, :].bitcast(F32),
                                        ALU.subtract).then_inc(mix_lo, 1)

            def power(self):
                self.n.add("pow", 1)
                self.e.wait_ge(rstd_ready, self.n("pow"))

            def head_norm(self, x, heads, gain, table, dst, tmp):
                t0, t1, t2 = (tiles(t[:, 0:heads * DH], heads) for t in tmp)
                src = x
                if gain is not None:
                    self.order(nc.vector.tensor_tensor(t0, x, x, ALU.mult))
                    self.order(nc.vector.tensor_reduce(variance[:, 0:heads], t0, AX.X, ALU.add))
                    nc.vector.tensor_scalar(variance[:, 0:heads], variance[:, 0:heads], 1.0 / DH, EPS, ALU.mult,
                                            ALU.add).then_inc(var_ready, 1)
                    self.power()
                    self.order(nc.vector.tensor_tensor(t0, x, rstd[:, 0:heads].unsqueeze(2).broadcast_to([P, heads, DH]), ALU.mult))
                    if len(gain.shape) == 2:
                        last = [(t0 if table else dst, t0, gain.unsqueeze(1).broadcast_to([P, heads, DH]))]
                    else:
                        hh = heads // 2
                        last = [((t0 if table else dst)[:, g * hh:(g + 1) * hh], t0[:, g * hh:(g + 1) * hh],
                                 gain[:, g, :].unsqueeze(1).broadcast_to([P, hh, DH])) for g in range(2)]
                    for a, b, c in last:
                        self.order(nc.vector.tensor_tensor(a, b, c, ALU.mult))
                    src = t0
                if table:
                    cos, sin, axes = table
                    w = DH // axes // 2
                    nc.vector.tensor_tensor(t1, src, cos.unsqueeze(1).broadcast_to([P, heads, DH]), ALU.mult)
                    sv, tv = (v.rearrange("p h (a b w) -> p h a b w", b=2, w=w) for v in (src, t2))
                    st = sin.rearrange("p (a b w) -> p a b w", b=2, w=w)
                    for half in range(2):
                        if axes == 1:
                            ins = nc.vector.tensor_tensor(tv[:, :, 0, half], sv[:, :, 0, 1 - half],
                                                          st[:, 0, half].unsqueeze(1).broadcast_to([P, heads, w]), ALU.mult)
                        else:
                            ins = nc.vector.tensor_tensor(tv[:, :, :, half], sv[:, :, :, 1 - half],
                                                          st[:, :, half].unsqueeze(1).broadcast_to([P, heads, axes, w]), ALU.mult)
                    self.order(ins)
                    self.order(nc.vector.tensor_tensor(dst, t1, t2, ALU.add))

            def heads1(self, s, kv_only):
                n, e = self.n, self.e
                e.wait_ge(drained_act, n("drained_act"))
                for t in range(TT):
                    table = (rope[1][0][:, t], rope[1][1][:, t], 2) if s == 0 else None
                    if not kv_only:
                        q = tiles(proj1[:, t, Q1:Q1 + NQ1 * DH], NQ1)
                        self.head_norm(q, NQ1, gains1[:, 0:DH], table, q, [x[:] for x in tmp1])
                    k = tiles(proj1[:, t, K1:K1 + NKV1 * DH], NKV1)
                    self.head_norm(k, NKV1, gains1[:, DH:2 * DH], table, k, [x[:] for x in tmp1])
                    kd = kdup[:, t].rearrange("p (h c) d -> p h c d", c=2)
                    for c in range(2):
                        ins = nc.vector.tensor_copy(kd[:, :, c, :], k)
                    ins.then_inc(rows_ready, 1)
                n.add("heads", 1)
                n.add("turned", 1 if kv_only else 3)

            def attention(self, items, probs):
                n, e = self.n, self.e
                s0, i0 = n.static("scores"), n.static("items")
                first = [0]
                for it in items:
                    first.append(first[-1] + len(it["scores"]))

                def maxima(j):
                    for s in range(first[j], first[j + 1]):
                        width = items[j]["keys"] * P
                        e.wait_ge(scored, s0 + s + 1)
                        nc.vector.tensor_reduce(neg_max[:, s:s + 1], bank[s % 4][:, 0:width], AX.X, ALU.max,
                                                negate=True).then_inc(max_ready, 1)

                def out_(j):
                    done = items[j]["done"]
                    if done and isinstance(done[1], tuple):
                        e.wait_ge(mixed, i0 + j + 1)
                        nc.vector.tensor_copy(diff_rows[:, done[1][1], :], bank[done[0]][:]).then_inc(diff_drained, 1)
                    elif done:
                        self.mix_out(bank[done[0]][:], done[1])
                maxima(0)
                for j, it in enumerate(items):
                    if j + 1 < len(items):
                        maxima(j + 1)
                    s = first[j]
                    width = it["keys"] * P
                    e.wait_ge(exped, s0 + first[j + 1])
                    if it.get("diff"):
                        self.order(nc.vector.reciprocal(total[:, s:s + 2], total[:, s:s + 2]))
                        self.order(nc.vector.tensor_tensor(total[:, s + 1:s + 2], total[:, s + 1:s + 2], lam[:, 4:5], ALU.mult))
                        self.order(nc.vector.tensor_scalar(probs[:, (s + 1) % 4, 0:width], probs[:, (s + 1) % 4, 0:width],
                                                           total[:, s + 1:s + 2], None, ALU.mult))
                        nc.vector.scalar_tensor_tensor(probs[:, s % 4, 0:width], probs[:, s % 4, 0:width], total[:, s:s + 1],
                                                       probs[:, (s + 1) % 4, 0:width], ALU.mult, ALU.subtract).then_inc(prob_ready, 1)
                    else:
                        self.order(nc.vector.reciprocal(total[:, s:s + 1], total[:, s:s + 1]))
                        nc.vector.tensor_scalar(probs[:, s % 4, 0:width], probs[:, s % 4, 0:width], total[:, s:s + 1],
                                                None, ALU.mult).then_inc(prob_ready, 1)
                    if j:
                        out_(j - 1)
                out_(len(items) - 1)
                n.add("scores", first[-1])
                n.add("items", len(items))

            def attend1(self, s):
                self.attention(items1(s), probs1)

            def fourier(self):
                self.mix_out(bank[2][:], 4)
                self.n.add("fourier", 1)

            def spatial_gate(self):
                n, e = self.n, self.e
                v = proj1[:, :, U1:U1 + 512]
                self.order(nc.vector.tensor_tensor(gtmp[:], v, v, ALU.mult))
                self.order(nc.vector.tensor_scalar(gtmp[:], gtmp[:], 0.044715, 1.0, ALU.mult, ALU.add))
                nc.vector.tensor_tensor(gtmp[:], gtmp[:], v, ALU.mult).then_inc(gelu_in, 1)
                e.wait_ge(gelu_tanh, n("gmlp", 1))
                self.order(nc.vector.tensor_scalar(gtmp[:], gtmp[:], 1.0, 0.5, ALU.add, ALU.mult))
                self.order(nc.vector.tensor_tensor(gates[:], gtmp[:], v, ALU.mult))
                gv = gates[:, :, 256:512]
                sq = gtmp[:, :, 256:512]
                self.order(nc.vector.tensor_tensor(sq, gv, gv, ALU.mult))
                var4 = variance[:, 0:4 * TT].rearrange("p (t h) -> p t h", t=TT)
                self.order(nc.vector.tensor_reduce(var4, sq.rearrange("p t (h d) -> p t h d", h=4), AX.X, ALU.add))
                nc.vector.tensor_scalar(variance[:, 0:4 * TT], variance[:, 0:4 * TT], 1.0 / DH, EPS, ALU.mult,
                                        ALU.add).then_inc(var_ready, 1)
                self.power()
                r4 = rstd[:, 0:4 * TT].rearrange("p (t h) -> p t h", t=TT)
                self.order(nc.vector.tensor_tensor(gv.rearrange("p t (h d) -> p t h d", h=4),
                                                   gv.rearrange("p t (h d) -> p t h d", h=4),
                                                   r4.unsqueeze(3).broadcast_to([P, TT, 4, DH]), ALU.mult))
                nc.vector.tensor_tensor(gv, gv, gains1[:, 2 * DH:].unsqueeze(1).broadcast_to([P, TT, 256]),
                                        ALU.mult).then_inc(rows_ready, 1)
                e.wait_ge(spatial, n("gmlp", 1))
                for h in range(4):
                    u = gates[:, :, h * DH:(h + 1) * DH]
                    ins = nc.vector.scalar_tensor_tensor(u, tiles(bank[4][:, h * P:(h + 1) * P], TT), b_sp[:, h:h + 1], u,
                                                         ALU.add, ALU.mult)
                ins.then_inc(rows_ready, 1)
                self.mix_out(bank[5][:], 6)
                n.add("gmlp", 1)
                n.add("turned", 1)

            def params(self, l):
                super().params(l)

            def heads2(self, l):
                n, e = self.n, self.e
                e.wait_ge(drained_act, n("drained_act"))
                for t in range(TT):
                    table = (rope[2][0][:, t], rope[2][1][:, t], 1)
                    for i, (base, heads) in enumerate(((MQ, 8), (DQ, 16), (SQ, 8))):
                        x = tiles(proj2[:, t, base:base + heads * DH], heads)
                        self.head_norm(x, heads, gains2[:, i], table, x, tmp2)
                    x = tiles(proj2[:, t, IQ:IQ + (IH + 1) * DH], IH + 1)
                    self.head_norm(x, IH + 1, None, table, x, tmp2)
                    for c in range(2):
                        ins = nc.vector.tensor_copy(ikdup[:, t, c, :], proj2[:, t, IK:IK + DH])
                    ins.then_inc(rows_ready, 1)
                n.add("heads", 1)
                n.add("turned", 11)

            def index2(self):
                n, e = self.n, self.e
                l = self.layer2
                self.order(nc.vector.tensor_scalar(proj2[:, :, IW:IW + IH], proj2[:, :, IW:IW + IH], float(np.float32(IH ** -0.5)),
                                                   None, ALU.mult))
                for i in range(IH * TT):
                    t, h = divmod(i, IH)
                    w = (t + 1) * P
                    e.wait_ge(logit_relu, n("logits", i + 1))
                    wt = proj2[:, t, IW + h:IW + h + 1]
                    sc = score[:, 0:w]
                    if h == 0:
                        nc.vector.tensor_scalar(sc, relu_t[:, i % 2, 0:w], wt, None, ALU.mult).then_inc(logit_used, 1)
                    else:
                        nc.vector.scalar_tensor_tensor(sc, relu_t[:, i % 2, 0:w], wt, sc, ALU.mult, ALU.add).then_inc(logit_used, 1)
                    e.wait_ge(logit_used, n("logits", i + 1))
                    if h < IH - 1:
                        continue
                    self.order(nc.vector.tensor_tensor(sc, sc, causal(t), ALU.add))
                    for _ in range(TOPK // 8):
                        self.order(nc.vector.max(best[:], sc))
                        self.order(nc.vector.match_replace(sc, best[:], sc, TAKEN))
                    sn = seen[:, t, 0:w]
                    self.order(nc.vector.tensor_scalar(sn, sc, TAKEN / 2, MASKED, ALU.is_gt, ALU.mult))
                    nc.vector.tensor_tensor(sn, sn, causal(t), ALU.add).then_inc(seen_ready, 1)
                n.add("logits", IH * TT)
                lv = lam_in[:].rearrange("p (a b d) -> p a b d", a=2, b=2)
                self.order(nc.vector.tensor_tensor(lv[:, :, 0, :], lv[:, :, 0, :], lv[:, :, 1, :], ALU.mult))
                nc.vector.tensor_reduce(lam[:, 0:2], lv[:, :, 0, :], AX.X, ALU.add).then_inc(lam_sums, 1)
                e.wait_ge(lam_exp, l + 1)
                init = 0.8 - 0.6 * float(np.exp(-0.3 * l))
                self.order(nc.vector.tensor_tensor(lam[:, 4:5], lam[:, 2:3], lam[:, 3:4], ALU.subtract))
                self.order(nc.vector.tensor_scalar(lam[:, 4:5], lam[:, 4:5], init, None, ALU.add))

            def attend2(self, l):
                n, e = self.n, self.e
                self.attention(items2(), probs2)
                e.wait_ge(diff_drained, TT * (l + 1))
                init = 0.8 - 0.6 * float(np.exp(-0.3 * l))
                for t in range(TT):
                    x = tiles(diff_rows[:, t, :], 4)
                    sq = tiles(scratch[:, 1, 0:512], 4)
                    self.order(nc.vector.tensor_tensor(sq, x, x, ALU.mult))
                    self.order(nc.vector.tensor_reduce(variance[:, 0:4], sq, AX.X, ALU.add))
                    nc.vector.tensor_scalar(variance[:, 0:4], variance[:, 0:4], 1.0 / (2 * DH), EPS, ALU.mult, ALU.add).then_inc(var_ready, 1)
                    self.power()
                    self.order(nc.vector.tensor_tensor(x, x, rstd[:, 0:4].unsqueeze(2).broadcast_to([P, 4, P]), ALU.mult))
                    self.order(nc.vector.tensor_tensor(x, x, sub_g[:].unsqueeze(1).broadcast_to([P, 4, P]), ALU.mult))
                    nc.vector.tensor_scalar(x, x, 1.0 - init, None, ALU.mult).then_inc(rows_ready, 1)
                for t in range(TT):
                    self.mix_out(bank[4 + t][:], 2 + 2 * t)
                self.n.add("done2", 1)

        class Tensor(Phases):
            def three(self, o, w, x, first):
                for i, (a, b) in enumerate(((0, 0), (0, 1), (1, 0))):
                    ins = nc.tensor.matmul(o, w[a], x[b], start=first and i == 0, stop=True, skip_group_check=True)
                return ins

            def stream(self, count, multiply, free=None, extra=None, tail=0):
                n, e = self.n, self.e

                def body(j, at):
                    if free is not None and (j >= 4 or n.it is not None):
                        e.wait_ge(free[0], n(free[1], -3))
                    for h in range(2):
                        e.wait_ge(lo_ready, n("halves", h + 1))
                        slot = (2 * n.static("chunks") + h) % SPLIT
                        multiply(j, at, h, w_hi[:, slot, :], w_lo[:, slot, :]).then_inc(multiplied, 1)
                    n.add("chunks", 1)
                    n.add("halves", 2)
                    if free is not None:
                        n.add(free[1], 1)

                per = dict(chunks=1, halves=2)
                if free is not None:
                    per[free[1]] = 1
                run_chunks(e, n, count, per, body, tail, 4 if free is not None else 1)

            def load(self):
                n, e = self.n, self.e
                e.wait_ge(inputs_in, 32)
                e.wait_ge(consts_in, 16)
                e.wait_ge(preset, 2)
                for k in range(KT):
                    for t in range(2 * TT):
                        ins = nc.tensor.transpose(bank[k][:, t * P:(t + 1) * P], rows_in[:, t, k * P:(k + 1) * P], ident)
                    ins.then_inc(turned, 1)
                n.add("turned", 8)
                e.wait_ge(turned_out, 8)
                e.wait_ge(cond_ready, 1)

            def ada(self, l):
                def multiply(j, at, h, hi, lo):
                    for k in range(4):
                        for i, w in enumerate((hi, lo)):
                            ins = nc.tensor.matmul(bank[j % 4][:, 0:CW], cond[:, 4 * h + k, :], tiles(w, 4)[:, k, :],
                                                   start=h == 0 and k == 0 and i == 0, stop=True, skip_group_check=True)
                    return ins
                self.stream(24, multiply, (drained_act, "drained_act"))

            def modulation(self, l):
                n, e = self.n, self.e
                e.wait_ge(drained_act, n("drained_act"))
                e.wait_ge(params_in, params_until("bias", l))
                for j in range(48):
                    ins = nc.tensor.matmul(bank[4][:, 2 * j:2 * j + 2], mod_rows[0:5, j * P:(j + 1) * P], sel[0:5, :],
                                           start=True, stop=True)
                ins.then_inc(mod_full, 1)
                n.add("mod", 1)

            def up(self, kind, count, w):
                n, e = self.n, self.e
                e.wait_ge(norm_lo, 2 * n("norm"))
                if kind in ("rows1", "rows2"):
                    width = IN2 if kind == "rows2" else IN1

                    def multiply(j, at, h, hi, lo):
                        wd = min(CW, width - j * CW)
                        for k in range(4):
                            for t in range(TT):
                                x = [a[:, 4 * h + k, t * P:(t + 1) * P] for a in (act_hi, act_lo)]
                                ins = self.three(tiles(bank[j % 4][:], TT)[:, t, 0:wd], x,
                                                 [tiles(v, 4)[:, k, 0:wd] for v in (hi, lo)], h == 0 and k == 0 and t == 0)
                        return ins
                    self.stream(count, multiply, (drained_act, "drained_act"), tail=1 if kind == "rows2" else 0)
                    return

                def multiply(j, at, h, hi, lo):
                    for k in range(4):
                        x = [a[:, 4 * h + k, :] for a in (act_hi, act_lo)]
                        for t in range(2):
                            ins = self.three(tiles(bank[j % 4][:], 2)[:, t, :], [tiles(v, 4)[:, k, t * P:(t + 1) * P] for v in (hi, lo)],
                                             x, h == 0 and k == 0 and t == 0)
                    return ins
                self.stream(count, multiply, (drained_act, "drained_act") if kind == "relu2" else (gated, "gated"))
                n.add("hidden", count)

            def down(self, kind, count, w, s, gate, last=False):
                n, e = self.n, self.e
                if kind == "mix":
                    e.wait_ge(mix_lo, n("mix"))
                    src = (act_hi, act_lo)
                else:
                    e.wait_ge(hidden, n("hidden"))
                    src = (hid_hi, hid_lo)

                def multiply(j, at, h, hi, lo):
                    x = [a[:, bass.ds(at * 2 + h, 1), :] for a in src]
                    for d in range(KT):
                        ins = self.three(tiles(bank[4 + d // 2][:], 2)[:, d % 2:d % 2 + 1, :], [v[:, d * P:(d + 1) * P] for v in (hi, lo)],
                                         x, j == 0 and h == 0 and d % 2 == 0)
                    return ins
                self.stream(count, multiply, tail=self.tail(count))
                n.add("residual", KT)

            def norm(self, s, b, which):
                n, e = self.n, self.e
                for k in range(KT):
                    if k % 4 == 0:
                        e.wait_ge(squares, 2 * n("norm") + k // 4 + 1)
                    for t in range(TT):
                        ins = nc.tensor.matmul(bank[0][:, t:t + 1], wide[:, k, t * P:(t + 1) * P], ones[:, 0:1],
                                               start=k == 0 and t == 0, stop=True, skip_group_check=True)
                ins.then_inc(sums, 1)
                e.wait_ge(rstd_diag, n("norm", 1))
                nc.tensor.matmul(bank[1][:, 0:NT], ones[:], diag[:].rearrange("p t n -> p (t n)"), start=True, stop=True).then_inc(rstd_wide, 1)
                n.add("norm", 1)
                n.add("pow", 1)

            def turn(self, b, srcs, wait=True):
                n, e = self.n, self.e
                if wait:
                    e.wait_ge(turned_out, n("turned", -3))
                for i, x in enumerate(srcs):
                    ins = nc.tensor.transpose(b[:, i * P:(i + 1) * P], x, ident)
                ins.then_inc(turned, 1)
                n.add("turned", 1)

            def heads1(self, s, kv_only):
                n, e = self.n, self.e
                e.wait_ge(rows_ready, n("rows", TT))
                if not kv_only:
                    for i in range(2):
                        self.turn(bank[n.static("turned") % 4], [proj1[:, t, (2 * i + j) * P:(2 * i + j + 1) * P]
                                                                 for j in range(2) for t in range(TT)])
                self.turn(bank[n.static("turned") % 4], [kdup[:, t].rearrange("p h d -> p (h d)")[:, j * P:(j + 1) * P]
                                                         for j in range(2) for t in range(TT)])
                n.add("rows", TT)
                n.add("heads", 1)
                n.add("pow", TT * (1 if kv_only else 2))

            def attention(self, items, probs, probs_t):
                n, e = self.n, self.e
                s0, i0 = n.static("scores"), n.static("items")
                first = [0]
                for it in items:
                    first.append(first[-1] + len(it["scores"]))

                def score_(j):
                    for i, (q, k, m) in enumerate(items[j]["scores"]):
                        s = first[j] + i
                        width = items[j]["keys"] * P
                        if s >= 4:
                            e.wait_ge(exped, s0 + s - 3)
                        o = bank[s % 4][:, 0:width]
                        ins = nc.tensor.matmul(o, q, k, start=True, stop=m is None)
                        if m is not None:
                            ins = nc.tensor.matmul(bank[s % 4][:, width - m.shape[-1]:width], ident_b[:], m, start=False, stop=True)
                        ins.then_inc(scored, 1)

                def values(j):
                    it = items[j]
                    e.wait_ge(prob_t, i0 + j + 1)
                    if it.get("diff") and j == 16:
                        e.wait_ge(mix_lo, n("mix", 2))
                    for k, v in enumerate(it["v"]):
                        pt = probs_t[:, j % 2, k, :]
                        a, b = (pt, v) if it.get("diff") else (v, pt)
                        ins = nc.tensor.matmul(it["o"], a, b, start=k == 0, stop=k == it["keys"] - 1)
                    ins.then_inc(mixed, 1)
                score_(0)
                for j, it in enumerate(items):
                    if j + 1 < len(items):
                        score_(j + 1)
                    if j:
                        values(j - 1)
                    e.wait_ge(prob_ready, i0 + j + 1)
                    if j >= 2:
                        e.wait_ge(prob_t, i0 + j - 1)
                    s = first[j]
                    for k in range(it["keys"]):
                        ins = nc.tensor.transpose(bank[4 + j % 2][:, k * P:(k + 1) * P], probs[:, s % 4, k * P:(k + 1) * P], ident)
                    ins.then_inc(prob_turned, 1)
                values(len(items) - 1)
                n.add("scores", first[-1])
                n.add("items", len(items))

            def attend1(self, s):
                self.e.wait_ge(turned_out, self.n("turned"))
                self.e.wait_ge(v_kept, self.n("heads"))
                self.attention(items1(s), probs1, probs_t1)
                self.n.add("mix", 2)

            def fourier(self):
                n, e = self.n, self.e
                e.wait_ge(exped, n("scores"))
                for i in range(2):
                    for t in range(TT):
                        ins = nc.tensor.matmul(bank[i][:], proj1[:, t, F1 + i * P:F1 + (i + 1) * P], dft_n[:, t, :],
                                               start=t == 0, stop=t == TT - 1)
                    ins.then_inc(dft_full, 1)
                for i in range(2):
                    e.wait_ge(dft_out, 2 * n("fourier") + i + 1)
                    o = bank[2][:, i * NT:(i + 1) * NT]
                    nc.tensor.matmul(o, cols["dft_c"], four[:, i, 0:NT], start=True, stop=False)
                    ins = nc.tensor.matmul(o, cols["dft_s"], four[:, i, NT:2 * NT], start=False, stop=True)
                ins.then_inc(mix_full, 1)
                n.add("fourier", 1)
                n.add("mix", 1)

            def spatial_gate(self):
                n, e = self.n, self.e
                self.turn(bank[3], [w_sp[:, h, :] for h in range(4)])
                e.wait_ge(turned_out, n("turned"))
                e.wait_ge(rows_ready, n("rows", 1))
                e.wait_ge(prob_t, n("items"))
                for h in range(4):
                    ins = nc.tensor.matmul(bank[4][:, h * P:(h + 1) * P], w_sp_t[:, h, :],
                                           gates[:, :, 256 + h * DH:256 + (h + 1) * DH], start=True, stop=True)
                ins.then_inc(spatial, 1)
                e.wait_ge(rows_ready, n("rows", 2))
                for i in range(2):
                    for t in range(TT):
                        ins = nc.tensor.transpose(bank[5][:, (2 * i + t) * P:(2 * i + t + 1) * P], gates[:, t, i * P:(i + 1) * P], ident)
                ins.then_inc(mix_full, 1)
                n.add("rows", 2)
                n.add("gmlp", 1)
                n.add("pow", 1)
                n.add("mix", 1)

            def heads2(self, l):
                n, e = self.n, self.e
                e.wait_ge(rows_ready, n("rows", TT))
                offs = [MQ, MK, DQ, DQ + 256, DK, DK + 256, SQ, SK, IQ, IQ + 256]
                for o in offs:
                    self.turn(bank[n.static("turned") % 4], [proj2[:, t, o + j * P:o + (j + 1) * P] for j in range(2) for t in range(TT)])
                self.turn(bank[n.static("turned") % 4], [ikdup[:, t].rearrange("p h d -> p (h d)") for t in range(TT)])
                n.add("rows", TT)
                n.add("heads", 1)
                n.add("pow", 3 * TT)

            def index2(self):
                n, e = self.n, self.e
                e.wait_ge(turned_out, n("turned"))
                for i in range(IH * TT):
                    t, h = divmod(i, IH)
                    w = (t + 1) * P
                    if i >= 4:
                        e.wait_ge(logit_relu, n("logits", i - 3))
                    nc.tensor.matmul(bank[i % 4][:, 0:w], pair("iq", h, t * P, w),
                                     pairs_t[DH * (h % 2):DH * (h % 2) + DH, PAIR["ik"], 0:w], start=True, stop=True).then_inc(logit_full, 1)
                n.add("logits", IH * TT)
                e.wait_ge(logit_relu, n("logits"))
                e.wait_ge(seen_ready, TT * (n("index") + 1))
                n.add("index", 1)

            def attend2(self, l):
                n, e = self.n, self.e
                self.attention(items2(), probs2, probs_t2)
                e.wait_ge(prob_t, n("items"))
                for t in range(TT):
                    e.wait_ge(rows_ready, n("rows", TT))
                    for j in range(2):
                        for q in range(TT):
                            h = 2 * t + j
                            ins = nc.tensor.transpose(bank[4 + t][:, (2 * j + q) * P:(2 * j + q + 1) * P],
                                                      diff_rows[:, q, h * P:(h + 1) * P], ident)
                    ins.then_inc(mix_full, 1)
                n.add("rows", TT)
                n.add("mix", 4)
                n.add("pow", TT)

            def finish(self):
                n, e = self.n, self.e
                e.wait_ge(residual_new, n("residual"))
                for t in range(TT):
                    for i in range(2):
                        for k in range(4):
                            ins = nc.tensor.transpose(bank[i + 2 * t][:, k * P:(k + 1) * P],
                                                      residual[:, 4 * i + k, (FIN * NT) + t * P:(FIN * NT) + (t + 1) * P], ident)
                        ins.then_inc(turned, 1)
                        n.add("turned", 1)

        FIN = debug[2] if debug else 0

        counter = Phases(None)
        program(counter)
        TOTAL[0] = counter.n.static("chunks")

        @block.sync
        def _(eng):
            program(Sync(eng))

        @block.gpsimd
        def _(eng):
            program(Pool(eng))

        @block.scalar
        def _(eng):
            program(Scalar(eng))

        @block.vector
        def _(eng):
            program(Vector(eng))

        @block.tensor
        def _(eng):
            program(Tensor(eng))


def kernel(**inputs):
    import numpy as _np
    import concourse.bacc as _bacc
    from concourse import mybir as _mybir
    from concourse.bass_utils import run_bass_kernel_spmd as _run

    nc = _bacc.Bacc("TRN2", target_bir_lowering=False, num_devices=1)
    arrays, aps = {}, {}
    for name, a in inputs.items():
        a = _np.ascontiguousarray(a)
        arrays[f"in_{name}"] = a
        aps[name] = nc.dram_tensor(f"in_{name}", a.shape, _mybir.dt.from_np(a.dtype), kind="ExternalInput").ap()
    arrays["consts"] = constant_table()
    consts = nc.dram_tensor("consts", arrays["consts"].shape, F32, kind="ExternalInput").ap()
    out = nc.dram_tensor("out", (1, NT, D), F32, kind="ExternalOutput").ap()
    build(nc, aps, consts, out)
    return _run(nc, [arrays], core_ids=[0]).results[0]["out"]
```

```python
from contextlib import ExitStack

import numpy as np

import concourse.bass as bass
from concourse import mybir

F32 = mybir.dt.float32
F32R = mybir.dt.float32r
BF16 = mybir.dt.bfloat16
ALU = mybir.AluOpType
ACT = mybir.ActivationFunctionType
AX = mybir.AxisListType

P = 128
D = 1024
KT = D // P
NT = 256
TT = NT // P
DH = 64
EPS = 1e-6
DEPTH = 2
MASKED = -1.0e30
TAKEN = -3.0e38
RAW, SPLIT = 4, 4
BODY = 4
WIDE = KT // 2
CW = 256

Q1, K1, V1, F1, U1, G1, IN1 = 0, 512, 640, 768, 1024, 1280, 1536
NQ1, NKV1 = 8, 2
FF1 = 4096
MQ, MK, MV, DQ, DK, DV, SQ, SK, SV, IQ, IK, IW, IN2 = (
    0, 256, 512, 768, 1280, 1792, 2304, 2560, 2816, 3072, 3584, 3648, 3656)
FF2 = 2816
IH = 8
TOPK = NT // 4

CONSTS = dict(ident=P, dft_n=TT * 2 * NT, dft_c=P, dft_s=P, cos1=TT * DH, sin1=TT * DH, cos2=TT * DH, sin2=TT * DH,
              mask=NT, sel=2)


def constant_table():
    t = {k: np.zeros((P, w), np.float32) for k, w in CONSTS.items()}
    t["ident"][:] = np.eye(P)
    n = np.arange(NT)
    ang = 2 * np.pi * ((n[:, None] * n[None, :]) % NT) / NT
    cs = np.concatenate([np.cos(ang), np.sin(ang)], 1)
    t["dft_n"][:] = cs.reshape(TT, P, 2 * NT).transpose(1, 0, 2).reshape(P, -1)
    d = np.arange(DH)
    ang = 2 * np.pi * ((d[:, None] * d[None, :]) % DH) / DH
    norm = 1.0 / np.sqrt(NT * DH)
    t["dft_c"][:] = np.kron(np.eye(2), np.cos(ang)) * norm
    t["dft_s"][:] = np.kron(np.eye(2), -np.sin(ang)) * norm
    pos = np.arange(NT, dtype=np.float32)
    inv = (np.float32(10000.0) ** (-np.arange(0, 32, 2, dtype=np.float32) / np.float32(32))).astype(np.float32)
    row, col = np.floor(pos / 64)[:, None] * inv, (pos % 64)[:, None] * inv
    inv2 = (np.float32(1.0) / (np.float32(10000.0) ** (np.arange(0, 64, 2, dtype=np.float32) / np.float32(64))))
    ang2 = pos[:, None] * inv2.astype(np.float32)
    for name, f, a in (("cos1", np.cos, 0), ("sin1", np.sin, 1), ("cos2", np.cos, 0), ("sin2", np.sin, 1)):
        parts = [row, row, col, col] if name[-1] == "1" else [ang2, ang2]
        v = [f(x) * (-1 if a and i % 2 == 0 else 1) for i, x in enumerate(parts)]
        t[name][:] = np.concatenate(v, 1).reshape(TT, P, DH).transpose(1, 0, 2).reshape(P, -1)
    t["mask"][:, P:] = np.where(np.arange(P)[None, :] <= np.arange(P)[:, None], 0, MASKED)
    t["sel"][0:5] = [[1, 0], [0, 1], [1, 0], [0, 1], [1, 1]]
    return np.concatenate([t[k] for k in CONSTS], 1).astype(np.float32)


class Tally:

    def __init__(self):
        self.n, self.it, self.step, self.last = {}, None, {}, {}

    def __call__(self, name, k=0):
        v = self.n.get(name, 0) + k
        s = self.step.get(name, 0)
        return v + self.it * s if self.it is not None and s else v

    def static(self, name):
        return self.n.get(name, 0)

    def add(self, name, k=1):
        self.n[name] = self.n.get(name, 0) + k

    def begin(self, it, step):
        self.it, self.step, self.last = it, step, dict(self.n)

    def end(self, times):
        for name, v in list(self.n.items()):
            d = v - self.last.get(name, 0)
            assert d == self.step.get(name, 0), (name, d, self.step.get(name, 0))
            self.n[name] = v + d * (times - 1)
        self.it, self.step = None, {}


def run_chunks(eng, n, count, per_chunk, body, tail=0, least=1):
    m = count - tail
    head = (m - 1) % BODY + 1 if m else 0
    while head < min(least, m):
        head += BODY
    times = (m - head) // BODY
    for j in range(head):
        body(j, j)
    if times == 1:
        for j in range(head, m):
            body(j, j)
    elif times > 1:
        with eng.Fori(0, times) as it:
            n.begin(it, {k: v * BODY for k, v in per_chunk.items()})
            for j in range(BODY):
                body(head + j, it * BODY + (head + j))
            n.end(times)
    for j in range(m, count):
        body(j, j)


def build(nc, A, consts, out, debug=None):
    top = ExitStack()
    with top:
        def sb(name, shape, dt=F32, stack=top):
            return stack.enter_context(nc.sbuf_tensor(name, shape, dt))

        def sem(name):
            return top.enter_context(nc.semaphore(name))

        residual = sb("residual", [P, KT, 2 * NT])
        act_hi = sb("act_hi", [P, KT, NT], F32R)
        act_lo = sb("act_lo", [P, KT, NT], F32R)
        raw = sb("raw", [P, RAW, 2048])
        w_hi = sb("w_hi", [P, SPLIT, 1024], F32R)
        w_lo = sb("w_lo", [P, SPLIT, 1024], F32R)
        const = sb("const", [P, sum(CONSTS.values())])
        cols, at = {}, 0
        for name, w in CONSTS.items():
            cols[name] = const[:, at:at + w]
            at += w
        ident, sel, mask = cols["ident"], cols["sel"], cols["mask"]
        dft_n = cols["dft_n"].rearrange("p (t n) -> p t n", t=TT)
        rope = {b: [cols[f"{f}{b}"].rearrange("p (t d) -> p t d", t=TT) for f in ("cos", "sin")] for b in (1, 2)}
        ones = sb("ones", [P, P])
        neg_half = sb("neg_half", [P, DH])
        cond = sb("cond", [P, KT, P], F32R)
        k_t = sb("k_t", [P, NKV1, 2 * NT])
        v_rows = sb("v_rows", [P, 2 * TT, NKV1 * DH])
        mod = sb("mod", [P, 48, 2])
        mscale = sb("mscale", [P, 2, KT, 2])
        norm_g = sb("norm_g", [P, 2, KT])
        gains1 = sb("gains1", [P, 2 * DH + 256])
        w_sp = sb("w_sp", [P, 4, P])
        b_sp = sb("b_sp", [P, 4])
        norm2_g = sb("norm2_g", [P, 2, KT])
        gains2 = sb("gains2", [P, 3, 2, DH])
        lam_in = sb("lam_in", [P, 4 * DH])
        sub_g = sb("sub_g", [P, 2 * DH])
        variance = sb("variance", [P, DH])
        rstd = sb("rstd", [P, DH])
        diag = sb("diag", [P, TT, P])
        ident_b = sb("ident_b", [P, P], BF16)
        mask_b = sb("mask_b", [P, P], BF16)
        neg_max = sb("neg_max", [P, 64])
        total = sb("total", [P, 64])
        lam = sb("lam", [P, 8])
        best = sb("best", [P, 8])

        with ExitStack() as s:
            rows_in = sb("rows_in", [P, 2 * TT, D], stack=s)
            cond_raw = sb("cond_raw", [P, 4, KT, 2], stack=s)
            mod_rows = sb("mod_rows", [5, 6 * D], stack=s)
        with ExitStack() as s:
            proj1 = sb("proj1", [P, TT, IN1], stack=s)
            q_t = sb("q_t", [P, NQ1 // 2, NT], stack=s)
            kdup = sb("kdup", [P, TT, 2 * NKV1, DH], stack=s)
            probs1 = sb("probs1", [P, 4, 2 * NT], stack=s)
            probs_t1 = sb("probs_t1", [P, 3, 2 * TT, P], stack=s)
            four = sb("four", [P, 2, 2 * NT], stack=s)
            w_sp_t = sb("w_sp_t", [P, 4, P], stack=s)
            gates = sb("gates", [P, TT, 512], stack=s)
            gtmp = sb("gtmp", [P, TT, 512], stack=s)
            head_sq1 = sb("head_sq1", [P, 2, 512], stack=s)
            rope_a1 = sb("rope_a1", [P, 2, 512], stack=s)
            rope_b1 = sb("rope_b1", [P, 2, 512], stack=s)
            cos_g1 = sb("cos_g1", [P, 2, TT, DH], stack=s)
            sin_g1 = sb("sin_g1", [P, 2, TT, DH], stack=s)
        with ExitStack() as s:
            proj2 = sb("proj2", [P, TT, IN2], stack=s)
            pairs_t = sb("pairs_t", [P, 21, NT], stack=s)
            ikdup = sb("ikdup", [P, TT, 2, DH], stack=s)
            seen = sb("seen", [P, TT, NT], BF16, stack=s)
            relu_t = sb("relu_t", [P, 2, NT], stack=s)
            score = sb("score", [P, TT, NT], stack=s)
            diff_rows = sb("diff_rows", [P, TT, 4 * P], stack=s)
            diff_sq = sb("diff_sq", [P, 4 * P], stack=s)
            cos_g2 = sb("cos_g2", [P, 6, TT, DH], stack=s)
            sin_g2 = sb("sin_g2", [P, 6, TT, DH], stack=s)
            with ExitStack() as s2:
                head_sq2 = sb("head_sq2", [P, 2, 512], stack=s2)
                rope_a2 = sb("rope_a2", [P, 2, 512], stack=s2)
                rope_b2 = sb("rope_b2", [P, 2, 512], stack=s2)
            with ExitStack() as s2:
                probs2 = sb("probs2", [P, 6, NT], stack=s2)
                probs_t2 = sb("probs_t2", [P, 3, TT, P], stack=s2)
        with ExitStack() as s:
            hid_hi = sb("hid_hi", [P, FF1 // P, NT], F32R, stack=s)
            hid_lo = sb("hid_lo", [P, FF1 // P, NT], F32R, stack=s)
            fa = sb("fa", [P, 2, 2 * NT], stack=s)
            fb = sb("fb", [P, 2, 2 * NT], stack=s)
            wide = sb("wide", [P, KT, NT], stack=s)

        bank = [top.enter_context(nc.psum_tensor(f"bank{i}", [P, 512], F32)) for i in range(8)]

        raw_loaded = [sem(f"raw_loaded{i}") for i in range(RAW)]
        hi_ready = sem("hi_ready")
        lo_ready = sem("lo_ready")
        multiplied = sem("multiplied")
        drained_act = sem("drained_act")
        squared = sem("squared")
        relued = sem("relued")
        gate_exp = sem("gate_exp")
        gated = sem("gated")
        gate_hi = sem("gate_hi")
        hidden = sem("hidden")
        residual_new = sem("residual_new")
        squares = sem("squares")
        folded = sem("folded")
        sums = sem("sums")
        rstd_diag = sem("rstd_diag")
        rstd_wide = sem("rstd_wide")
        var_ready = sem("var_ready")
        rstd_ready = sem("rstd_ready")
        modulated = sem("modulated")
        norm_hi = sem("norm_hi")
        norm_lo = sem("norm_lo")
        consts_in = sem("consts_in")
        inputs_in = sem("inputs_in")
        cond_in = sem("cond_in")
        params_in = sem("params_in")
        params2_in = sem("params2_in")
        preset = sem("preset")
        cond_exp = sem("cond_exp")
        cond_hi = sem("cond_hi")
        cond_ready = sem("cond_ready")
        mod_full = sem("mod_full")
        mod_ready = sem("mod_ready")
        turned = sem("turned")
        turned_out = sem("turned_out")
        head_squares = sem("head_squares")
        rope_cos = sem("rope_cos")
        gates_ready = sem("gates_ready")
        tables_ready = sem("tables_ready")
        rows_ready = sem("rows_ready")
        v_kept = sem("v_kept")
        scored = sem("scored")
        max_ready = sem("max_ready")
        exped = sem("exped")
        prob_ready = sem("prob_ready")
        prob_turned = sem("prob_turned")
        prob_t = sem("prob_t")
        mixed = sem("mixed")
        mix_hi = sem("mix_hi")
        mix_lo = sem("mix_lo")
        dft_full = sem("dft_full")
        dft_out = sem("dft_out")
        mix_full = sem("mix_full")
        gelu_in = sem("gelu_in")
        gelu_tanh = sem("gelu_tanh")
        spatial = sem("spatial")
        logit_full = sem("logit_full")
        logit_relu = sem("logit_relu")
        logit_used = sem("logit_used")
        seen_ready = sem("seen_ready")
        lam_exp = sem("lam_exp")
        lam_sums = sem("lam_sums")
        diff_drained = sem("diff_drained")
        final_rows = sem("final_rows")
        stored = sem("stored")
        act_order = sem("act_order")
        dve_order = sem("dve_order")
        block = top.enter_context(nc.Block())

        A_ = A
        TOTAL = [0]

        def program(ph):
            ph.load()
            ph.params(0)
            for l in range(DEPTH):
                ph.ada(l)
                ph.modulation(l)
                for s in (1, 0):
                    kv_only = s == 1 and l == DEPTH - 1
                    ph.norm(s, 1, 0, False)
                    ph.rows(rows1(s, kv_only), A_["w_in"], l)
                    if kv_only:
                        continue
                    ph.attend1(s)
                    ph.fourier()
                    ph.spatial_gate()
                    ph.down("mix", D // P // 2, dict(w=A_["w_out"], l=l), s, 16, True)
                    if debug == ("wout", l, s): return ph.finish()
                    ph.norm(s, 1, 1, True)
                    ph.up("relu2", FF1 // CW, dict(w=A_["w_mlp1"], l=l, base=0))
                    ph.down("hidden", FF1 // P // 2, dict(w=A_["w_mlp2"], l=l), s, 40, l == DEPTH - 1)
                    if debug == ("layer", l, s): return ph.finish()
                if l + 1 < DEPTH:
                    ph.params(l + 1)
            for l in range(DEPTH):
                ph.params2(l)
                ph.norm(0, 2, 0, True)
                ph.rows(rows2(), A_["w_in_2"], l)
                ph.attend2(l)
                ph.down("mix", D // P // 2, dict(w=A_["w_out_2"], l=l), 0, None, True)
                ph.norm(0, 2, 1, True)
                ph.up("silu", FF2 // P, dict(w=A_["w_gate_2"], w2=A_["w_up_2"], l=l, base=0))
                ph.down("hidden", FF2 // P // 2, dict(w=A_["w_down_2"], l=l), 0, None, l < DEPTH - 1)
                if debug == ("layer2", l, 0): return ph.finish()
            ph.finish()

        PER_CHUNK = {}

        def tiles(ap, k):
            return ap.rearrange("p (k n) -> p k n", k=k)

        class Phases:

            def __init__(self, eng):
                self.e, self.n = eng, Tally()
                self.behind = ()

            def tail(self, count):
                return BODY if self.n.static("chunks") + count == TOTAL[0] else 0

            def load(self): self.n.add("turned", 8)
            def params(self, l): self.n.add("params", 1)
            params2 = params
            def ada(self, l): self.chunks("ada", 24)
            def up(self, kind, count, w): self.chunks(kind, count)
            def down(self, kind, count, w, s, gate, norm_next):
                self.chunks("down", count)
                self.n.add("residual", KT)

            def chunks(self, kind, count):
                self.n.add("chunks", count)
                if kind in ("rows1", "rows2", "ada"):
                    self.n.add("drained_act", count)
                if kind == "relu2":
                    self.n.add("drained_act", count)
                    self.n.add("hidden", count)
                if kind == "silu":
                    self.n.add("gated", count)
                    self.n.add("hidden", count)

            def modulation(self, l): self.n.add("mod", 1)
            def norm(self, s, b, which, summed):
                self.n.add("norm", 1)
                self.n.add("pow", 1)
            def rows(self, plan, w, l):
                self.n.add("chunks", len(plan))
                self.n.add("drained_act", len(plan))

            def attend1(self, s):
                self.n.add("scores", 16)
                self.n.add("items", 16)
                self.n.add("mix", 2)
            def fourier(self):
                self.n.add("fourier", 1)
                self.n.add("mix", 1)
            def spatial_gate(self):
                self.n.add("gmlp", 1)
                self.n.add("turned", 1)
                self.n.add("mix", 1)
            def attend2(self, l):
                self.n.add("scores", 32)
                self.n.add("items", 24)
                self.n.add("mix", 4)
            def finish(self): pass

        def items1(s):
            keys = TT if s == 1 else 2 * TT
            out = []
            for h in range(NQ1):
                kv, half = h // (NQ1 // NKV1), DH * (h % 2)
                for qt in range(TT):
                    q = q_t[half:half + DH, h // 2, qt * P:(qt + 1) * P]
                    k = k_t[half:half + DH, kv, 0:keys * P]
                    v = [v_rows[:, i, kv * DH:(kv + 1) * DH] for i in range(keys)]
                    o = bank[6 + h // 4][half:half + DH, (h // 2 % 2) * NT + qt * P:(h // 2 % 2) * NT + (qt + 1) * P]
                    out.append(dict(scores=[(q, k, None)], keys=keys, v=v, o=o,
                                    done=(6 + h // 4, 2 * (h // 4)) if h % 4 == 3 and qt == TT - 1 else None))
            return out

        PAIR = dict(mq=0, mk=2, dq=4, dk=8, sq=12, sk=14, iq=16, ik=20)

        def pair(name, h, lo, hi):
            half = DH * (h % 2)
            return pairs_t[half:half + DH, PAIR[name] + h // 2, lo:hi]

        def heads_of(ap):
            return ap.rearrange("p t (h d) -> p t h d", d=DH)

        def rows1(s, kv_only):
            sin = [sin_g1[:, i] if s == 0 else None for i in range(2)]
            cos = [cos_g1[:, i] if s == 0 else gains1[:, i * DH:(i + 1) * DH].unsqueeze(1).broadcast_to([P, TT, DH])
                   for i in range(2)]
            kd = kdup[:].rearrange("p t (h c) d -> p t h c d", c=2)
            kt0 = 0 if s == 1 else TT
            common = dict(block=1, stream=s, normed=True, axes=2, sq=head_sq1, a=rope_a1, b=rope_b1)
            plan = [dict(col=K1, wd=CW, v_kept=kt0,
                         heads=dict(common, n=NKV1, x=heads_of(proj1[:, :, K1:K1 + NKV1 * DH]), cos=cos[1], sin=sin[1],
                                    dst=[kd[:, :, :, c, :] for c in range(2)],
                                    turn=[kdup[:, t, 2 * j:2 * j + 2, :].rearrange("p h d -> p (h d)") for j in range(2) for t in range(TT)],
                                    out=k_t[:, :, kt0 * P:(kt0 + TT) * P], scale=None))]
            if kv_only:
                return plan
            for i in range(2):
                c = Q1 + i * CW
                x = heads_of(proj1[:, :, c:c + CW])
                plan.append(dict(col=c, wd=CW, heads=dict(
                    common, n=4, x=x, cos=cos[0], sin=sin[0], dst=[x],
                    turn=[proj1[:, t, c + j * P:c + (j + 1) * P] for j in range(2) for t in range(TT)],
                    out=q_t[:, 2 * i:2 * i + 2, :], scale=DH ** -0.5)))
            plan += [dict(col=G1, wd=CW, gelu=1), dict(col=U1, wd=CW, gelu=0), dict(col=F1, wd=CW)]
            return plan

        INDEX_AT, SEARCH_AT = 6, 11

        def rows2():
            common = dict(block=2, stream=0, axes=1, sq=head_sq2, a=rope_a2, b=rope_b2)
            plan = []
            for c, p0, g, q in ((IQ, 16, None, 1), (IQ + CW, 18, None, 1), (IK, 20, None, 0), (MQ, 0, 0, 1), (MK, 2, 1, 0),
                                (SQ, 12, 4, 1), (SK, 14, 5, 0), (DQ, 4, 2, 1), (DQ + CW, 6, 2, 1), (DK, 8, 3, 0), (DK + CW, 10, 3, 0)):
                one = c == IK
                n = 1 if one else 4
                x = heads_of(proj2[:, :, c:c + n * DH])
                plan.append(dict(col=c, wd=IN2 - IK if one else CW, heads=dict(
                    common, normed=g is not None, n=n, x=x, dst=[ikdup[:, :, i:i + 1, :] for i in range(2)] if one else [x],
                    cos=rope[2][0] if g is None else cos_g2[:, g], sin=rope[2][1] if g is None else sin_g2[:, g],
                    turn=[ikdup[:, t].rearrange("p h d -> p (h d)") for t in range(TT)] if one else
                         [proj2[:, t, c + j * P:c + (j + 1) * P] for j in range(2) for t in range(TT)],
                    out=pairs_t[:, p0:p0 + (1 if one else 2), :], scale=DH ** -0.5 if q else None)))
            return plan + [dict(col=c, wd=CW) for c in (SV, MV, DV, DV + CW)]

        def causal(qt):
            return mask[:, P:2 * P] if qt == 0 else mask[:, :]

        def items2():
            out = []
            for h in range(4):
                for qt in range(TT):
                    n = (qt + 1) * P
                    half = DH * (h % 2)
                    o = bank[6][half:half + DH, h // 2 * NT + qt * P:h // 2 * NT + (qt + 1) * P]
                    out.append(dict(scores=[(pair("mq", h, qt * P, n), pair("mk", h, 0, n), mask_b[:])], keys=qt + 1,
                                    v=[proj2[:, i, MV + h * DH:MV + (h + 1) * DH] for i in range(qt + 1)], o=o,
                                    done=(6, 0) if h == 3 and qt == TT - 1 else None))
            dsa = []
            for h in range(4):
                for qt in range(TT):
                    n = (qt + 1) * P
                    half = DH * (h % 2)
                    o = bank[7][half:half + DH, h // 2 * NT + qt * P:h // 2 * NT + (qt + 1) * P]
                    dsa.append(dict(scores=[(pair("sq", h, qt * P, n), pair("sk", h, 0, n), seen[:, qt, 0:n])],
                                    keys=qt + 1, o=o, done=(7, 6) if h == 3 and qt == TT - 1 else None,
                                    v=[proj2[:, i, SV + h * DH:SV + (h + 1) * DH] for i in range(qt + 1)]))
            for qt in range(TT):
                for h in range(4):
                    n = (qt + 1) * P
                    o = bank[7 - qt][:, h * P:(h + 1) * P]
                    out.append(dict(scores=[(pair("dq", 2 * h + i, qt * P, n), pair("dk", 2 * h + i, 0, n), mask_b[:])
                                            for i in range(2)],
                                    keys=qt + 1, o=o, diff=True, done=(7 - qt, ("rows", qt)) if h == 3 else None,
                                    v=[proj2[:, i, DV + h * P:DV + (h + 1) * P] for i in range(qt + 1)]))
            return out + dsa

        class Sync(Phases):
            def load(self):
                super().load()
                self.e.dma_start(rows_in[:, 0:TT, :], A_["x"][0].rearrange("(t p) n -> p t n", p=P)).then_inc(inputs_in, 16)
                self.e.dma_start(rows_in[:, TT:, :], A_["ctx"][0].rearrange("(t p) n -> p t n", p=P)).then_inc(inputs_in, 16)
                self.e.dma_start(const[:], consts).then_inc(consts_in, 16)

            def chunk_loads(self, count, pieces, tail=0):
                e, n = self.e, self.n
                base = n.static("chunks")

                def body(j, at):
                    slot = (base + j) % RAW
                    if n.static("chunks") >= RAW:
                        e.wait_ge(lo_ready, n("halves", -2 * (RAW - 1)))
                    for dst, src in pieces(slot, j, at):
                        e.dma_start(dst, src).then_inc(raw_loaded[slot], 16)
                    n.add("chunks", 1)
                    n.add("halves", 2)

                run_chunks(e, n, count, dict(chunks=1, halves=2), body, tail)

            def kslices(self, w, l, base, width):
                src = w[l].rearrange("(k p) n -> p k n", p=P)

                def pieces(slot, j, at):
                    dst = tiles(raw[:, slot, :], KT)
                    wd = min(CW, width - j * CW)
                    for h in range(2):
                        yield (dst[:, 4 * h:4 * h + 4, 0:wd], src[:, 4 * h:4 * h + 4, bass.ds(at * CW + base, wd)])
                return pieces

            def ada(self, l):
                self.chunk_loads(24, self.kslices(A_["w_ada"], l, 0, 6 * D))

            def up(self, kind, count, w):
                if kind != "silu":
                    self.chunk_loads(count, self.kslices(w["w"], w["l"], w["base"], FF1))
                    return
                gate, up_ = (w[k][w["l"]].rearrange("(k p) n -> p k n", p=P) for k in ("w", "w2"))

                def pieces(slot, j, at):
                    dst = tiles(raw[:, slot, :], KT)
                    yield dst[:, :, 0:P], gate[:, :, bass.ds(at * P, P)]
                    yield dst[:, :, P:2 * P], up_[:, :, bass.ds(at * P, P)]
                self.chunk_loads(count, pieces)

            def rows(self, plan, w, l):
                src = w[l].rearrange("(k p) n -> p k n", p=P)

                def pieces(slot, j, at):
                    c = plan[j]
                    for h in range(2):
                        yield (tiles(raw[:, slot, :], KT)[:, 4 * h:4 * h + 4, 0:c["wd"]],
                               src[:, 4 * h:4 * h + 4, c["col"]:c["col"] + c["wd"]])
                self.chunk_loads(len(plan), pieces, len(plan))

            def down(self, kind, count, w, s, gate, norm_next):
                src = w["w"][w["l"]].rearrange("(c k p) n -> p c k n", p=P, k=2)

                last = w["w"][w["l"]].rearrange("(k p) n -> p k n", p=P)[:, 2 * count - KT:, :]

                def pieces(slot, j, at):
                    c = j - (count - WIDE)
                    for k in range(2):
                        if c < 0:
                            yield tiles(raw[:, slot, :], 2)[:, k, :], src[:, at, k, :]
                        else:
                            yield tiles(raw[:, slot, :], KT)[:, 4 * k:4 * k + 4, :], last[:, 4 * k:4 * k + 4, c * CW:(c + 1) * CW]
                self.chunk_loads(count, pieces, WIDE)
                self.n.add("residual", KT)

            def modulation(self, l):
                super().modulation(l)

            def finish(self):
                for i in range(2):
                    self.e.wait_ge(final_rows, 2 * TT * (i + 1))
                    self.e.dma_start(out[0].rearrange("(t p) n -> p t n", p=P)[:, :, i * 512:(i + 1) * 512],
                                     rows_in[:, 0:TT, i * 512:(i + 1) * 512]).then_inc(stored, 16)
                self.e.wait_ge(stored, 2 * 16)

        class Pool(Phases):
            def load(self):
                super().load()
                nc.gpsimd.memset(ones[:], 1.0).then_inc(preset, 1)
                nc.gpsimd.memset(neg_half[:], -0.5).then_inc(preset, 1)
                for i, name in enumerate(("c", "c_ctx")):
                    src = A_["c"][0] if name == "c" else A_["c_ctx"]
                    self.e.dma_start(cond_raw[:, 0, :, i], src.rearrange("(k p) -> p k", p=P), allow_slow_non_contiguous=True).then_inc(cond_in, 16)
                self.e.wait_ge(preset, 2)

            def ada(self, l):
                if l == 0:
                    self.e.wait_ge(turned_out, 8)
                else:
                    self.e.wait_ge(residual_new, self.n("residual"))
                self.e.dma_start(mod_rows[4:5, :], A_["b_ada"][l:l + 1, :]).then_inc(params_in, 16)
                super().ada(l)

            def params(self, l):
                e = self.e
                if l:
                    e.wait_ge(residual_new, self.n("residual"))
                for i, k in enumerate(("norm1_g", "norm2_g")):
                    e.dma_start(norm_g[:, i, :], A_[k][l].rearrange("(k p) -> p k", p=P), allow_slow_non_contiguous=True).then_inc(params_in, 16)
                at = 0
                for k, w in (("q_norm_g", DH), ("k_norm_g", DH), ("gmlp_v_g", 256)):
                    e.dma_start(gains1[:, at:at + w], A_[k][l:l + 1, :].broadcast_to([P, w])).then_inc(params_in, 16)
                    at += w
                e.dma_start(w_sp[:], A_["w_spatial"][l].rearrange("h p q -> p h q")).then_inc(params_in, 16)
                e.dma_start(b_sp[:], A_["b_spatial"][l].rearrange("h p -> p h"), allow_slow_non_contiguous=True).then_inc(params_in, 16)
                super().params(l)

            def params2(self, l):
                e = self.e
                if l:
                    e.wait_ge(residual_new, self.n("residual"))
                for i, k in enumerate(("attn_norm_g_2", "ffn_norm_g_2")):
                    e.dma_start(norm2_g[:, i, :], A_[k][l].rearrange("(k p) -> p k", p=P), allow_slow_non_contiguous=True).then_inc(params2_in, 16)
                for i, k in enumerate(("q_norm_g_2", "k_norm_g_2")):
                    e.dma_start(gains2[:, :, i, :], A_[k][l:l + 1].broadcast_to([P, 3, DH])).then_inc(params2_in, 16)
                e.dma_start(tiles(lam_in[:], 4), A_["diff_lambda_2"][l:l + 1].broadcast_to([P, 4, DH])).then_inc(params2_in, 16)
                e.dma_start(sub_g[:], A_["diff_subln_g_2"][l:l + 1, :].broadcast_to([P, P])).then_inc(params2_in, 16)
                self.n.add("params", 1)

            def power(self, at, w):
                self.e.wait_ge(var_ready, self.n("pow", 1))
                nc.gpsimd.tensor_tensor(rstd[:, at:at + w], variance[:, at:at + w], neg_half[:, 0:w], ALU.pow).then_inc(rstd_ready, 1)
                self.n.add("pow", 1)

            def norm(self, s, b, which, summed):
                n, e = self.n, self.e

                def fold(step, squared_, o, a, b):
                    e.wait_ge(squares, 5 * n("norm") + squared_)
                    if step:
                        e.wait_ge(folded, 3 * n("norm") + step)
                    nc.gpsimd.tensor_tensor(o, a, b, ALU.add).then_inc(folded, 1)
                fold(0, 2, wide[:, 0:2, :], wide[:, 0:2, :], wide[:, 2:4, :])
                fold(1, 3, wide[:, 0:2, :], wide[:, 0:2, :], wide[:, 4:6, :])
                fold(2, 3, wide[:, 0:1, :], wide[:, 0:1, :], wide[:, 1:2, :])
                self.power(0, TT)
                n.add("norm", 1)

            def rows(self, plan, w, l):
                n, e = self.n, self.e
                n.add("tables", 1)
                e.wait_ge(tables_ready, n("tables"))
                r = m = 0
                for j, c in enumerate(plan):
                    n.add("drained_act", 1)
                    h = c.get("heads")
                    if h:
                        e.wait_ge(drained_act, n("drained_act"))
                        if r >= 2:
                            e.wait_ge(rows_ready, n("rows", r - 1))
                        x = h["x"]
                        nc.gpsimd.tensor_tensor(heads_of(tiles(h["a"][:, r % 2, 0:TT * h["n"] * DH], TT)), x,
                                                h["cos"].unsqueeze(2).broadcast_to([P, TT, h["n"], DH]), ALU.mult).then_inc(rope_cos, 1)
                        r += 1
                        if h["normed"]:
                            self.power(16 * (m % 2), TT * h["n"])
                            m += 1
                    if c.get("gelu") == 1:
                        self.power(32, 4 * TT)
                n.add("chunks", len(plan))
                n.add("rows", r)

            def attend2(self, l):
                for t in range(TT):
                    self.power(8 * t, 4)
                self.n.add("rows", TT)
                super().attend2(l)

        PARAM_DMAS = [0]

        def params_until(phase, l):
            if phase == "params":
                return 16 * (8 * l + 7)
            if phase == "bias":
                return 16 * (8 * l + 8)
            return 16 * (8 * DEPTH + 6 * (l + 1))

        class Scalar(Phases):
            def __init__(self, eng):
                super().__init__(eng)
                self.var0 = 0

            def order(self, ins):
                ins.then_inc(act_order, 1)
                self.n.add("act_order", 1)
                self.e.wait_ge(act_order, self.n("act_order"))

            def split(self, k, halves=(0, 1)):
                n, e = self.n, self.e
                c = n.static("chunks") + k
                e.wait_ge(raw_loaded[c % RAW], self.loaded(c, k))
                for h in halves:
                    if 2 * c + h >= SPLIT:
                        e.wait_ge(multiplied, n("halves", 2 * k + h + 1 - SPLIT))
                    nc.scalar.copy(w_hi[:, (2 * c + h) % SPLIT, :], raw[:, c % RAW, h * 1024:(h + 1) * 1024]).then_inc(hi_ready, 1)

            def loaded(self, c, k):
                v = 32 * (c // RAW + 1)
                s = self.n.step.get("chunks", 0)
                return v + self.n.it * (32 * (s // RAW)) if self.n.it is not None and s else v

            def stream(self, count, kind, drain, extra=None, tail=0, finish=None, early=False):
                n = self.n
                self.catch_up()

                def body(j, at):
                    if drain:
                        self.e.wait_ge(multiplied, n("halves", 2))
                        drain(j, at)
                    if n.static("chunks") + 2 < TOTAL[0]:
                        if j < count - 1:
                            self.split(2)
                        elif early:
                            self.split(2, (0,))
                    if finish:
                        finish(j, at)
                    n.add("chunks", 1)
                    n.add("halves", 2)

                run_chunks(self.e, n, count, dict(chunks=1, halves=2, **(extra or {})), body, max(tail, 1))
                self.behind = ((1,) if early else (0, 1)) if n.static("chunks") + 1 < TOTAL[0] else ()

            def catch_up(self):
                if self.behind:
                    self.split(1, self.behind)
                    self.behind = ()

            def load(self):
                super().load()
                e = self.e
                e.wait_ge(cond_in, 32)
                nc.scalar.activation(cond_raw[:, 1, :, :], cond_raw[:, 0, :, :], ACT.Exp, scale=-1.0).then_inc(cond_exp, 1)
                self.split(0)
                self.split(1)

            def ada(self, l):
                def drain(j, at):
                    b = bank[j % 4]
                    self.e.wait_ge(preset, 2)
                    nc.scalar.copy(mod_rows[0:4, bass.ds(at * CW, CW)], b[0:4, 0:CW]).then_inc(drained_act, 1)
                    self.n.add("drained_act", 1)
                if l == 0:
                    self.e.wait_ge(turned_out, 8)
                self.stream(24, "ada", drain, dict(drained_act=1))

            def up(self, kind, count, w):
                n, e = self.n, self.e
                if kind == "relu2":
                    def drain(j, at):
                        if j >= 2:
                            e.wait_ge(hidden, n("hidden", -1))
                        nc.scalar.activation(fa[:, j % 2, :], bank[j % 4][:], ACT.Relu).then_inc(drained_act, 1)
                        n.add("drained_act", 1)
                        n.add("hidden", 1)
                        e.wait_ge(drained_act, n("drained_act"))
                        e.wait_ge(preset, 2)
                        nc.scalar.activation(hid_hi[:, bass.ds(at * 2, 2), :], tiles(fa[:, j % 2, :], 2),
                                             ACT.Square).then_inc(squared, 1)
                    self.stream(count, kind, drain, dict(drained_act=1, hidden=1))
                else:
                    def drain(j, at):
                        if j >= 2:
                            e.wait_ge(hidden, n("hidden", -1))
                        ex = fa[:, j % 2, 0:NT]
                        self.order(nc.scalar.activation(ex, bank[j % 4][:, 0:NT], ACT.Exp, scale=-1.0))
                        nc.scalar.add(ex, ex, 1.0).then_inc(gate_exp, 1)

                    def finish(j, at):
                        n.add("hidden", 1)
                        n.add("gated", 1)
                        e.wait_ge(gated, n("gated"))
                        e.wait_ge(preset, 2)
                        nc.scalar.copy(hid_hi[:, bass.ds(at, 1), :], tiles(fb[:, j % 2, 0:NT], 1)).then_inc(gate_hi, 1)
                    self.stream(count, kind, drain, dict(hidden=1, gated=1, act_order=1), finish=finish)

            def down(self, kind, count, w, s, gate, norm_next):
                n, e = self.n, self.e

                def finish(j, at):
                    if norm_next and j >= count - WIDE:
                        self.square(s, j - (count - WIDE), True)
                self.stream(count, kind, None, tail=WIDE, finish=finish, early=True)
                n.add("residual", KT)

            def square(self, s, c, updated):
                for k, w in ((2 * c, 2),) if c < WIDE - 1 else ((2 * c, 1), (2 * c + 1, 1)):
                    if updated:
                        self.e.wait_ge(residual_new, self.n("residual", k + w))
                    nc.scalar.activation(wide[:, k:k + w, :], residual[:, k:k + w, s * NT:(s + 1) * NT],
                                         ACT.Square).then_inc(squares, 1)

            def norm(self, s, b, which, summed):
                n, e = self.n, self.e
                if not summed:
                    if n.static("residual"):
                        e.wait_ge(residual_new, n("residual"))
                    for c in range(WIDE):
                        self.square(s, c, False)
                self.catch_up()
                self.var0 += 1
                for k in range(KT):
                    e.wait_ge(modulated, KT * n("norm") + k + 1)
                    o, x = act_hi[:, k, :], wide[:, k, :]
                    if b == 1:
                        ins = nc.scalar.activation(o, x, ACT.Identity, bias=mod[:, 24 * which + k, s:s + 1])
                    else:
                        ins = nc.scalar.copy(o, x)
                    ins.then_inc(norm_hi, 1)
                n.add("norm", 1)
                n.add("pow", 1)

            def turn_out(self, dst, src, scale=None):
                n, e = self.n, self.e
                e.wait_ge(turned, n("turned", 1))
                if scale is None:
                    nc.scalar.copy(dst, src).then_inc(turned_out, 1)
                else:
                    nc.scalar.mul(dst, src, scale).then_inc(turned_out, 1)
                n.add("turned", 1)

            def mix_out(self, b, k):
                nc.scalar.copy(act_hi[:, k:k + 2, :], tiles(b, 2)).then_inc(mix_hi, 1)

            def rows(self, plan, w, l):
                n, e = self.n, self.e
                roped = [c["heads"] for c in plan if "heads" in c]
                proj = proj1 if roped[0]["block"] == 1 else proj2
                base = n.static("head_squares")

                def drain(j, at):
                    c = plan[j]
                    src = tiles(bank[j % 4][:], TT)[:, :, 0:c["wd"]]
                    h = c.get("heads")
                    if h and h["normed"]:
                        m = n.static("head_squares") - base
                        if m >= 2:
                            e.wait_ge(var_ready, self.var0 + m - 1)
                        nc.scalar.activation(tiles(h["sq"][:, m % 2, 0:TT * h["n"] * DH], TT), src[:, :, 0:h["n"] * DH],
                                             ACT.Square).then_inc(head_squares, 1)
                        n.add("head_squares", 1)
                    if "v_kept" in c:
                        nc.scalar.copy(v_rows[:, c["v_kept"]:c["v_kept"] + TT, :], src[:, :, P:2 * P]).then_inc(v_kept, 1)
                        n.add("v_kept", 1)
                    nc.scalar.copy(proj[:, :, c["col"]:c["col"] + c["wd"]], src).then_inc(drained_act, 1)
                    n.add("drained_act", 1)

                def finish(j, at):
                    if j < len(plan) and "gelu" in plan[j]:
                        e.wait_ge(gelu_in, n("gelus", 1))
                        g = gtmp[:, :, 256 * plan[j]["gelu"]:256 * (plan[j]["gelu"] + 1)]
                        nc.scalar.activation(g, g, ACT.Tanh, scale=float(np.sqrt(2 / np.pi))).then_inc(gelu_tanh, 1)
                        n.add("gelus", 1)
                    if 0 <= j - 3 < len(roped):
                        h = roped[j - 3]
                        w_ = h["out"].shape[1]
                        self.turn_out(h["out"], tiles(bank[4 + (j - 3) % 2][:, 0:w_ * NT], w_), h["scale"])
                    if proj is proj2 and INDEX_AT <= j < INDEX_AT + 8:
                        for i in range(2 * (j - INDEX_AT), 2 * (j - INDEX_AT) + 2):
                            wd = (i // IH + 1) * P
                            e.wait_ge(logit_full, n("logits", 1))
                            if i >= 2:
                                e.wait_ge(logit_used, n("logits", -1))
                            nc.scalar.activation(relu_t[:, i % 2, 0:wd], bank[6 + i % 2][:, 0:wd], ACT.Relu).then_inc(logit_relu, 1)
                            n.add("logits", 1)

                self.stream(len(plan), "rows", drain, None, len(plan), finish)
                for j in range(len(plan), len(roped) + 3):
                    finish(j, j)
                self.var0 += sum(h["normed"] for h in roped) + (1 if len(plan) == 6 else 0)

            def attention(self, items, probs, probs_t):
                n, e = self.n, self.e
                s0, i0 = n.static("scores"), n.static("items")
                first = [0]
                for it in items:
                    first.append(first[-1] + len(it["scores"]))

                slots = probs.shape[1]

                def exps(j):
                    if j >= len(items):
                        return
                    for s in range(first[j], first[j + 1]):
                        width = items[j]["keys"] * P
                        e.wait_ge(max_ready, s0 + s + 1)
                        if s >= slots:
                            prev = next(x for x in range(len(items)) if first[x] <= s - slots < first[x + 1])
                            e.wait_ge(prob_turned, i0 + prev + 1)
                        nc.scalar.activation(probs[:, s % slots, 0:width], bank[s % 4][:, 0:width], ACT.Exp,
                                             bias=neg_max[:, s:s + 1], accum_out=total[:, s:s + 1]).then_inc(exped, 1)

                def out_(j):
                    done = items[j]["done"] if j >= 0 else None
                    if done and not isinstance(done[1], tuple):
                        e.wait_ge(mixed, i0 + j + 1)
                        self.mix_out(bank[done[0]][:], done[1])
                exps(0)
                exps(1)
                for j, it in enumerate(items):
                    exps(j + 2)
                    e.wait_ge(prob_turned, i0 + j + 1)
                    if j >= 3:
                        e.wait_ge(mixed, i0 + j - 2)
                    w = it["keys"]
                    nc.scalar.copy(probs_t[:, j % 3, 0:w, :], tiles(bank[4 + j % 2][:, 0:w * P], w)).then_inc(prob_t, 1)
                    out_(j - 2)
                out_(len(items) - 2)
                out_(len(items) - 1)
                n.add("scores", first[-1])
                n.add("items", len(items))

            def attend1(self, s):
                self.attention(items1(s), probs1, probs_t1)
                self.n.add("mix", 2)

            def fourier(self):
                n, e = self.n, self.e
                for i in range(2):
                    e.wait_ge(dft_full, 2 * n("fourier") + i + 1)
                    nc.scalar.copy(four[:, i, :], bank[i][:]).then_inc(dft_out, 1)
                e.wait_ge(mix_full, 2 * n("fourier") + 1)
                self.mix_out(bank[2][:], 4)
                n.add("fourier", 1)
                n.add("mix", 1)

            def spatial_gate(self):
                n, e = self.n, self.e
                self.turn_out(w_sp_t[:], tiles(bank[3][:], 4))
                e.wait_ge(mix_full, 2 * n("gmlp") + 2)
                self.mix_out(bank[5][:], 6)
                n.add("gmlp", 1)
                n.add("mix", 1)

            def attend2(self, l):
                n, e = self.n, self.e
                self.attention(items2(), probs2, probs_t2)
                for t in range(TT):
                    e.wait_ge(mix_full, 2 * n("gmlp") + 2 * l + t + 1)
                    self.mix_out(bank[4 + t][:], 2 + 2 * t)
                self.var0 += TT
                n.add("mix", 4)

            def params2(self, l):
                super().params2(l)
                self.e.wait_ge(lam_sums, l + 1)
                nc.scalar.activation(lam[:, 2:4], lam[:, 0:2], ACT.Exp).then_inc(lam_exp, 1)

            def finish(self):
                n, e = self.n, self.e
                for i in range(2):
                    for t in range(TT):
                        e.wait_ge(turned, n("turned", 1))
                        for q in range(2):
                            nc.scalar.copy(rows_in[:, t, i * 512 + q * 256:i * 512 + (q + 1) * 256],
                                           bank[i + 2 * t][:, q * 256:(q + 1) * 256]).then_inc(final_rows, 1)
                        n.add("turned", 1)

        class Vector(Phases):
            def order(self, ins):
                ins.then_inc(dve_order, 1)
                self.n.add("dve_order", 1)
                self.e.wait_ge(dve_order, self.n("dve_order"))

            def split(self, k, halves=(0, 1)):
                n, e = self.n, self.e
                c = n.static("chunks") + k
                for h in halves:
                    e.wait_ge(hi_ready, n("halves", 2 * k + h + 1))
                    slot = (2 * c + h) % SPLIT
                    nc.vector.tensor_tensor(w_lo[:, slot, :], raw[:, c % RAW, h * 1024:(h + 1) * 1024],
                                            w_hi[:, slot, :].bitcast(F32), ALU.subtract).then_inc(lo_ready, 1)

            def stream(self, count, drain, extra=None, tail=0, finish=None, early=False):
                n = self.n
                self.catch_up()

                def body(j, at):
                    if drain:
                        drain(j, at)
                    if n.static("chunks") + 2 < TOTAL[0]:
                        if j < count - 1:
                            self.split(2)
                        elif early:
                            self.split(2, (0,))
                    if finish:
                        finish(j, at)
                    n.add("chunks", 1)
                    n.add("halves", 2)

                run_chunks(self.e, n, count, dict(chunks=1, halves=2, **(extra or {})), body, max(tail, 1))
                self.behind = ((1,) if early else (0, 1)) if n.static("chunks") + 1 < TOTAL[0] else ()

            def catch_up(self):
                if self.behind:
                    self.split(1, self.behind)
                    self.behind = ()

            def load(self):
                n, e = self.n, self.e
                for k in range(KT):
                    e.wait_ge(turned, k + 1)
                    nc.vector.tensor_copy(residual[:, k, :], bank[k][:]).then_inc(turned_out, 1)
                n.add("turned", 8)
                nc.vector.tensor_copy(ident_b[:], ident)
                nc.vector.tensor_copy(mask_b[:], causal(0))
                self.order(nc.vector.memset(cond[:].bitcast(mybir.dt.uint32), 0))
                e.wait_ge(cond_exp, 1)
                self.order(nc.vector.tensor_scalar(cond_raw[:, 1], cond_raw[:, 1], 1.0, None, ALU.add))
                self.order(nc.vector.reciprocal(cond_raw[:, 1], cond_raw[:, 1]))
                e.wait_ge(cond_in, 32)
                self.order(nc.vector.tensor_tensor(cond_raw[:, 2], cond_raw[:, 0], cond_raw[:, 1], ALU.mult))
                self.order(nc.vector.tensor_copy(cond[:, :, 0:2], cond_raw[:, 2]))
                nc.vector.tensor_tensor(cond[:, :, 2:4], cond_raw[:, 2], cond[:, :, 0:2].bitcast(F32),
                                        ALU.subtract).then_inc(cond_ready, 1)
                self.split(0)
                self.split(1)

            def ada(self, l):
                self.stream(24, None)
                self.n.add("drained_act", 24)

            def modulation(self, l):
                n, e = self.n, self.e
                e.wait_ge(mod_full, l + 1)
                self.order(nc.vector.tensor_copy(mod[:], bank[4][:, 0:96].rearrange("p (j s) -> p j s", s=2)))
                e.wait_ge(params_in, params_until("params", l))
                for i in range(2):
                    sc = mod[:, 8 + 24 * i:16 + 24 * i, :]
                    self.order(nc.vector.tensor_scalar(mscale[:, i], sc, 1.0, None, ALU.add))
                    self.order(nc.vector.tensor_tensor(mscale[:, i], mscale[:, i],
                                                       norm_g[:, i, :].unsqueeze(2).broadcast_to([P, KT, 2]), ALU.mult))
                n.add("mod", 1)

            def up(self, kind, count, w):
                n, e = self.n, self.e
                if kind == "relu2":
                    def drain(j, at):
                        e.wait_ge(drained_act, n("drained_act", 1))
                        self.order(nc.vector.tensor_tensor(fb[:, j % 2, :], fa[:, j % 2, :], fa[:, j % 2, :], ALU.mult))

                    def finish(j, at):
                        n.add("drained_act", 1)
                        n.add("hidden", 1)
                        e.wait_ge(squared, n("squared", 1))
                        n.add("squared", 1)
                        nc.vector.tensor_tensor(hid_lo[:, bass.ds(at * 2, 2), :], tiles(fb[:, j % 2, :], 2),
                                                hid_hi[:, bass.ds(at * 2, 2), :].bitcast(F32), ALU.subtract).then_inc(hidden, 1)
                    self.stream(count, drain, dict(drained_act=1, hidden=1, squared=1, dve_order=1), finish=finish)
                else:
                    def drain(j, at):
                        ex, b, f = fa[:, j % 2, 0:NT], bank[j % 4], fb[:, j % 2, 0:NT]
                        e.wait_ge(gate_exp, n("silus", 1))
                        self.order(nc.vector.reciprocal(ex, ex))
                        self.order(nc.vector.tensor_tensor(ex, b[:, 0:NT], ex, ALU.mult))
                        nc.vector.tensor_tensor(f, b[:, NT:2 * NT], ex, ALU.mult).then_inc(gated, 1)

                    def finish(j, at):
                        f = fb[:, j % 2, 0:NT]
                        n.add("silus", 1)
                        n.add("hidden", 1)
                        n.add("gated", 1)
                        e.wait_ge(gate_hi, n("silus"))
                        nc.vector.tensor_tensor(hid_lo[:, bass.ds(at, 1), :], tiles(f, 1),
                                                hid_hi[:, bass.ds(at, 1), :].bitcast(F32), ALU.subtract).then_inc(hidden, 1)
                    self.stream(count, drain, dict(silus=1, hidden=1, gated=1, dve_order=2), finish=finish)

            def down(self, kind, count, w, s, gate, norm_next):
                n, e = self.n, self.e

                def finish(j, at):
                    c = j - (count - WIDE)
                    if c < 0:
                        return
                    e.wait_ge(multiplied, n("halves", 2))
                    for d in (2 * c, 2 * c + 1):
                        x = residual[:, d, s * NT:(s + 1) * NT]
                        src = tiles(bank[4 + c][:], 2)[:, d % 2, :]
                        if gate is None:
                            nc.vector.tensor_tensor(x, src, x, ALU.add).then_inc(residual_new, 1)
                        else:
                            nc.vector.scalar_tensor_tensor(x, src, mod[:, gate + d, s:s + 1], x, ALU.mult, ALU.add).then_inc(residual_new, 1)
                self.stream(count, None, None, WIDE, finish, True)
                n.add("residual", KT)

            def norm(self, s, b, which, summed):
                n, e = self.n, self.e
                self.catch_up()
                e.wait_ge(sums, n("norm", 1))
                nc.vector.tensor_scalar(variance[:, 0:TT], bank[0][:, 0:TT], 1.0 / D, EPS, ALU.mult, ALU.add).then_inc(var_ready, 1)
                n.add("pow", 1)
                e.wait_ge(rstd_ready, n("pow"))
                for t in range(TT):
                    ins = nc.vector.tensor_scalar(diag[:, t, :], ident, rstd[:, t:t + 1], None, ALU.mult)
                ins.then_inc(rstd_diag, 1)
                e.wait_ge(rstd_wide, n("norm", 1))

                def low(k):
                    e.wait_ge(norm_hi, KT * n("norm") + k + 1)
                    o, x, hi = act_lo[:, k, :], wide[:, k, :], act_hi[:, k, :].bitcast(F32)
                    if b == 1:
                        ins = nc.vector.scalar_tensor_tensor(o, x, mod[:, 24 * which + k, s:s + 1], hi, ALU.add, ALU.subtract)
                    else:
                        ins = nc.vector.tensor_tensor(o, x, hi, ALU.subtract)
                    ins.then_inc(norm_lo, 1)
                for k in range(KT):
                    scale = mscale[:, which, k, s:s + 1] if b == 1 else norm2_g[:, which, k:k + 1]
                    nc.vector.scalar_tensor_tensor(wide[:, k, :], residual[:, k, s * NT:(s + 1) * NT], scale, bank[1][:, 0:NT],
                                                   ALU.mult, ALU.mult).then_inc(modulated, 1)
                    if k:
                        low(k - 1)
                low(KT - 1)
                n.add("norm", 1)

            def mix_out(self, b, k):
                n, e = self.n, self.e
                n.add("mix", 1)
                e.wait_ge(mix_hi, n("mix"))
                nc.vector.tensor_tensor(act_lo[:, k:k + 2, :], tiles(b, 2), act_hi[:, k:k + 2, :].bitcast(F32),
                                        ALU.subtract).then_inc(mix_lo, 1)

            def power(self):
                self.n.add("pow", 1)
                self.e.wait_ge(rstd_ready, self.n("pow"))

            def tables(self, b, cos_g, sin_g, gain):
                kinds = gain.shape[1]
                cos, sin = rope[b]
                nc.vector.tensor_tensor(cos_g[:], cos.unsqueeze(1).broadcast_to([P, kinds, TT, DH]),
                                        gain.unsqueeze(2).broadcast_to([P, kinds, TT, DH]), ALU.mult)
                axes = 2 if b == 1 else 1
                w = DH // axes // 2
                for a in range(axes):
                    for half in range(2):
                        lo, other = (2 * a + half) * w, (2 * a + 1 - half) * w
                        ins = nc.vector.tensor_tensor(
                            sin_g[:, :, :, lo:lo + w], sin[:, :, lo:lo + w].unsqueeze(1).broadcast_to([P, kinds, TT, w]),
                            gain[:, :, other:other + w].unsqueeze(2).broadcast_to([P, kinds, TT, w]), ALU.mult)
                ins.then_inc(tables_ready, 1)

            def rows(self, plan, w, l):
                n, e = self.n, self.e
                roped = [c["heads"] for c in plan if "heads" in c]
                block2 = roped[0]["block"] == 2
                k0 = n.static("drained_act")
                m0 = n.static("head_squares")
                if block2:
                    self.tables(2, cos_g2, sin_g2, gains2[:].rearrange("p i k d -> p (i k) d"))
                else:
                    self.tables(1, cos_g1, sin_g1, tiles(gains1[:, 0:2 * DH], 2))
                n.add("tables", 1)
                e.wait_ge(tables_ready, n("tables"))
                sines = {}
                norms = []

                def scratch_of(h, name, r):
                    return heads_of(tiles(h[name][:, r % 2, 0:TT * h["n"] * DH], TT))

                def first_half(j):
                    h, m = roped[j], n.static("head_squares") - m0
                    heads = h["n"]
                    if h["normed"]:
                        at = 16 * (m % 2)
                        e.wait_ge(head_squares, n("head_squares", 1))
                        v = variance[:, at:at + TT * heads]
                        self.order(nc.vector.tensor_reduce(v.rearrange("p (t h) -> p t h", t=TT), scratch_of(h, "sq", m), AX.X, ALU.add))
                        nc.vector.tensor_scalar(v, v, 1.0 / DH, EPS, ALU.mult, ALU.add).then_inc(var_ready, 1)
                        n.add("head_squares", 1)
                        n.add("pow", 1)
                        norms.append((at, n.static("pow")))
                    else:
                        norms.append(None)
                    e.wait_ge(drained_act, k0 + j + 1)
                    if h["sin"] is None:
                        return
                    if j >= 2:
                        e.wait_ge(rows_ready, n("rows", j - 1))
                    x, t2, sin, wd = h["x"], scratch_of(h, "b", j), h["sin"], DH // h["axes"] // 2
                    if h["axes"] == 1:
                        for half in range(2):
                            lo, other = half * wd, (1 - half) * wd
                            ins = nc.vector.tensor_tensor(t2[:, :, :, lo:lo + wd], x[:, :, :, other:other + wd],
                                                          sin[:, :, lo:lo + wd].unsqueeze(2).broadcast_to([P, TT, heads, wd]), ALU.mult)
                    else:
                        for t in range(TT):
                            xv, tv = (v[:, t].rearrange("p h (a b w) -> p h a b w", b=2, w=wd) for v in (x, t2))
                            sv = sin[:, t].rearrange("p (a b w) -> p a b w", b=2, w=wd)
                            for half in range(2):
                                ins = nc.vector.tensor_tensor(tv[:, :, :, half], xv[:, :, :, 1 - half],
                                                              sv[:, :, half].unsqueeze(1).broadcast_to([P, heads, 2, wd]), ALU.mult)
                    ins.then_inc(dve_order, 1)
                    n.add("dve_order", 1)
                    sines[j] = n.static("dve_order")

                def second_half(r):
                    h, t1, t2 = roped[r], scratch_of(roped[r], "a", r), scratch_of(roped[r], "b", r)
                    e.wait_ge(rope_cos, n("rope", 1))
                    n.add("rope", 1)
                    if h["sin"] is not None:
                        e.wait_ge(dve_order, sines[r])
                    if h["sin"] is not None and norms[r]:
                        self.order(nc.vector.tensor_tensor(t1, t1, t2, ALU.add))
                    if norms[r]:
                        at, value = norms[r]
                        e.wait_ge(rstd_ready, value)
                        f = rstd[:, at:at + TT * h["n"]].rearrange("p (t h) -> p t h", t=TT).unsqueeze(3).broadcast_to([P, TT, h["n"], DH])
                    for d in h["dst"]:
                        ins = nc.vector.tensor_tensor(d, t1, f, ALU.mult) if norms[r] else nc.vector.tensor_tensor(d, t1, t2, ALU.add)
                    ins.then_inc(rows_ready, 1)

                def gelu_a(c, j):
                    g = c["gelu"]
                    x = proj1[:, :, U1 + 256 * g:U1 + 256 * (g + 1)]
                    t = gtmp[:, :, 256 * g:256 * (g + 1)]
                    e.wait_ge(drained_act, k0 + j + 1)
                    self.order(nc.vector.tensor_tensor(t, x, x, ALU.mult))
                    self.order(nc.vector.tensor_scalar(t, t, 0.044715, 1.0, ALU.mult, ALU.add))
                    nc.vector.tensor_tensor(t, t, x, ALU.mult).then_inc(gelu_in, 1)

                def gelu_b(c):
                    g = c["gelu"]
                    t = gtmp[:, :, 256 * g:256 * (g + 1)]
                    n.add("gelus", 1)
                    e.wait_ge(gelu_tanh, n("gelus"))
                    self.order(nc.vector.tensor_scalar(t, t, 1.0, 0.5, ALU.add, ALU.mult))
                    o = gates[:, :, 256 * g:256 * (g + 1)]
                    self.order(nc.vector.tensor_tensor(o, t, proj1[:, :, U1 + 256 * g:U1 + 256 * (g + 1)], ALU.mult))
                    if g:
                        self.order(nc.vector.tensor_tensor(t, o, o, ALU.mult))
                        v = variance[:, 32:32 + 4 * TT]
                        self.order(nc.vector.tensor_reduce(v.rearrange("p (t h) -> p t h", t=TT), heads_of(t), AX.X, ALU.add))
                        nc.vector.tensor_scalar(v, v, 1.0 / DH, EPS, ALU.mult, ALU.add).then_inc(var_ready, 1)

                def gelu_c():
                    self.power()
                    gv = gates[:, :, 256:512]
                    f = rstd[:, 32:32 + 4 * TT].rearrange("p (t h) -> p t h", t=TT).unsqueeze(3).broadcast_to([P, TT, 4, DH])
                    self.order(nc.vector.tensor_tensor(heads_of(gv), heads_of(gv), f, ALU.mult))
                    nc.vector.tensor_tensor(gv, gv, gains1[:, 2 * DH:].unsqueeze(1).broadcast_to([P, TT, 256]),
                                            ALU.mult).then_inc(gates_ready, 1)

                def drain(j, at):
                    if j < len(roped):
                        first_half(j)
                    if "gelu" in plan[j]:
                        gelu_a(plan[j], j)

                def finish(j, at):
                    if 0 <= j - 1 < len(roped):
                        second_half(j - 1)
                    if 0 < j <= len(plan) and "gelu" in plan[j - 1]:
                        gelu_b(plan[j - 1])
                    if len(plan) == 6 and j == 5:
                        gelu_c()
                    if not block2:
                        return
                    if j == 3:
                        self.order(nc.vector.tensor_scalar(proj2[:, :, IW:IW + IH], proj2[:, :, IW:IW + IH],
                                                           float(np.float32(IH ** -0.5)), None, ALU.mult))
                    if INDEX_AT <= j < INDEX_AT + 8:
                        for i in range(2 * (j - INDEX_AT), 2 * (j - INDEX_AT) + 2):
                            self.index_score(i)
                    if j >= SEARCH_AT:
                        for _ in range(2):
                            self.search(0)

                self.round = [0, 0]
                self.stream(len(plan), drain, None, len(plan), finish)
                for j in range(len(plan), len(roped) + 1):
                    finish(j, j)
                n.add("rows", len(roped))
                n.add("drained_act", len(plan))

            def index_score(self, i):
                n, e = self.n, self.e
                t, h = divmod(i, IH)
                wd = (t + 1) * P
                n.add("logits", 1)
                e.wait_ge(logit_relu, n("logits"))
                wt, sc = proj2[:, t, IW + h:IW + h + 1], score[:, t, 0:wd]
                if h == 0:
                    ins = nc.vector.tensor_scalar(sc, relu_t[:, i % 2, 0:wd], wt, None, ALU.mult)
                else:
                    ins = nc.vector.scalar_tensor_tensor(sc, relu_t[:, i % 2, 0:wd], wt, sc, ALU.mult, ALU.add)
                ins.then_inc(logit_used, 1)
                e.wait_ge(logit_used, n("logits"))
                if h == IH - 1:
                    self.order(nc.vector.tensor_tensor(sc, sc, causal(t), ALU.add))

            def search(self, t):
                sc = score[:, t, 0:(t + 1) * P]
                self.order(nc.vector.max(best[:], sc))
                self.order(nc.vector.match_replace(sc, best[:], sc, TAKEN))
                self.round[t] += 1
                if self.round[t] == TOPK // 8:
                    self.order(nc.vector.tensor_scalar(sc, sc, TAKEN / 2, MASKED, ALU.is_gt, ALU.mult))
                    nc.vector.tensor_tensor(seen[:, t, 0:(t + 1) * P], sc, causal(t), ALU.add).then_inc(seen_ready, 1)

            def attention(self, items, probs, beside=None):
                n, e = self.n, self.e
                s0, i0 = n.static("scores"), n.static("items")
                first = [0]
                for it in items:
                    first.append(first[-1] + len(it["scores"]))

                slots = probs.shape[1]

                def maxima(j):
                    if j >= len(items):
                        return
                    for s in range(first[j], first[j + 1]):
                        width = items[j]["keys"] * P
                        e.wait_ge(scored, s0 + s + 1)
                        nc.vector.tensor_reduce(neg_max[:, s:s + 1], bank[s % 4][:, 0:width], AX.X, ALU.max,
                                                negate=True).then_inc(max_ready, 1)

                def out_(j):
                    done = items[j]["done"] if j >= 0 else None
                    if done and isinstance(done[1], tuple):
                        e.wait_ge(mixed, i0 + j + 1)
                        nc.vector.tensor_copy(diff_rows[:, done[1][1], :], bank[done[0]][:]).then_inc(diff_drained, 1)
                    elif done:
                        self.mix_out(bank[done[0]][:], done[1])
                maxima(0)
                maxima(1)
                for j, it in enumerate(items):
                    s = first[j]
                    width = it["keys"] * P
                    a, b = probs[:, s % slots, 0:width], probs[:, (s + 1) % slots, 0:width]
                    e.wait_ge(exped, s0 + first[j + 1])
                    if it.get("diff"):
                        self.order(nc.vector.reciprocal(total[:, s:s + 2], total[:, s:s + 2]))
                        self.order(nc.vector.tensor_tensor(total[:, s + 1:s + 2], total[:, s + 1:s + 2], lam[:, 4:5], ALU.mult))
                        self.order(nc.vector.tensor_scalar(b, b, total[:, s + 1:s + 2], None, ALU.mult))
                        nc.vector.scalar_tensor_tensor(a, a, total[:, s:s + 1], b, ALU.mult, ALU.subtract).then_inc(prob_ready, 1)
                    else:
                        self.order(nc.vector.reciprocal(total[:, s:s + 1], total[:, s:s + 1]))
                        nc.vector.tensor_scalar(a, a, total[:, s:s + 1], None, ALU.mult).then_inc(prob_ready, 1)
                    maxima(j + 2)
                    if beside:
                        beside(j)
                    out_(j - 2)
                out_(len(items) - 2)
                out_(len(items) - 1)
                n.add("scores", first[-1])
                n.add("items", len(items))

            def attend1(self, s):
                self.attention(items1(s), probs1)

            def fourier(self):
                self.mix_out(bank[2][:], 4)
                self.n.add("fourier", 1)

            def spatial_gate(self):
                n, e = self.n, self.e
                e.wait_ge(spatial, n("gmlp", 1))
                for h in range(4):
                    u = gates[:, :, h * DH:(h + 1) * DH]
                    ins = nc.vector.scalar_tensor_tensor(u, tiles(bank[4][:, h * P:(h + 1) * P], TT), b_sp[:, h:h + 1], u,
                                                         ALU.add, ALU.mult)
                ins.then_inc(gates_ready, 1)
                self.mix_out(bank[5][:], 6)
                n.add("gmlp", 1)
                n.add("turned", 1)

            def params2(self, l):
                super().params2(l)
                n, e = self.n, self.e
                self.layer2 = l
                e.wait_ge(params2_in, 96 * (l + 1))
                lv = lam_in[:].rearrange("p (a b d) -> p a b d", a=2, b=2)
                self.order(nc.vector.tensor_tensor(lv[:, :, 0, :], lv[:, :, 0, :], lv[:, :, 1, :], ALU.mult))
                nc.vector.tensor_reduce(lam[:, 0:2], lv[:, :, 0, :], AX.X, ALU.add).then_inc(lam_sums, 1)
                e.wait_ge(lam_exp, l + 1)
                init = 0.8 - 0.6 * float(np.exp(-0.3 * l))
                self.order(nc.vector.tensor_tensor(lam[:, 4:5], lam[:, 2:3], lam[:, 3:4], ALU.subtract))
                self.order(nc.vector.tensor_scalar(lam[:, 4:5], lam[:, 4:5], init, None, ALU.add))
                self.order(nc.vector.tensor_scalar(sub_g[:], sub_g[:], 1.0 - init, None, ALU.mult))

            def attend2(self, l):
                n, e = self.n, self.e

                def norm_rows(t, part):
                    x = tiles(diff_rows[:, t, :], 4)
                    v = variance[:, 8 * t:8 * t + 4]
                    if part == 0:
                        e.wait_ge(diff_drained, TT * l + t + 1)
                        self.order(nc.vector.tensor_tensor(tiles(diff_sq[:], 4), x, x, ALU.mult))
                        self.order(nc.vector.tensor_reduce(v, tiles(diff_sq[:], 4), AX.X, ALU.add))
                        nc.vector.tensor_scalar(v, v, 1.0 / (2 * DH), EPS, ALU.mult, ALU.add).then_inc(var_ready, 1)
                        return
                    self.power()
                    self.order(nc.vector.tensor_tensor(x, x, rstd[:, 8 * t:8 * t + 4].unsqueeze(2).broadcast_to([P, 4, P]), ALU.mult))
                    nc.vector.tensor_tensor(x, x, sub_g[:].unsqueeze(1).broadcast_to([P, 4, P]), ALU.mult).then_inc(rows_ready, 1)

                def beside(j):
                    if j < TOPK // 8:
                        self.search(1)
                    for k, (t, part) in {18: (0, 0), 19: (0, 1), 20: (1, 0), 21: (1, 1)}.items():
                        if j == k:
                            norm_rows(t, part)
                self.attention(items2(), probs2, beside)
                n.add("rows", TT)
                for t in range(TT):
                    self.mix_out(bank[4 + t][:], 2 + 2 * t)

        class Tensor(Phases):
            def three(self, o, w, x, first):
                for i, (a, b) in enumerate(((0, 0), (0, 1), (1, 0))):
                    ins = nc.tensor.matmul(o, w[a], x[b], start=first and i == 0, stop=True, skip_group_check=True)
                return ins

            def stream(self, count, multiply, free=None, extra=None, tail=0, after=None):
                n, e = self.n, self.e

                def body(j, at):
                    if free is not None and (j >= 4 or n.it is not None):
                        e.wait_ge(free[0], n(free[1], -3))
                    for h in range(2):
                        e.wait_ge(lo_ready, n("halves", h + 1))
                        slot = (2 * n.static("chunks") + h) % SPLIT
                        multiply(j, at, h, w_hi[:, slot, :], w_lo[:, slot, :]).then_inc(multiplied, 1)
                    n.add("chunks", 1)
                    n.add("halves", 2)
                    if free is not None:
                        n.add(free[1], 1)
                    if after:
                        after(j)

                per = dict(chunks=1, halves=2)
                if free is not None:
                    per[free[1]] = 1
                run_chunks(e, n, count, per, body, tail, 4 if free is not None else 1)

            def load(self):
                n, e = self.n, self.e
                e.wait_ge(inputs_in, 32)
                e.wait_ge(consts_in, 16)
                e.wait_ge(preset, 2)
                for k in range(KT):
                    for t in range(2 * TT):
                        ins = nc.tensor.transpose(bank[k][:, t * P:(t + 1) * P], rows_in[:, t, k * P:(k + 1) * P], ident)
                    ins.then_inc(turned, 1)
                n.add("turned", 8)
                e.wait_ge(turned_out, 8)
                e.wait_ge(cond_ready, 1)

            def ada(self, l):
                def multiply(j, at, h, hi, lo):
                    for k in range(4):
                        for i, w in enumerate((hi, lo)):
                            ins = nc.tensor.matmul(bank[j % 4][:, 0:CW], cond[:, 4 * h + k, :], tiles(w, 4)[:, k, :],
                                                   start=h == 0 and k == 0 and i == 0, stop=True, skip_group_check=True)
                    return ins
                self.stream(24, multiply, (drained_act, "drained_act"))

            def modulation(self, l):
                n, e = self.n, self.e
                e.wait_ge(drained_act, n("drained_act"))
                e.wait_ge(params_in, params_until("bias", l))
                for j in range(48):
                    ins = nc.tensor.matmul(bank[4][:, 2 * j:2 * j + 2], mod_rows[0:5, j * P:(j + 1) * P], sel[0:5, :],
                                           start=True, stop=True)
                ins.then_inc(mod_full, 1)
                n.add("mod", 1)

            def up(self, kind, count, w):
                n, e = self.n, self.e

                def multiply(j, at, h, hi, lo):
                    for k in range(4):
                        if j == 0:
                            e.wait_ge(norm_lo, KT * (n("norm") - 1) + 4 * h + k + 1)
                        x = [a[:, 4 * h + k, :] for a in (act_hi, act_lo)]
                        for t in range(2):
                            ins = self.three(tiles(bank[j % 4][:], 2)[:, t, :], [tiles(v, 4)[:, k, t * P:(t + 1) * P] for v in (hi, lo)],
                                             x, h == 0 and k == 0 and t == 0)
                    return ins
                self.stream(count, multiply, (drained_act, "drained_act") if kind == "relu2" else (gated, "gated"))
                n.add("hidden", count)

            def down(self, kind, count, w, s, gate, norm_next):
                n, e = self.n, self.e
                src = (act_hi, act_lo) if kind == "mix" else (hid_hi, hid_lo)

                def multiply(j, at, h, hi, lo):
                    if j == 0 and kind == "mix":
                        e.wait_ge(mix_lo, n("mix", h - 1))
                    elif j == 0 and h == 0:
                        e.wait_ge(hidden, n("hidden"))
                    c = j - (count - WIDE)
                    if c < 0:
                        x = [a[:, bass.ds(at * 2 + h, 1), :] for a in src]
                        for d in range(KT):
                            ins = self.three(tiles(bank[4 + d // 2][:], 2)[:, d % 2:d % 2 + 1, :], [v[:, d * P:(d + 1) * P] for v in (hi, lo)],
                                             x, j == 0 and h == 0 and d % 2 == 0)
                        return ins
                    for k in range(4):
                        x = [a[:, 2 * count - KT + 4 * h + k, :] for a in src]
                        for t in range(2):
                            ins = self.three(tiles(bank[4 + c][:], 2)[:, t, :], [tiles(v, 4)[:, k, t * P:(t + 1) * P] for v in (hi, lo)],
                                             x, count == WIDE and h == 0 and k == 0 and t == 0)
                    return ins
                self.stream(count, multiply, tail=WIDE)
                n.add("residual", KT)

            def norm(self, s, b, which, summed):
                n, e = self.n, self.e
                for i, k in enumerate((0, KT - 2, KT - 1)):
                    if i == 0:
                        e.wait_ge(folded, 3 * (n("norm") + 1))
                    else:
                        e.wait_ge(squares, 5 * n("norm") + 3 + i)
                    for t in range(TT):
                        ins = nc.tensor.matmul(bank[0][:, t:t + 1], wide[:, k, t * P:(t + 1) * P], ones[:, 0:1],
                                               start=i == 0 and t == 0, stop=True, skip_group_check=True)
                ins.then_inc(sums, 1)
                e.wait_ge(rstd_diag, n("norm", 1))
                nc.tensor.matmul(bank[1][:, 0:NT], ones[:], diag[:].rearrange("p t n -> p (t n)"), start=True, stop=True).then_inc(rstd_wide, 1)
                n.add("norm", 1)
                n.add("pow", 1)

            def turn(self, b, srcs, wait=True):
                n, e = self.n, self.e
                if wait:
                    e.wait_ge(turned_out, n("turned", -1))
                for i, x in enumerate(srcs):
                    ins = nc.tensor.transpose(b[:, i * P:(i + 1) * P], x, ident)
                ins.then_inc(turned, 1)
                n.add("turned", 1)

            def rows(self, plan, w, l):
                n, e = self.n, self.e
                roped = [c["heads"] for c in plan if "heads" in c]

                def multiply(j, at, h, hi, lo):
                    wd = plan[j]["wd"]
                    for k in range(4):
                        if j == 0:
                            e.wait_ge(norm_lo, KT * (n("norm") - 1) + 4 * h + k + 1)
                        for t in range(TT):
                            x = [a[:, 4 * h + k, t * P:(t + 1) * P] for a in (act_hi, act_lo)]
                            ins = self.three(tiles(bank[j % 4][:], TT)[:, t, 0:wd], x,
                                             [tiles(v, 4)[:, k, 0:wd] for v in (hi, lo)], h == 0 and k == 0 and t == 0)
                    return ins

                def after(j):
                    if 0 <= j - 2 < len(roped):
                        e.wait_ge(rows_ready, n("rows", 1))
                        n.add("rows", 1)
                        self.turn(bank[4 + (j - 2) % 2], roped[j - 2]["turn"])
                    if roped[0]["block"] == 2 and INDEX_AT <= j < INDEX_AT + 8:
                        for i in range(2 * (j - INDEX_AT), 2 * (j - INDEX_AT) + 2):
                            t, h = divmod(i, IH)
                            wd = (t + 1) * P
                            if i == 0:
                                e.wait_ge(turned_out, n("turned") - (j - 1) + 3)
                            if i >= 2:
                                e.wait_ge(logit_relu, n("logits", -1))
                            nc.tensor.matmul(bank[6 + i % 2][:, 0:wd], pair("iq", h, t * P, wd),
                                             pairs_t[DH * (h % 2):DH * (h % 2) + DH, PAIR["ik"], 0:wd], start=True, stop=True).then_inc(logit_full, 1)
                            n.add("logits", 1)

                self.stream(len(plan), multiply, (drained_act, "drained_act"), tail=len(plan), after=after)
                for j in range(len(plan), len(roped) + 2):
                    after(j)

            def attention(self, items, probs, probs_t):
                n, e = self.n, self.e
                s0, i0 = n.static("scores"), n.static("items")
                first = [0]
                for it in items:
                    first.append(first[-1] + len(it["scores"]))

                slots = probs.shape[1]

                def score_(j):
                    if j >= len(items):
                        return
                    for i, (q, k, m) in enumerate(items[j]["scores"]):
                        s = first[j] + i
                        width = items[j]["keys"] * P
                        if s >= 4:
                            e.wait_ge(exped, s0 + s - 3)
                        if j == 16 + i and len(items) > 16:
                            e.wait_ge(seen_ready, TT * (n("index") + 1))
                        o = bank[s % 4][:, 0:width]
                        ins = nc.tensor.matmul(o, q, k, start=True, stop=m is None)
                        if m is not None:
                            ins = nc.tensor.matmul(bank[s % 4][:, width - m.shape[-1]:width], ident_b[:], m, start=False, stop=True)
                        ins.then_inc(scored, 1)

                def values(j):
                    if j < 0:
                        return
                    it = items[j]
                    e.wait_ge(prob_t, i0 + j + 1)
                    if len(items) > 16 and j == 12:
                        e.wait_ge(mix_lo, n("mix", 1))
                    if len(items) > 16 and j == 16:
                        e.wait_ge(diff_drained, TT * n("index") + 1)
                    for k, v in enumerate(it["v"]):
                        pt = probs_t[:, j % 3, k, :]
                        a, b = (pt, v) if it.get("diff") else (v, pt)
                        ins = nc.tensor.matmul(it["o"], a, b, start=k == 0, stop=k == it["keys"] - 1)
                    ins.then_inc(mixed, 1)
                score_(0)
                score_(1)
                for j, it in enumerate(items):
                    score_(j + 2)
                    values(j - 2)
                    e.wait_ge(prob_ready, i0 + j + 1)
                    if j >= 2:
                        e.wait_ge(prob_t, i0 + j - 1)
                    s = first[j]
                    for k in range(it["keys"]):
                        ins = nc.tensor.transpose(bank[4 + j % 2][:, k * P:(k + 1) * P], probs[:, s % slots, k * P:(k + 1) * P], ident)
                    ins.then_inc(prob_turned, 1)
                values(len(items) - 2)
                values(len(items) - 1)
                n.add("scores", first[-1])
                n.add("items", len(items))

            def attend1(self, s):
                self.e.wait_ge(turned_out, self.n("turned"))
                self.e.wait_ge(v_kept, self.n("heads", 1))
                self.n.add("heads", 1)
                self.attention(items1(s), probs1, probs_t1)
                self.n.add("mix", 2)

            def fourier(self):
                n, e = self.n, self.e
                e.wait_ge(exped, n("scores"))
                for i in range(2):
                    for t in range(TT):
                        ins = nc.tensor.matmul(bank[i][:], proj1[:, t, F1 + i * P:F1 + (i + 1) * P], dft_n[:, t, :],
                                               start=t == 0, stop=t == TT - 1)
                    ins.then_inc(dft_full, 1)
                for i in range(2):
                    e.wait_ge(dft_out, 2 * n("fourier") + i + 1)
                    o = bank[2][:, i * NT:(i + 1) * NT]
                    nc.tensor.matmul(o, cols["dft_c"], four[:, i, 0:NT], start=True, stop=False)
                    ins = nc.tensor.matmul(o, cols["dft_s"], four[:, i, NT:2 * NT], start=False, stop=True)
                ins.then_inc(mix_full, 1)
                n.add("fourier", 1)
                n.add("mix", 1)

            def spatial_gate(self):
                n, e = self.n, self.e
                self.turn(bank[3], [w_sp[:, h, :] for h in range(4)])
                e.wait_ge(turned_out, n("turned"))
                e.wait_ge(gates_ready, 2 * n("gmlp") + 1)
                e.wait_ge(prob_t, n("items"))
                for h in range(4):
                    ins = nc.tensor.matmul(bank[4][:, h * P:(h + 1) * P], w_sp_t[:, h, :],
                                           gates[:, :, 256 + h * DH:256 + (h + 1) * DH], start=True, stop=True)
                ins.then_inc(spatial, 1)
                e.wait_ge(gates_ready, 2 * n("gmlp") + 2)
                e.wait_ge(prob_t, n("items"))
                for i in range(2):
                    for t in range(TT):
                        ins = nc.tensor.transpose(bank[5][:, (2 * i + t) * P:(2 * i + t + 1) * P], gates[:, t, i * P:(i + 1) * P], ident)
                ins.then_inc(mix_full, 1)
                n.add("gmlp", 1)
                n.add("mix", 1)

            def attend2(self, l):
                n, e = self.n, self.e
                e.wait_ge(turned_out, n("turned"))
                e.wait_ge(drained_act, n("drained_act"))
                self.attention(items2(), probs2, probs_t2)
                n.add("index", 1)
                e.wait_ge(prob_t, n("items"))
                for t in range(TT):
                    e.wait_ge(rows_ready, n("rows", TT))
                    for j in range(2):
                        for q in range(TT):
                            h = 2 * t + j
                            ins = nc.tensor.transpose(bank[4 + t][:, (2 * j + q) * P:(2 * j + q + 1) * P],
                                                      diff_rows[:, q, h * P:(h + 1) * P], ident)
                    ins.then_inc(mix_full, 1)
                n.add("rows", TT)
                n.add("mix", 4)

            def finish(self):
                n, e = self.n, self.e
                for i in range(2):
                    e.wait_ge(residual_new, n("residual", 4 * (i - 1)))
                    for t in range(TT):
                        for k in range(4):
                            ins = nc.tensor.transpose(bank[i + 2 * t][:, k * P:(k + 1) * P],
                                                      residual[:, 4 * i + k, (FIN * NT) + t * P:(FIN * NT) + (t + 1) * P], ident)
                        ins.then_inc(turned, 1)
                        n.add("turned", 1)

        FIN = debug[2] if debug else 0

        counter = Phases(None)
        program(counter)
        TOTAL[0] = counter.n.static("chunks")

        @block.sync
        def _(eng):
            program(Sync(eng))

        @block.gpsimd
        def _(eng):
            program(Pool(eng))

        @block.scalar
        def _(eng):
            program(Scalar(eng))

        @block.vector
        def _(eng):
            program(Vector(eng))

        @block.tensor
        def _(eng):
            program(Tensor(eng))


def kernel(**inputs):
    import numpy as _np
    import concourse.bacc as _bacc
    from concourse import mybir as _mybir
    from concourse.bass_utils import run_bass_kernel_spmd as _run

    nc = _bacc.Bacc("TRN2", target_bir_lowering=False, num_devices=1)
    arrays, aps = {}, {}
    for name, a in inputs.items():
        a = _np.ascontiguousarray(a)
        arrays[f"in_{name}"] = a
        aps[name] = nc.dram_tensor(f"in_{name}", a.shape, _mybir.dt.from_np(a.dtype), kind="ExternalInput").ap()
    arrays["consts"] = constant_table()
    consts = nc.dram_tensor("consts", arrays["consts"].shape, F32, kind="ExternalInput").ap()
    out = nc.dram_tensor("out", (1, NT, D), F32, kind="ExternalOutput").ap()
    build(nc, aps, consts, out)
    return _run(nc, [arrays], core_ids=[0]).results[0]["out"]
```

```python
from contextlib import ExitStack

import numpy as np

import concourse.bass as bass
from concourse import mybir

F32 = mybir.dt.float32
F32R = mybir.dt.float32r
BF16 = mybir.dt.bfloat16
ALU = mybir.AluOpType
ACT = mybir.ActivationFunctionType
AX = mybir.AxisListType

P = 128
D = 1024
KT = D // P
NT = 256
TT = NT // P
DH = 64
EPS = 1e-6
DEPTH = 2
MASKED = -1.0e30
TAKEN = -3.0e38
RAW, SPLIT = 4, 4
BODY = 4
WIDE = KT // 2
ADA_NORM = 12
NORM_AT = 48
DFT0, DFT1, DFT_OUT, TURN_W, SPATIAL, GATE_OUT = 0, 2, 4, 6, 8, 10
DIFF_NORM = 14
CW = 256

Q1, K1, V1, F1, U1, G1, IN1 = 0, 512, 640, 768, 1024, 1280, 1536
NQ1, NKV1 = 8, 2
FF1 = 4096
MQ, MK, MV, DQ, DK, DV, SQ, SK, SV, IQ, IK, IW, IN2 = (
    0, 256, 512, 768, 1280, 1792, 2304, 2560, 2816, 3072, 3584, 3648, 3656)
FF2 = 2816
IH = 8
TOPK = NT // 4

CONSTS = dict(ident=P, dft_n=TT * 2 * NT, dft_c=P, dft_s=P, cos1=TT * DH, sin1=TT * DH, cos2=TT * DH, sin2=TT * DH,
              mask=NT, sel=2)


def constant_table():
    t = {k: np.zeros((P, w), np.float32) for k, w in CONSTS.items()}
    t["ident"][:] = np.eye(P)
    n = np.arange(NT)
    ang = 2 * np.pi * ((n[:, None] * n[None, :]) % NT) / NT
    cs = np.concatenate([np.cos(ang), np.sin(ang)], 1)
    t["dft_n"][:] = cs.reshape(TT, P, 2 * NT).transpose(1, 0, 2).reshape(P, -1)
    d = np.arange(DH)
    ang = 2 * np.pi * ((d[:, None] * d[None, :]) % DH) / DH
    norm = 1.0 / np.sqrt(NT * DH)
    t["dft_c"][:] = np.kron(np.eye(2), np.cos(ang)) * norm
    t["dft_s"][:] = np.kron(np.eye(2), -np.sin(ang)) * norm
    pos = np.arange(NT, dtype=np.float32)
    inv = (np.float32(10000.0) ** (-np.arange(0, 32, 2, dtype=np.float32) / np.float32(32))).astype(np.float32)
    row, col = np.floor(pos / 64)[:, None] * inv, (pos % 64)[:, None] * inv
    inv2 = (np.float32(1.0) / (np.float32(10000.0) ** (np.arange(0, 64, 2, dtype=np.float32) / np.float32(64))))
    ang2 = pos[:, None] * inv2.astype(np.float32)
    for name, f, a in (("cos1", np.cos, 0), ("sin1", np.sin, 1), ("cos2", np.cos, 0), ("sin2", np.sin, 1)):
        parts = [row, row, col, col] if name[-1] == "1" else [ang2, ang2]
        v = [f(x) * (-1 if a and i % 2 == 0 else 1) for i, x in enumerate(parts)]
        t[name][:] = np.concatenate(v, 1).reshape(TT, P, DH).transpose(1, 0, 2).reshape(P, -1)
    t["mask"][:, P:] = np.where(np.arange(P)[None, :] <= np.arange(P)[:, None], 0, MASKED)
    t["sel"][0:4] = [[1, 0], [0, 1], [1, 0], [0, 1]]
    return np.concatenate([t[k] for k in CONSTS], 1).astype(np.float32)


class Tally:

    def __init__(self):
        self.n, self.it, self.step, self.last = {}, None, {}, {}

    def __call__(self, name, k=0):
        v = self.n.get(name, 0) + k
        s = self.step.get(name, 0)
        return v + self.it * s if self.it is not None and s else v

    def static(self, name):
        return self.n.get(name, 0)

    def add(self, name, k=1):
        self.n[name] = self.n.get(name, 0) + k

    def begin(self, it, step):
        self.it, self.step, self.last = it, step, dict(self.n)

    def end(self, times):
        for name, v in list(self.n.items()):
            d = v - self.last.get(name, 0)
            assert d == self.step.get(name, 0), (name, d, self.step.get(name, 0))
            self.n[name] = v + d * (times - 1)
        self.it, self.step = None, {}


def run_chunks(eng, n, count, per_chunk, body, tail=0, least=1):
    m = count - tail
    head = (m - 1) % BODY + 1 if m else 0
    while head < min(least, m):
        head += BODY
    times = (m - head) // BODY
    for j in range(head):
        body(j, j)
    if times == 1:
        for j in range(head, m):
            body(j, j)
    elif times > 1:
        with eng.Fori(0, times) as it:
            n.begin(it, {k: v * BODY for k, v in per_chunk.items()})
            for j in range(BODY):
                body(head + j, it * BODY + (head + j))
            n.end(times)
    for j in range(m, count):
        body(j, j)


def build(nc, A, consts, out):
    top = ExitStack()
    with top:
        def sb(name, shape, dt=F32, stack=top):
            return stack.enter_context(nc.sbuf_tensor(name, shape, dt))

        def sem(name):
            return top.enter_context(nc.semaphore(name))

        residual = sb("residual", [P, KT, 2 * NT])
        act_hi = sb("act_hi", [P, KT, NT], F32R)
        act_lo = sb("act_lo", [P, KT, NT], F32R)
        raw = sb("raw", [P, RAW, 2048])
        w_hi = sb("w_hi", [P, SPLIT, 1024], F32R)
        w_lo = sb("w_lo", [P, SPLIT, 1024], F32R)
        const = sb("const", [P, sum(CONSTS.values())])
        cols, at = {}, 0
        for name, w in CONSTS.items():
            cols[name] = const[:, at:at + w]
            at += w
        ident, sel, mask = cols["ident"], cols["sel"], cols["mask"]
        dft_n = cols["dft_n"].rearrange("p (t n) -> p t n", t=TT)
        rope = {b: [cols[f"{f}{b}"].rearrange("p (t d) -> p t d", t=TT) for f in ("cos", "sin")] for b in (1, 2)}
        ones = sb("ones", [P, P])
        neg_half = sb("neg_half", [P, 16])
        cond = sb("cond", [P, KT, P], F32R)
        k_t = sb("k_t", [P, NKV1, 2 * NT])
        v_rows = sb("v_rows", [P, 2 * TT, NKV1 * DH])
        mod = sb("mod", [P, 48, 2])
        mscale = sb("mscale", [P, 2, KT, 2])
        norm_g = sb("norm_g", [P, 2, KT])
        gains1 = sb("gains1", [P, 2 * DH + 256])
        w_sp = sb("w_sp", [P, 4, P])
        b_sp = sb("b_sp", [P, 4])
        norm2_g = sb("norm2_g", [P, DEPTH, 2, KT])
        gains2 = sb("gains2", [P, DEPTH, 3, 2, DH])
        lam_in = sb("lam_in", [P, DEPTH, 4 * DH])
        sub_g = sb("sub_g", [P, DEPTH, 2 * DH])
        variance = sb("variance", [P, DH])
        rstd = sb("rstd", [P, DH])
        diag = sb("diag", [P, TT, P])
        ident_b = sb("ident_b", [P, P], BF16)
        mask_b = sb("mask_b", [P, P], BF16)
        neg_max = sb("neg_max", [P, 32])
        total = sb("total", [P, 32])
        lam = sb("lam", [P, DEPTH, 8])
        best = sb("best", [P, 8])

        with ExitStack() as s:
            rows_in = sb("rows_in", [P, 2 * TT, D], stack=s)
            cond_raw = sb("cond_raw", [P, 4, KT, 2], stack=s)
            mod_rows = sb("mod_rows", [4, 4, CW], stack=s)
            bias_rows = sb("bias_rows", [6 * KT, P], stack=s)
        with ExitStack() as s:
            proj1 = sb("proj1", [P, TT, IN1], stack=s)
            q_t = sb("q_t", [P, NQ1 // 2, NT], stack=s)
            kdup = sb("kdup", [P, TT, 2 * NKV1, DH], stack=s)
            probs1 = sb("probs1", [P, 4, 2 * NT], stack=s)
            probs_t1 = sb("probs_t1", [P, 3, 2 * TT, P], stack=s)
            four = sb("four", [P, 2, 2 * NT], stack=s)
            w_sp_t = sb("w_sp_t", [P, 4, P], stack=s)
            gates = sb("gates", [P, TT, 512], stack=s)
            gtmp = sb("gtmp", [P, TT, 512], stack=s)
            head_sq1 = sb("head_sq1", [P, 2, 512], stack=s)
            rope_a1 = sb("rope_a1", [P, 2, 512], stack=s)
            rope_b1 = sb("rope_b1", [P, 2, 512], stack=s)
            cos_g1 = sb("cos_g1", [P, 2, TT, DH], stack=s)
            sin_g1 = sb("sin_g1", [P, 2, TT, DH], stack=s)
        with ExitStack() as s:
            proj2 = sb("proj2", [P, TT, IN2], stack=s)
            pairs_t = sb("pairs_t", [P, 21, NT], stack=s)
            ikdup = sb("ikdup", [P, TT, 2, DH], stack=s)
            seen = sb("seen", [P, TT, NT], BF16, stack=s)
            relu_t = sb("relu_t", [P, 2, NT], stack=s)
            score = sb("score", [P, TT, NT], stack=s)
            diff_rows = sb("diff_rows", [P, TT, 4 * P], stack=s)
            diff_sq = sb("diff_sq", [P, 4 * P], stack=s)
            cos_g2 = sb("cos_g2", [P, 6, TT, DH], stack=s)
            sin_g2 = sb("sin_g2", [P, 6, TT, DH], stack=s)
            with ExitStack() as s2:
                head_sq2 = sb("head_sq2", [P, 2, 512], stack=s2)
                rope_a2 = sb("rope_a2", [P, 2, 512], stack=s2)
                rope_b2 = sb("rope_b2", [P, 2, 512], stack=s2)
            with ExitStack() as s2:
                probs2 = sb("probs2", [P, 6, NT], stack=s2)
                probs_t2 = sb("probs_t2", [P, 3, TT, P], stack=s2)
        with ExitStack() as s:
            hid_hi = sb("hid_hi", [P, FF1 // P, NT], F32R, stack=s)
            hid_lo = sb("hid_lo", [P, FF1 // P, NT], F32R, stack=s)
            fa = sb("fa", [P, 2, 2 * NT], stack=s)
            fb = sb("fb", [P, 2, 2 * NT], stack=s)
            wide = sb("wide", [P, KT, NT], stack=s)

        bank = [top.enter_context(nc.psum_tensor(f"bank{i}", [P, 512], F32)) for i in range(8)]

        raw_loaded = [sem(f"raw_loaded{i}") for i in range(RAW)]
        hi_ready = sem("hi_ready")
        lo_ready = sem("lo_ready")
        multiplied = sem("multiplied")
        drained_act = sem("drained_act")
        squared = sem("squared")
        gate_exp = sem("gate_exp")
        gated = sem("gated")
        gate_hi = sem("gate_hi")
        hidden = sem("hidden")
        residual_new = sem("residual_new")
        squares = sem("squares")
        folded = sem("folded")
        sums = sem("sums")
        rstd_diag = sem("rstd_diag")
        rstd_wide = sem("rstd_wide")
        var_ready = sem("var_ready")
        rstd_ready = sem("rstd_ready")
        modulated = sem("modulated")
        norm_hi = sem("norm_hi")
        norm_lo = sem("norm_lo")
        consts_in = sem("consts_in")
        inputs_in = sem("inputs_in")
        cond_in = sem("cond_in")
        params_in = sem("params_in")
        params2_in = sem("params2_in")
        preset = sem("preset")
        cond_exp = sem("cond_exp")
        cond_ready = sem("cond_ready")
        mod_turned = sem("mod_turned")
        mod_out = sem("mod_out")
        bias_turned = sem("bias_turned")
        turned = sem("turned")
        turned_out = sem("turned_out")
        head_squares = sem("head_squares")
        rope_cos = sem("rope_cos")
        gates_ready = sem("gates_ready")
        tables_ready = sem("tables_ready")
        rows_ready = sem("rows_ready")
        v_kept = sem("v_kept")
        scored = sem("scored")
        max_ready = sem("max_ready")
        exped = sem("exped")
        prob_ready = sem("prob_ready")
        prob_turned = sem("prob_turned")
        prob_t = sem("prob_t")
        mixed = sem("mixed")
        mix_hi = sem("mix_hi")
        mix_lo = sem("mix_lo")
        dft_full = sem("dft_full")
        dft_out = sem("dft_out")
        mix_full = sem("mix_full")
        gelu_in = sem("gelu_in")
        gelu_tanh = sem("gelu_tanh")
        spatial = sem("spatial")
        logit_full = sem("logit_full")
        logit_relu = sem("logit_relu")
        logit_used = sem("logit_used")
        seen_ready = sem("seen_ready")
        lam_exp = sem("lam_exp")
        lam_sums = sem("lam_sums")
        diff_drained = sem("diff_drained")
        diff_squares = sem("diff_squares")
        final_rows = sem("final_rows")
        stored = sem("stored")
        act_order = sem("act_order")
        dve_order = sem("dve_order")
        block = top.enter_context(nc.Block())

        A_ = A
        TOTAL = [0]

        def program(ph):
            ph.load()
            ph.params(0)
            for l in range(DEPTH):
                ph.ada(l)
                ph.modulation(l)
                for s in (1, 0):
                    kv_only = s == 1 and l == DEPTH - 1
                    ph.norm(s, 1, 0, False, l)
                    ph.rows(rows1(s, kv_only), A_["w_in"], l)
                    if kv_only:
                        continue
                    ph.attend1(s)
                    ph.down("mix", D // P // 2, dict(w=A_["w_out"], l=l), s, 16, True)
                    ph.norm(s, 1, 1, True, l)
                    if l == DEPTH - 1:
                        for i in range(DEPTH):
                            ph.params2(i)
                    ph.up("relu2", FF1 // CW, dict(w=A_["w_mlp1"], l=l, base=0))
                    ph.down("hidden", FF1 // P // 2, dict(w=A_["w_mlp2"], l=l), s, 40, l == DEPTH - 1)
                if l + 1 < DEPTH:
                    ph.params(l + 1)
            for l in range(DEPTH):
                ph.norm(0, 2, 0, True, l)
                ph.rows(rows2(), A_["w_in_2"], l)
                ph.attend2(l)
                ph.down("mix", D // P // 2, dict(w=A_["w_out_2"], l=l), 0, None, True)
                ph.norm(0, 2, 1, True, l)
                ph.up("silu", FF2 // P, dict(w=A_["w_gate_2"], w2=A_["w_up_2"], l=l, base=0))
                ph.down("hidden", FF2 // P // 2, dict(w=A_["w_down_2"], l=l), 0, None, l < DEPTH - 1)
            ph.finish()

        def tiles(ap, k):
            return ap.rearrange("p (k n) -> p k n", k=k)

        class Phases:

            def __init__(self, eng):
                self.e, self.n = eng, Tally()
                self.behind = ()

            def load(self): self.n.add("turned", 8)
            def params(self, l): self.n.add("params", 1)
            params2 = params
            def ada(self, l): self.chunks("ada", 24)
            def up(self, kind, count, w): self.chunks(kind, count)
            def down(self, kind, count, w, s, gate, norm_next):
                self.chunks("down", count)
                self.n.add("residual", KT)

            def chunks(self, kind, count):
                self.n.add("chunks", count)
                if kind == "ada":
                    self.n.add("drained_act", count)
                if kind == "relu2":
                    self.n.add("drained_act", count)
                    self.n.add("hidden", count)
                if kind == "silu":
                    self.n.add("gated", count)
                    self.n.add("hidden", count)

            def modulation(self, l): self.n.add("mod", 1)
            def norm(self, s, b, which, summed, l):
                self.n.add("norm", 1)
            def rows(self, plan, w, l):
                self.n.add("chunks", len(plan))
                self.n.add("drained_act", len(plan))

            def attend1(self, s):
                self.n.add("scores", 16)
                self.n.add("items", 16)
                self.n.add("fourier", 1)
                self.n.add("gmlp", 1)
                self.n.add("turned", 1)
                self.n.add("mix", 4)
            def attend2(self, l):
                self.n.add("scores", 32)
                self.n.add("items", 24)
                self.n.add("mix", 4)
            def finish(self): pass

        def items1(s):
            keys = TT if s == 1 else 2 * TT
            out = []
            for h in range(NQ1):
                kv, half = h // (NQ1 // NKV1), DH * (h % 2)
                for qt in range(TT):
                    q = q_t[half:half + DH, h // 2, qt * P:(qt + 1) * P]
                    k = k_t[half:half + DH, kv, 0:keys * P]
                    v = [v_rows[:, i, kv * DH:(kv + 1) * DH] for i in range(keys)]
                    o = bank[6 + h // 4][half:half + DH, (h // 2 % 2) * NT + qt * P:(h // 2 % 2) * NT + (qt + 1) * P]
                    out.append(dict(scores=[(q, k, None)], keys=keys, v=v, o=o,
                                    done=(6 + h // 4, 2 * (h // 4)) if h % 4 == 3 and qt == TT - 1 else None))
            return out

        PAIR = dict(mq=0, mk=2, dq=4, dk=8, sq=12, sk=14, iq=16, ik=20)

        def pair(name, h, lo, hi):
            half = DH * (h % 2)
            return pairs_t[half:half + DH, PAIR[name] + h // 2, lo:hi]

        def heads_of(ap):
            return ap.rearrange("p t (h d) -> p t h d", d=DH)

        def rows1(s, kv_only):
            sin = [sin_g1[:, i] if s == 0 else None for i in range(2)]
            cos = [cos_g1[:, i] if s == 0 else gains1[:, i * DH:(i + 1) * DH].unsqueeze(1).broadcast_to([P, TT, DH])
                   for i in range(2)]
            kd = kdup[:].rearrange("p t (h c) d -> p t h c d", c=2)
            kt0 = 0 if s == 1 else TT
            common = dict(block=1, stream=s, normed=True, axes=2, sq=head_sq1, a=rope_a1, b=rope_b1)
            plan = [dict(col=K1, wd=CW, v_kept=kt0,
                         heads=dict(common, n=NKV1, x=heads_of(proj1[:, :, K1:K1 + NKV1 * DH]), cos=cos[1], sin=sin[1],
                                    dst=[kd[:, :, :, c, :] for c in range(2)],
                                    turn=[kdup[:, t, 2 * j:2 * j + 2, :].rearrange("p h d -> p (h d)") for j in range(2) for t in range(TT)],
                                    out=k_t[:, :, kt0 * P:(kt0 + TT) * P], scale=None))]
            if kv_only:
                return plan
            for i in range(2):
                c = Q1 + i * CW
                x = heads_of(proj1[:, :, c:c + CW])
                plan.append(dict(col=c, wd=CW, heads=dict(
                    common, n=4, x=x, cos=cos[0], sin=sin[0], dst=[x],
                    turn=[proj1[:, t, c + j * P:c + (j + 1) * P] for j in range(2) for t in range(TT)],
                    out=q_t[:, 2 * i:2 * i + 2, :], scale=DH ** -0.5)))
            plan += [dict(col=G1, wd=CW, gelu=1), dict(col=U1, wd=CW, gelu=0), dict(col=F1, wd=CW)]
            return plan

        INDEX_AT, SEARCH_AT = 6, 11

        def rows2():
            common = dict(block=2, stream=0, axes=1, sq=head_sq2, a=rope_a2, b=rope_b2)
            plan = []
            for c, p0, g, q in ((IQ, 16, None, 1), (IQ + CW, 18, None, 1), (IK, 20, None, 0), (MQ, 0, 0, 1), (MK, 2, 1, 0),
                                (SQ, 12, 4, 1), (SK, 14, 5, 0), (DQ, 4, 2, 1), (DQ + CW, 6, 2, 1), (DK, 8, 3, 0), (DK + CW, 10, 3, 0)):
                one = c == IK
                n = 1 if one else 4
                x = heads_of(proj2[:, :, c:c + n * DH])
                plan.append(dict(col=c, wd=IN2 - IK if one else CW, heads=dict(
                    common, normed=g is not None, n=n, x=x, dst=[ikdup[:, :, i:i + 1, :] for i in range(2)] if one else [x],
                    cos=rope[2][0] if g is None else cos_g2[:, g], sin=rope[2][1] if g is None else sin_g2[:, g],
                    turn=[ikdup[:, t].rearrange("p h d -> p (h d)") for t in range(TT)] if one else
                         [proj2[:, t, c + j * P:c + (j + 1) * P] for j in range(2) for t in range(TT)],
                    out=pairs_t[:, p0:p0 + (1 if one else 2), :], scale=DH ** -0.5 if q else None)))
            return plan + [dict(col=c, wd=CW) for c in (SV, MV, DV, DV + CW)]

        def causal(qt):
            return mask[:, P:2 * P] if qt == 0 else mask[:, :]

        def items2():
            out = []
            for h in range(4):
                for qt in range(TT):
                    n = (qt + 1) * P
                    half = DH * (h % 2)
                    o = bank[6][half:half + DH, h // 2 * NT + qt * P:h // 2 * NT + (qt + 1) * P]
                    out.append(dict(scores=[(pair("mq", h, qt * P, n), pair("mk", h, 0, n), mask_b[:])], keys=qt + 1,
                                    v=[proj2[:, i, MV + h * DH:MV + (h + 1) * DH] for i in range(qt + 1)], o=o,
                                    done=(6, 0) if h == 3 and qt == TT - 1 else None))
            dsa = []
            for h in range(4):
                for qt in range(TT):
                    n = (qt + 1) * P
                    half = DH * (h % 2)
                    o = bank[7][half:half + DH, h // 2 * NT + qt * P:h // 2 * NT + (qt + 1) * P]
                    dsa.append(dict(scores=[(pair("sq", h, qt * P, n), pair("sk", h, 0, n), seen[:, qt, 0:n])],
                                    keys=qt + 1, o=o, done=(7, 6) if h == 3 and qt == TT - 1 else None,
                                    v=[proj2[:, i, SV + h * DH:SV + (h + 1) * DH] for i in range(qt + 1)]))
            for qt in range(TT):
                for h in range(4):
                    n = (qt + 1) * P
                    o = bank[7 - qt][:, h * P:(h + 1) * P]
                    out.append(dict(scores=[(pair("dq", 2 * h + i, qt * P, n), pair("dk", 2 * h + i, 0, n), mask_b[:])
                                            for i in range(2)],
                                    keys=qt + 1, o=o, diff=True, done=(7 - qt, ("rows", qt)) if h == 3 else None,
                                    v=[proj2[:, i, DV + h * P:DV + (h + 1) * P] for i in range(qt + 1)]))
            return out + dsa

        class Sync(Phases):
            def load(self):
                super().load()
                self.e.dma_start(rows_in[:, 0:TT, :], A_["x"][0].rearrange("(t p) n -> p t n", p=P)).then_inc(inputs_in, 16)
                self.e.dma_start(rows_in[:, TT:, :], A_["ctx"][0].rearrange("(t p) n -> p t n", p=P)).then_inc(inputs_in, 16)
                self.e.dma_start(const[:], consts).then_inc(consts_in, 16)

            def chunk_loads(self, count, pieces, tail=0):
                e, n = self.e, self.n
                base = n.static("chunks")

                def body(j, at):
                    slot = (base + j) % RAW
                    if n.static("chunks") >= RAW:
                        e.wait_ge(lo_ready, n("halves", -2 * (RAW - 1)))
                    for dst, src in pieces(slot, j, at):
                        e.dma_start(dst, src).then_inc(raw_loaded[slot], 16)
                    n.add("chunks", 1)
                    n.add("halves", 2)

                run_chunks(e, n, count, dict(chunks=1, halves=2), body, tail)

            def kslices(self, w, l, base, width):
                src = w[l].rearrange("(k p) n -> p k n", p=P)

                def pieces(slot, j, at):
                    dst = tiles(raw[:, slot, :], KT)
                    wd = min(CW, width - j * CW)
                    for h in range(2):
                        yield (dst[:, 4 * h:4 * h + 4, 0:wd], src[:, 4 * h:4 * h + 4, bass.ds(at * CW + base, wd)])
                return pieces

            def ada(self, l):
                self.chunk_loads(24, self.kslices(A_["w_ada"], l, 0, 6 * D))

            def up(self, kind, count, w):
                if kind != "silu":
                    self.chunk_loads(count, self.kslices(w["w"], w["l"], w["base"], FF1))
                    return
                gate, up_ = (w[k][w["l"]].rearrange("(k p) n -> p k n", p=P) for k in ("w", "w2"))

                def pieces(slot, j, at):
                    dst = tiles(raw[:, slot, :], KT)
                    yield dst[:, :, 0:P], gate[:, :, bass.ds(at * P, P)]
                    yield dst[:, :, P:2 * P], up_[:, :, bass.ds(at * P, P)]
                self.chunk_loads(count, pieces)

            def rows(self, plan, w, l):
                src = w[l].rearrange("(k p) n -> p k n", p=P)

                def pieces(slot, j, at):
                    c = plan[j]
                    for h in range(2):
                        yield (tiles(raw[:, slot, :], KT)[:, 4 * h:4 * h + 4, 0:c["wd"]],
                               src[:, 4 * h:4 * h + 4, c["col"]:c["col"] + c["wd"]])
                self.chunk_loads(len(plan), pieces, len(plan))

            def down(self, kind, count, w, s, gate, norm_next):
                src = w["w"][w["l"]].rearrange("(c k p) n -> p c k n", p=P, k=2)

                last = w["w"][w["l"]].rearrange("(k p) n -> p k n", p=P)[:, 2 * count - KT:, :]

                def pieces(slot, j, at):
                    c = j - (count - WIDE)
                    for k in range(2):
                        if c < 0:
                            yield tiles(raw[:, slot, :], 2)[:, k, :], src[:, at, k, :]
                        else:
                            yield tiles(raw[:, slot, :], KT)[:, 4 * k:4 * k + 4, :], last[:, 4 * k:4 * k + 4, c * CW:(c + 1) * CW]
                self.chunk_loads(count, pieces, WIDE)
                self.n.add("residual", KT)

            def finish(self):
                for i in range(2):
                    self.e.wait_ge(final_rows, 2 * TT * (i + 1))
                    self.e.dma_start(out[0].rearrange("(t p) n -> p t n", p=P)[:, :, i * 512:(i + 1) * 512],
                                     rows_in[:, 0:TT, i * 512:(i + 1) * 512]).then_inc(stored, 16)
                self.e.wait_ge(stored, 2 * 16)

        class Pool(Phases):
            def load(self):
                super().load()
                nc.gpsimd.memset(ones[:], 1.0).then_inc(preset, 1)
                nc.gpsimd.memset(neg_half[:], -0.5).then_inc(preset, 1)
                for i, name in enumerate(("c", "c_ctx")):
                    src = A_["c"][0] if name == "c" else A_["c_ctx"]
                    self.e.dma_start(cond_raw[:, 0, :, i], src.rearrange("(k p) -> p k", p=P), allow_slow_non_contiguous=True).then_inc(cond_in, 16)
                self.e.wait_ge(preset, 2)

            def ada(self, l):
                if l == 0:
                    self.e.wait_ge(turned_out, 8)
                else:
                    self.e.wait_ge(residual_new, self.n("residual"))
                self.e.dma_start(bias_rows[:], A_["b_ada"][l].rearrange("(j p) -> j p", p=P)).then_inc(params_in, 16)
                super().ada(l)
                for s in (1, 0):
                    self.sum_up(s)

            def params(self, l):
                e = self.e
                if l:
                    e.wait_ge(residual_new, self.n("residual"))
                for i, k in enumerate(("norm1_g", "norm2_g")):
                    e.dma_start(norm_g[:, i, :], A_[k][l].rearrange("(k p) -> p k", p=P), allow_slow_non_contiguous=True).then_inc(params_in, 16)
                at = 0
                for k, w in (("q_norm_g", DH), ("k_norm_g", DH), ("gmlp_v_g", 256)):
                    e.dma_start(gains1[:, at:at + w], A_[k][l:l + 1, :].broadcast_to([P, w])).then_inc(params_in, 16)
                    at += w
                e.dma_start(w_sp[:], A_["w_spatial"][l].rearrange("h p q -> p h q")).then_inc(params_in, 16)
                e.dma_start(b_sp[:], A_["b_spatial"][l].rearrange("h p -> p h"), allow_slow_non_contiguous=True).then_inc(params_in, 16)
                super().params(l)

            def attend1(self, s):
                if s == 1:
                    for l in range(DEPTH):
                        self.load_params2(l)
                super().attend1(s)

            def load_params2(self, l):
                e = self.e
                for i, k in enumerate(("attn_norm_g_2", "ffn_norm_g_2")):
                    e.dma_start(norm2_g[:, l, i, :], A_[k][l].rearrange("(k p) -> p k", p=P), allow_slow_non_contiguous=True).then_inc(params2_in, 16)
                for i, k in enumerate(("q_norm_g_2", "k_norm_g_2")):
                    e.dma_start(gains2[:, l, :, i, :], A_[k][l:l + 1].broadcast_to([P, 3, DH])).then_inc(params2_in, 16)
                e.dma_start(tiles(lam_in[:, l], 4), A_["diff_lambda_2"][l:l + 1].broadcast_to([P, 4, DH])).then_inc(params2_in, 16)
                e.dma_start(sub_g[:, l], A_["diff_subln_g_2"][l:l + 1, :].broadcast_to([P, P])).then_inc(params2_in, 16)

            def power(self, at, w):
                self.e.wait_ge(var_ready, self.n("pow", 1))
                nc.gpsimd.tensor_tensor(rstd[:, at:at + w], variance[:, at:at + w], neg_half[:, 0:w], ALU.pow).then_inc(rstd_ready, 1)
                self.n.add("pow", 1)

            def norm(self, s, b, which, summed, l):
                if summed:
                    self.sum_up(s)
                self.n.add("norm", 1)

            def sum_up(self, s):
                n, e = self.n, self.e

                def fold(step, squared_, o, a, b):
                    e.wait_ge(squares, 5 * n("sum") + squared_)
                    if step:
                        e.wait_ge(folded, 3 * n("sum") + step)
                    nc.gpsimd.tensor_tensor(o, a, b, ALU.add).then_inc(folded, 1)
                fold(0, 2, wide[:, 0:2, :], wide[:, 0:2, :], wide[:, 2:4, :])
                fold(1, 3, wide[:, 0:2, :], wide[:, 0:2, :], wide[:, 4:6, :])
                fold(2, 3, wide[:, 0:1, :], wide[:, 0:1, :], wide[:, 1:2, :])
                self.power(NORM_AT + TT * s, TT)
                n.add("sum", 1)

            def rows(self, plan, w, l):
                n, e = self.n, self.e
                n.add("tables", 1)
                e.wait_ge(tables_ready, n("tables"))
                r = m = 0
                for j, c in enumerate(plan):
                    n.add("drained_act", 1)
                    h = c.get("heads")
                    if h:
                        e.wait_ge(drained_act, n("drained_act"))
                        if r >= 2:
                            e.wait_ge(rows_ready, n("rows", r - 1))
                        x = h["x"]
                        nc.gpsimd.tensor_tensor(heads_of(tiles(h["a"][:, r % 2, 0:TT * h["n"] * DH], TT)), x,
                                                h["cos"].unsqueeze(2).broadcast_to([P, TT, h["n"], DH]), ALU.mult).then_inc(rope_cos, 1)
                        r += 1
                        if h["normed"]:
                            self.power(16 * (m % 2), TT * h["n"])
                            m += 1
                    if c.get("gelu") == 1:
                        self.power(32, 4 * TT)
                n.add("chunks", len(plan))
                n.add("rows", r)

            def attend2(self, l):
                for t in range(TT):
                    self.power(8 * t, 4)
                self.n.add("rows", TT)
                super().attend2(l)

        def params_until(phase, l):
            return 16 * (8 * l + (8 if phase == "bias" else 7))

        class Scalar(Phases):
            def __init__(self, eng):
                super().__init__(eng)
                self.var0 = 0

            def order(self, ins):
                ins.then_inc(act_order, 1)
                self.n.add("act_order", 1)
                self.e.wait_ge(act_order, self.n("act_order"))

            def split(self, k, halves=(0, 1)):
                n, e = self.n, self.e
                c = n.static("chunks") + k
                e.wait_ge(raw_loaded[c % RAW], self.loaded(c, k))
                for h in halves:
                    if 2 * c + h >= SPLIT:
                        e.wait_ge(multiplied, n("halves", 2 * k + h + 1 - SPLIT))
                    nc.scalar.copy(w_hi[:, (2 * c + h) % SPLIT, :], raw[:, c % RAW, h * 1024:(h + 1) * 1024]).then_inc(hi_ready, 1)

            def loaded(self, c, k):
                v = 32 * (c // RAW + 1)
                s = self.n.step.get("chunks", 0)
                return v + self.n.it * (32 * (s // RAW)) if self.n.it is not None and s else v

            def stream(self, count, kind, drain, extra=None, tail=0, finish=None, early=False):
                n = self.n
                self.catch_up()

                def body(j, at):
                    if drain:
                        self.e.wait_ge(multiplied, n("halves", 2))
                        drain(j, at)
                    if n.static("chunks") + 2 < TOTAL[0]:
                        if j < count - 1:
                            self.split(2)
                        elif early:
                            self.split(2, (0,))
                    if finish:
                        finish(j, at)
                    n.add("chunks", 1)
                    n.add("halves", 2)

                run_chunks(self.e, n, count, dict(chunks=1, halves=2, **(extra or {})), body, max(tail, 1))
                self.behind = ((1,) if early else (0, 1)) if n.static("chunks") + 1 < TOTAL[0] else ()

            def catch_up(self):
                if self.behind:
                    self.split(1, self.behind)
                    self.behind = ()

            def load(self):
                super().load()
                e = self.e
                e.wait_ge(cond_in, 32)
                nc.scalar.activation(cond_raw[:, 1, :, :], cond_raw[:, 0, :, :], ACT.Exp, scale=-1.0).then_inc(cond_exp, 1)
                self.split(0)
                self.split(1)

            def ada(self, l):
                def drain(j, at):
                    nc.scalar.copy(mod_rows[:, j % 4, :], bank[j % 4][0:4, 0:CW]).then_inc(drained_act, 1)
                    self.n.add("drained_act", 1)
                if l == 0:
                    self.e.wait_ge(turned_out, 8)

                def finish(j, at):
                    for i, s in enumerate((1, 0)):
                        if j == ADA_NORM + 5 * i:
                            if i:
                                self.e.wait_ge(sums, self.n("sum"))
                            if l:
                                self.e.wait_ge(residual_new, self.n("residual"))
                            for c in range(WIDE):
                                self.square(s, c, False)
                            self.n.add("sum", 1)
                            self.var0 += 1
                self.stream(24, "ada", drain, dict(drained_act=1), 24 - ADA_NORM, finish)

            def up(self, kind, count, w):
                n, e = self.n, self.e
                if kind == "relu2":
                    def drain(j, at):
                        if j >= 2:
                            e.wait_ge(hidden, n("hidden", -1))
                        nc.scalar.activation(fa[:, j % 2, :], bank[j % 4][:], ACT.Relu).then_inc(drained_act, 1)
                        n.add("drained_act", 1)
                        n.add("hidden", 1)
                        e.wait_ge(drained_act, n("drained_act"))
                        e.wait_ge(preset, 2)
                        nc.scalar.activation(hid_hi[:, bass.ds(at * 2, 2), :], tiles(fa[:, j % 2, :], 2),
                                             ACT.Square).then_inc(squared, 1)
                    self.stream(count, kind, drain, dict(drained_act=1, hidden=1))
                else:
                    def drain(j, at):
                        if j >= 2:
                            e.wait_ge(hidden, n("hidden", -1))
                        ex = fa[:, j % 2, 0:NT]
                        self.order(nc.scalar.activation(ex, bank[j % 4][:, 0:NT], ACT.Exp, scale=-1.0))
                        nc.scalar.add(ex, ex, 1.0).then_inc(gate_exp, 1)

                    def finish(j, at):
                        n.add("hidden", 1)
                        n.add("gated", 1)
                        e.wait_ge(gated, n("gated"))
                        e.wait_ge(preset, 2)
                        nc.scalar.copy(hid_hi[:, bass.ds(at, 1), :], tiles(fb[:, j % 2, 0:NT], 1)).then_inc(gate_hi, 1)
                    self.stream(count, kind, drain, dict(hidden=1, gated=1, act_order=1), finish=finish)

            def down(self, kind, count, w, s, gate, norm_next):
                n, e = self.n, self.e

                def finish(j, at):
                    if norm_next and j >= count - WIDE:
                        self.square(s, j - (count - WIDE), True)
                self.stream(count, kind, None, tail=WIDE, finish=finish, early=True)
                n.add("residual", KT)

            def square(self, s, c, updated):
                for k, w in ((2 * c, 2),) if c < WIDE - 1 else ((2 * c, 1), (2 * c + 1, 1)):
                    if updated:
                        self.e.wait_ge(residual_new, self.n("residual", k + w))
                    nc.scalar.activation(wide[:, k:k + w, :], residual[:, k:k + w, s * NT:(s + 1) * NT],
                                         ACT.Square).then_inc(squares, 1)

            def norm(self, s, b, which, summed, l):
                n, e = self.n, self.e
                if summed:
                    self.catch_up()
                    n.add("sum", 1)
                    self.var0 += 1
                for k in range(KT):
                    e.wait_ge(modulated, KT * n("norm") + k + 1)
                    o, x = act_hi[:, k, :], wide[:, k, :]
                    if b == 1:
                        ins = nc.scalar.activation(o, x, ACT.Identity, bias=mod[:, 24 * which + k, s:s + 1])
                    else:
                        ins = nc.scalar.copy(o, x)
                    ins.then_inc(norm_hi, 1)
                self.catch_up()
                n.add("norm", 1)

            def turn_out(self, dst, src, scale=None):
                n, e = self.n, self.e
                e.wait_ge(turned, n("turned", 1))
                if scale is None:
                    nc.scalar.copy(dst, src).then_inc(turned_out, 1)
                else:
                    nc.scalar.mul(dst, src, scale).then_inc(turned_out, 1)
                n.add("turned", 1)

            def mix_out(self, b, k):
                nc.scalar.copy(act_hi[:, k:k + 2, :], tiles(b, 2)).then_inc(mix_hi, 1)

            def rows(self, plan, w, l):
                n, e = self.n, self.e
                roped = [c["heads"] for c in plan if "heads" in c]
                proj = proj1 if roped[0]["block"] == 1 else proj2
                base = n.static("head_squares")

                def drain(j, at):
                    c = plan[j]
                    src = tiles(bank[j % 4][:], TT)[:, :, 0:c["wd"]]
                    h = c.get("heads")
                    if h and h["normed"]:
                        m = n.static("head_squares") - base
                        if m >= 2:
                            e.wait_ge(var_ready, self.var0 + m - 1)
                        nc.scalar.activation(tiles(h["sq"][:, m % 2, 0:TT * h["n"] * DH], TT), src[:, :, 0:h["n"] * DH],
                                             ACT.Square).then_inc(head_squares, 1)
                        n.add("head_squares", 1)
                    if "v_kept" in c:
                        nc.scalar.copy(v_rows[:, c["v_kept"]:c["v_kept"] + TT, :], src[:, :, P:2 * P]).then_inc(v_kept, 1)
                        n.add("v_kept", 1)
                    nc.scalar.copy(proj[:, :, c["col"]:c["col"] + c["wd"]], src).then_inc(drained_act, 1)
                    n.add("drained_act", 1)

                def finish(j, at):
                    if j < len(plan) and "gelu" in plan[j]:
                        e.wait_ge(gelu_in, n("gelus", 1))
                        g = gtmp[:, :, 256 * plan[j]["gelu"]:256 * (plan[j]["gelu"] + 1)]
                        nc.scalar.activation(g, g, ACT.Tanh, scale=float(np.sqrt(2 / np.pi))).then_inc(gelu_tanh, 1)
                        n.add("gelus", 1)
                    if 0 <= j - 3 < len(roped):
                        h = roped[j - 3]
                        w_ = h["out"].shape[1]
                        self.turn_out(h["out"], tiles(bank[4 + (j - 3) % 2][:, 0:w_ * NT], w_), h["scale"])
                    if proj is proj2 and INDEX_AT <= j < INDEX_AT + 8:
                        for i in range(2 * (j - INDEX_AT), 2 * (j - INDEX_AT) + 2):
                            wd = (i // IH + 1) * P
                            e.wait_ge(logit_full, n("logits", 1))
                            if i >= 2:
                                e.wait_ge(logit_used, n("logits", -1))
                            nc.scalar.activation(relu_t[:, i % 2, 0:wd], bank[6 + i % 2][:, 0:wd], ACT.Relu).then_inc(logit_relu, 1)
                            n.add("logits", 1)

                self.stream(len(plan), "rows", drain, None, len(plan), finish)
                for j in range(len(plan), len(roped) + 3):
                    finish(j, j)
                self.var0 += sum(h["normed"] for h in roped) + (1 if len(plan) == 6 else 0)

            def attention(self, items, probs, probs_t, ring=4, beside={}):
                n, e = self.n, self.e
                s0, i0 = n.static("scores"), n.static("items")
                first = [0]
                for it in items:
                    first.append(first[-1] + len(it["scores"]))

                slots = probs.shape[1]

                def exps(j):
                    if j >= len(items):
                        return
                    for s in range(first[j], first[j + 1]):
                        width = items[j]["keys"] * P
                        e.wait_ge(max_ready, s0 + s + 1)
                        if s >= slots:
                            prev = next(x for x in range(len(items)) if first[x] <= s - slots < first[x + 1])
                            e.wait_ge(prob_turned, i0 + prev + 1)
                        nc.scalar.activation(probs[:, s % slots, 0:width], bank[s % ring][:, 0:width], ACT.Exp,
                                             bias=neg_max[:, s:s + 1], accum_out=total[:, s:s + 1]).then_inc(exped, 1)

                def out_(j):
                    done = items[j]["done"] if j >= 0 else None
                    if done and not isinstance(done[1], tuple):
                        e.wait_ge(mixed, i0 + j + 1)
                        self.mix_out(bank[done[0]][:], done[1])
                exps(0)
                exps(1)
                for j, it in enumerate(items):
                    exps(j + 2)
                    e.wait_ge(prob_turned, i0 + j + 1)
                    if j >= 3:
                        e.wait_ge(mixed, i0 + j - 2)
                    w = it["keys"]
                    nc.scalar.copy(probs_t[:, j % 3, 0:w, :], tiles(bank[4 + j % 2][:, 0:w * P], w)).then_inc(prob_t, 1)
                    out_(j - 2)
                    if j in beside:
                        beside[j]()
                out_(len(items) - 2)
                out_(len(items) - 1)
                n.add("scores", first[-1])
                n.add("items", len(items))

            def attend1(self, s):
                n, e = self.n, self.e

                def spectrum(i):
                    e.wait_ge(dft_full, 2 * n("fourier") + i + 1)
                    nc.scalar.copy(four[:, i, :], bank[3][:]).then_inc(dft_out, 1)

                def mixed_out(i):
                    e.wait_ge(mix_full, 2 * n("gmlp") + i + 1)
                    self.mix_out(bank[3][:], 4 + 2 * i)
                self.attention(items1(s), probs1, probs_t1, 3, {
                    DFT0: lambda: spectrum(0), DFT1: lambda: spectrum(1), DFT_OUT: lambda: mixed_out(0),
                    TURN_W: lambda: self.turn_out(w_sp_t[:], tiles(bank[3][:], 4)), GATE_OUT: lambda: mixed_out(1)})
                n.add("fourier", 1)
                n.add("gmlp", 1)
                n.add("mix", 4)

            def attend2(self, l):
                n, e = self.n, self.e
                def diff_square(t):
                    e.wait_ge(diff_drained, TT * l + t + 1)
                    for h in range(4):
                        ins = nc.scalar.activation(diff_sq[:, h * P:(h + 1) * P], diff_rows[:, t, h * P:(h + 1) * P], ACT.Square,
                                                   accum_out=variance[:, 8 * t + h:8 * t + h + 1])
                    ins.then_inc(diff_squares, 1)
                self.attention(items2(), probs2, probs_t2, beside={DIFF_NORM: lambda: diff_square(0), DIFF_NORM + 4: lambda: diff_square(1)})
                for t in range(TT):
                    e.wait_ge(mix_full, 2 * n("gmlp") + 2 * l + t + 1)
                    self.mix_out(bank[4 + t][:], 2 + 2 * t)
                self.var0 += TT
                n.add("mix", 4)

            def params2(self, l):
                super().params2(l)
                self.e.wait_ge(lam_sums, l + 1)
                nc.scalar.activation(lam[:, l, 2:4], lam[:, l, 0:2], ACT.Exp).then_inc(lam_exp, 1)

            def finish(self):
                n, e = self.n, self.e
                for i in range(2):
                    for t in range(TT):
                        e.wait_ge(turned, n("turned", 1))
                        for q in range(2):
                            nc.scalar.copy(rows_in[:, t, i * 512 + q * 256:i * 512 + (q + 1) * 256],
                                           bank[i + 2 * t][:, q * 256:(q + 1) * 256]).then_inc(final_rows, 1)
                        n.add("turned", 1)

        class Vector(Phases):
            def order(self, ins):
                ins.then_inc(dve_order, 1)
                self.n.add("dve_order", 1)
                self.e.wait_ge(dve_order, self.n("dve_order"))

            def split(self, k, halves=(0, 1)):
                n, e = self.n, self.e
                c = n.static("chunks") + k
                for h in halves:
                    e.wait_ge(hi_ready, n("halves", 2 * k + h + 1))
                    slot = (2 * c + h) % SPLIT
                    nc.vector.tensor_tensor(w_lo[:, slot, :], raw[:, c % RAW, h * 1024:(h + 1) * 1024],
                                            w_hi[:, slot, :].bitcast(F32), ALU.subtract).then_inc(lo_ready, 1)

            def stream(self, count, drain, extra=None, tail=0, finish=None, early=False):
                n = self.n
                self.catch_up()

                def body(j, at):
                    if drain:
                        drain(j, at)
                    if n.static("chunks") + 2 < TOTAL[0]:
                        if j < count - 1:
                            self.split(2)
                        elif early:
                            self.split(2, (0,))
                    if finish:
                        finish(j, at)
                    n.add("chunks", 1)
                    n.add("halves", 2)

                run_chunks(self.e, n, count, dict(chunks=1, halves=2, **(extra or {})), body, max(tail, 1))
                self.behind = ((1,) if early else (0, 1)) if n.static("chunks") + 1 < TOTAL[0] else ()

            def catch_up(self):
                if self.behind:
                    self.split(1, self.behind)
                    self.behind = ()

            def load(self):
                n, e = self.n, self.e
                for k in range(KT):
                    e.wait_ge(turned, k + 1)
                    nc.vector.tensor_copy(residual[:, k, :], bank[k][:]).then_inc(turned_out, 1)
                n.add("turned", 8)
                nc.vector.tensor_copy(ident_b[:], ident)
                nc.vector.tensor_copy(mask_b[:], causal(0))
                self.order(nc.vector.memset(cond[:].bitcast(mybir.dt.uint32), 0))
                e.wait_ge(cond_exp, 1)
                self.order(nc.vector.tensor_scalar(cond_raw[:, 1], cond_raw[:, 1], 1.0, None, ALU.add))
                self.order(nc.vector.reciprocal(cond_raw[:, 1], cond_raw[:, 1]))
                e.wait_ge(cond_in, 32)
                self.order(nc.vector.tensor_tensor(cond_raw[:, 2], cond_raw[:, 0], cond_raw[:, 1], ALU.mult))
                self.order(nc.vector.tensor_copy(cond[:, :, 0:2], cond_raw[:, 2]))
                nc.vector.tensor_tensor(cond[:, :, 2:4], cond_raw[:, 2], cond[:, :, 0:2].bitcast(F32),
                                        ALU.subtract).then_inc(cond_ready, 1)
                self.split(0)
                self.split(1)

            def ada(self, l):
                n, e = self.n, self.e

                def out_(j, at, turned_):
                    e.wait_ge(mod_turned, turned_)
                    nc.vector.tensor_copy(mod[:, bass.ds(2 * at, 2), :],
                                          bank[4 + j % 2][:, 0:4].rearrange("p (j s) -> p j s", s=2)).then_inc(mod_out, 1)

                def finish(j, at):
                    if j >= 2:
                        out_(j - 2, at - 2, n("adas", -1))
                    n.add("adas", 1)
                    for i, s in enumerate((1, 0)):
                        if j == ADA_NORM + 5 * i + 4:
                            self.mean_square(s, bank[6])
                self.stream(24, None, dict(adas=1), 24 - ADA_NORM, finish)
                for j in (22, 23):
                    out_(j, j, n("adas", j - 23))
                n.add("drained_act", 24)

            def modulation(self, l):
                n, e = self.n, self.e
                e.wait_ge(bias_turned, l + 1)
                e.wait_ge(mod_out, n("adas"))
                self.order(nc.vector.tensor_tensor(mod[:], mod[:], bank[3][:, 0:6 * KT].unsqueeze(2).broadcast_to([P, 6 * KT, 2]), ALU.add))
                e.wait_ge(params_in, params_until("params", l))
                for i in range(2):
                    sc = mod[:, 8 + 24 * i:16 + 24 * i, :]
                    self.order(nc.vector.tensor_scalar(mscale[:, i], sc, 1.0, None, ALU.add))
                    self.order(nc.vector.tensor_tensor(mscale[:, i], mscale[:, i],
                                                       norm_g[:, i, :].unsqueeze(2).broadcast_to([P, KT, 2]), ALU.mult))
                n.add("mod", 1)

            def up(self, kind, count, w):
                n, e = self.n, self.e
                if kind == "relu2":
                    def drain(j, at):
                        e.wait_ge(drained_act, n("drained_act", 1))
                        self.order(nc.vector.tensor_tensor(fb[:, j % 2, :], fa[:, j % 2, :], fa[:, j % 2, :], ALU.mult))

                    def finish(j, at):
                        n.add("drained_act", 1)
                        n.add("hidden", 1)
                        e.wait_ge(squared, n("squared", 1))
                        n.add("squared", 1)
                        nc.vector.tensor_tensor(hid_lo[:, bass.ds(at * 2, 2), :], tiles(fb[:, j % 2, :], 2),
                                                hid_hi[:, bass.ds(at * 2, 2), :].bitcast(F32), ALU.subtract).then_inc(hidden, 1)
                    self.stream(count, drain, dict(drained_act=1, hidden=1, squared=1, dve_order=1), finish=finish)
                else:
                    def drain(j, at):
                        ex, b, f = fa[:, j % 2, 0:NT], bank[j % 4], fb[:, j % 2, 0:NT]
                        e.wait_ge(gate_exp, n("silus", 1))
                        self.order(nc.vector.reciprocal(ex, ex))
                        self.order(nc.vector.tensor_tensor(ex, b[:, 0:NT], ex, ALU.mult))
                        nc.vector.tensor_tensor(f, b[:, NT:2 * NT], ex, ALU.mult).then_inc(gated, 1)

                    def finish(j, at):
                        f = fb[:, j % 2, 0:NT]
                        n.add("silus", 1)
                        n.add("hidden", 1)
                        n.add("gated", 1)
                        e.wait_ge(gate_hi, n("silus"))
                        nc.vector.tensor_tensor(hid_lo[:, bass.ds(at, 1), :], tiles(f, 1),
                                                hid_hi[:, bass.ds(at, 1), :].bitcast(F32), ALU.subtract).then_inc(hidden, 1)
                    self.stream(count, drain, dict(silus=1, hidden=1, gated=1, dve_order=2), finish=finish)

            def down(self, kind, count, w, s, gate, norm_next):
                n, e = self.n, self.e

                def finish(j, at):
                    c = j - (count - WIDE)
                    if c < 0:
                        return
                    e.wait_ge(multiplied, n("halves", 2))
                    for d in (2 * c, 2 * c + 1):
                        x = residual[:, d, s * NT:(s + 1) * NT]
                        src = tiles(bank[4 + c][:], 2)[:, d % 2, :]
                        if gate is None:
                            nc.vector.tensor_tensor(x, src, x, ALU.add).then_inc(residual_new, 1)
                        else:
                            nc.vector.scalar_tensor_tensor(x, src, mod[:, gate + d, s:s + 1], x, ALU.mult, ALU.add).then_inc(residual_new, 1)
                self.stream(count, None, None, WIDE, finish, True)
                n.add("residual", KT)

            def mean_square(self, s, b):
                n, e = self.n, self.e
                n.add("sum", 1)
                e.wait_ge(sums, n("sum"))
                at = NORM_AT + TT * s
                nc.vector.tensor_scalar(variance[:, at:at + TT], b[:, 0:TT], 1.0 / D, EPS, ALU.mult, ALU.add).then_inc(var_ready, 1)
                n.add("pow", 1)

            def norm(self, s, b, which, summed, l):
                n, e = self.n, self.e
                if summed:
                    self.mean_square(s, bank[0])
                e.wait_ge(rstd_ready, n("pow"))
                at = NORM_AT + TT * s
                for t in range(TT):
                    ins = nc.vector.tensor_scalar(diag[:, t, :], ident, rstd[:, at + t:at + t + 1], None, ALU.mult)
                ins.then_inc(rstd_diag, 1)
                if summed:
                    self.catch_up()
                e.wait_ge(rstd_wide, n("norm", 1))

                def low(k):
                    e.wait_ge(norm_hi, KT * n("norm") + k + 1)
                    o, x, hi = act_lo[:, k, :], wide[:, k, :], act_hi[:, k, :].bitcast(F32)
                    if b == 1:
                        ins = nc.vector.scalar_tensor_tensor(o, x, mod[:, 24 * which + k, s:s + 1], hi, ALU.add, ALU.subtract)
                    else:
                        ins = nc.vector.tensor_tensor(o, x, hi, ALU.subtract)
                    ins.then_inc(norm_lo, 1)
                for k in range(KT):
                    scale = mscale[:, which, k, s:s + 1] if b == 1 else norm2_g[:, l, which, k:k + 1]
                    nc.vector.scalar_tensor_tensor(wide[:, k, :], residual[:, k, s * NT:(s + 1) * NT], scale, bank[1][:, 0:NT],
                                                   ALU.mult, ALU.mult).then_inc(modulated, 1)
                    if k:
                        low(k - 1)
                low(KT - 1)
                self.catch_up()
                n.add("norm", 1)

            def mix_out(self, b, k):
                n, e = self.n, self.e
                n.add("mix", 1)
                e.wait_ge(mix_hi, n("mix"))
                nc.vector.tensor_tensor(act_lo[:, k:k + 2, :], tiles(b, 2), act_hi[:, k:k + 2, :].bitcast(F32),
                                        ALU.subtract).then_inc(mix_lo, 1)

            def power(self):
                self.n.add("pow", 1)
                self.e.wait_ge(rstd_ready, self.n("pow"))

            def tables(self, b, cos_g, sin_g, gain):
                kinds = gain.shape[1]
                cos, sin = rope[b]
                nc.vector.tensor_tensor(cos_g[:], cos.unsqueeze(1).broadcast_to([P, kinds, TT, DH]),
                                        gain.unsqueeze(2).broadcast_to([P, kinds, TT, DH]), ALU.mult)
                axes = 2 if b == 1 else 1
                w = DH // axes // 2
                for a in range(axes):
                    for half in range(2):
                        lo, other = (2 * a + half) * w, (2 * a + 1 - half) * w
                        ins = nc.vector.tensor_tensor(
                            sin_g[:, :, :, lo:lo + w], sin[:, :, lo:lo + w].unsqueeze(1).broadcast_to([P, kinds, TT, w]),
                            gain[:, :, other:other + w].unsqueeze(2).broadcast_to([P, kinds, TT, w]), ALU.mult)
                ins.then_inc(tables_ready, 1)

            def rows(self, plan, w, l):
                n, e = self.n, self.e
                roped = [c["heads"] for c in plan if "heads" in c]
                block2 = roped[0]["block"] == 2
                k0 = n.static("drained_act")
                m0 = n.static("head_squares")
                if block2:
                    self.tables(2, cos_g2, sin_g2, gains2[:, l].rearrange("p i k d -> p (i k) d"))
                else:
                    self.tables(1, cos_g1, sin_g1, tiles(gains1[:, 0:2 * DH], 2))
                n.add("tables", 1)
                e.wait_ge(tables_ready, n("tables"))
                sines = {}
                norms = []

                def scratch_of(h, name, r):
                    return heads_of(tiles(h[name][:, r % 2, 0:TT * h["n"] * DH], TT))

                def first_half(j):
                    h, m = roped[j], n.static("head_squares") - m0
                    heads = h["n"]
                    if h["normed"]:
                        at = 16 * (m % 2)
                        e.wait_ge(head_squares, n("head_squares", 1))
                        v = variance[:, at:at + TT * heads]
                        self.order(nc.vector.tensor_reduce(v.rearrange("p (t h) -> p t h", t=TT), scratch_of(h, "sq", m), AX.X, ALU.add))
                        nc.vector.tensor_scalar(v, v, 1.0 / DH, EPS, ALU.mult, ALU.add).then_inc(var_ready, 1)
                        n.add("head_squares", 1)
                        n.add("pow", 1)
                        norms.append((at, n.static("pow")))
                    else:
                        norms.append(None)
                    e.wait_ge(drained_act, k0 + j + 1)
                    if h["sin"] is None:
                        return
                    if j >= 2:
                        e.wait_ge(rows_ready, n("rows", j - 1))
                    x, t2, sin, wd = h["x"], scratch_of(h, "b", j), h["sin"], DH // h["axes"] // 2
                    if h["axes"] == 1:
                        for half in range(2):
                            lo, other = half * wd, (1 - half) * wd
                            ins = nc.vector.tensor_tensor(t2[:, :, :, lo:lo + wd], x[:, :, :, other:other + wd],
                                                          sin[:, :, lo:lo + wd].unsqueeze(2).broadcast_to([P, TT, heads, wd]), ALU.mult)
                    else:
                        for t in range(TT):
                            xv, tv = (v[:, t].rearrange("p h (a b w) -> p h a b w", b=2, w=wd) for v in (x, t2))
                            sv = sin[:, t].rearrange("p (a b w) -> p a b w", b=2, w=wd)
                            for half in range(2):
                                ins = nc.vector.tensor_tensor(tv[:, :, :, half], xv[:, :, :, 1 - half],
                                                              sv[:, :, half].unsqueeze(1).broadcast_to([P, heads, 2, wd]), ALU.mult)
                    ins.then_inc(dve_order, 1)
                    n.add("dve_order", 1)
                    sines[j] = n.static("dve_order")

                def second_half(r):
                    h, t1, t2 = roped[r], scratch_of(roped[r], "a", r), scratch_of(roped[r], "b", r)
                    e.wait_ge(rope_cos, n("rope", 1))
                    n.add("rope", 1)
                    if h["sin"] is not None:
                        e.wait_ge(dve_order, sines[r])
                    if h["sin"] is not None and norms[r]:
                        self.order(nc.vector.tensor_tensor(t1, t1, t2, ALU.add))
                    if norms[r]:
                        at, value = norms[r]
                        e.wait_ge(rstd_ready, value)
                        f = rstd[:, at:at + TT * h["n"]].rearrange("p (t h) -> p t h", t=TT).unsqueeze(3).broadcast_to([P, TT, h["n"], DH])
                    for d in h["dst"]:
                        ins = nc.vector.tensor_tensor(d, t1, f, ALU.mult) if norms[r] else nc.vector.tensor_tensor(d, t1, t2, ALU.add)
                    ins.then_inc(rows_ready, 1)

                def gelu_a(c, j):
                    g = c["gelu"]
                    x = proj1[:, :, U1 + 256 * g:U1 + 256 * (g + 1)]
                    t = gtmp[:, :, 256 * g:256 * (g + 1)]
                    e.wait_ge(drained_act, k0 + j + 1)
                    self.order(nc.vector.tensor_tensor(t, x, x, ALU.mult))
                    self.order(nc.vector.tensor_scalar(t, t, 0.044715, 1.0, ALU.mult, ALU.add))
                    nc.vector.tensor_tensor(t, t, x, ALU.mult).then_inc(gelu_in, 1)

                def gelu_b(c):
                    g = c["gelu"]
                    t = gtmp[:, :, 256 * g:256 * (g + 1)]
                    n.add("gelus", 1)
                    e.wait_ge(gelu_tanh, n("gelus"))
                    self.order(nc.vector.tensor_scalar(t, t, 1.0, 0.5, ALU.add, ALU.mult))
                    o = gates[:, :, 256 * g:256 * (g + 1)]
                    self.order(nc.vector.tensor_tensor(o, t, proj1[:, :, U1 + 256 * g:U1 + 256 * (g + 1)], ALU.mult))
                    if g:
                        self.order(nc.vector.tensor_tensor(t, o, o, ALU.mult))
                        v = variance[:, 32:32 + 4 * TT]
                        self.order(nc.vector.tensor_reduce(v.rearrange("p (t h) -> p t h", t=TT), heads_of(t), AX.X, ALU.add))
                        nc.vector.tensor_scalar(v, v, 1.0 / DH, EPS, ALU.mult, ALU.add).then_inc(var_ready, 1)

                def drain(j, at):
                    if j < len(roped):
                        first_half(j)
                    if "gelu" in plan[j]:
                        gelu_a(plan[j], j)

                def finish(j, at):
                    if 0 <= j - 1 < len(roped):
                        second_half(j - 1)
                    if 0 < j <= len(plan) and "gelu" in plan[j - 1]:
                        gelu_b(plan[j - 1])
                    if not block2:
                        return
                    if j == 3:
                        self.order(nc.vector.tensor_scalar(proj2[:, :, IW:IW + IH], proj2[:, :, IW:IW + IH],
                                                           float(np.float32(IH ** -0.5)), None, ALU.mult))
                    if INDEX_AT <= j < INDEX_AT + 8:
                        for i in range(2 * (j - INDEX_AT), 2 * (j - INDEX_AT) + 2):
                            self.index_score(i)
                    if j >= SEARCH_AT:
                        for _ in range(2):
                            self.search(0)

                self.round = [0, 0]
                self.stream(len(plan), drain, None, len(plan), finish)
                for j in range(len(plan), len(roped) + 1):
                    finish(j, j)
                n.add("rows", len(roped))
                n.add("drained_act", len(plan))

            def index_score(self, i):
                n, e = self.n, self.e
                t, h = divmod(i, IH)
                wd = (t + 1) * P
                n.add("logits", 1)
                e.wait_ge(logit_relu, n("logits"))
                wt, sc = proj2[:, t, IW + h:IW + h + 1], score[:, t, 0:wd]
                if h == 0:
                    ins = nc.vector.tensor_scalar(sc, relu_t[:, i % 2, 0:wd], wt, None, ALU.mult)
                else:
                    ins = nc.vector.scalar_tensor_tensor(sc, relu_t[:, i % 2, 0:wd], wt, sc, ALU.mult, ALU.add)
                ins.then_inc(logit_used, 1)
                e.wait_ge(logit_used, n("logits"))
                if h == IH - 1:
                    self.order(nc.vector.tensor_tensor(sc, sc, causal(t), ALU.add))

            def search(self, t):
                sc = score[:, t, 0:(t + 1) * P]
                self.order(nc.vector.max(best[:], sc))
                self.order(nc.vector.match_replace(sc, best[:], sc, TAKEN))
                self.round[t] += 1
                if self.round[t] == TOPK // 8:
                    self.order(nc.vector.tensor_scalar(sc, sc, TAKEN / 2, MASKED, ALU.is_gt, ALU.mult))
                    nc.vector.tensor_tensor(seen[:, t, 0:(t + 1) * P], sc, causal(t), ALU.add).then_inc(seen_ready, 1)

            def attention(self, items, probs, ring, beside, l=0):
                n, e = self.n, self.e
                s0, i0 = n.static("scores"), n.static("items")
                first = [0]
                for it in items:
                    first.append(first[-1] + len(it["scores"]))

                slots = probs.shape[1]

                def maxima(j):
                    if j >= len(items):
                        return
                    for s in range(first[j], first[j + 1]):
                        width = items[j]["keys"] * P
                        e.wait_ge(scored, s0 + s + 1)
                        nc.vector.tensor_reduce(neg_max[:, s:s + 1], bank[s % ring][:, 0:width], AX.X, ALU.max,
                                                negate=True).then_inc(max_ready, 1)

                def out_(j):
                    done = items[j]["done"] if j >= 0 else None
                    if done and isinstance(done[1], tuple):
                        e.wait_ge(mixed, i0 + j + 1)
                        nc.vector.tensor_copy(diff_rows[:, done[1][1], :], bank[done[0]][:]).then_inc(diff_drained, 1)
                    elif done:
                        self.mix_out(bank[done[0]][:], done[1])
                maxima(0)
                maxima(1)
                for j, it in enumerate(items):
                    s = first[j]
                    width = it["keys"] * P
                    a, b = probs[:, s % slots, 0:width], probs[:, (s + 1) % slots, 0:width]
                    e.wait_ge(exped, s0 + first[j + 1])
                    if it.get("diff"):
                        self.order(nc.vector.reciprocal(total[:, s:s + 2], total[:, s:s + 2]))
                        self.order(nc.vector.tensor_tensor(total[:, s + 1:s + 2], total[:, s + 1:s + 2], lam[:, l, 4:5], ALU.mult))
                        self.order(nc.vector.tensor_scalar(b, b, total[:, s + 1:s + 2], None, ALU.mult))
                        nc.vector.scalar_tensor_tensor(a, a, total[:, s:s + 1], b, ALU.mult, ALU.subtract).then_inc(prob_ready, 1)
                    else:
                        self.order(nc.vector.reciprocal(total[:, s:s + 1], total[:, s:s + 1]))
                        nc.vector.tensor_scalar(a, a, total[:, s:s + 1], None, ALU.mult).then_inc(prob_ready, 1)
                    maxima(j + 2)
                    beside(j)
                    out_(j - 2)
                out_(len(items) - 2)
                out_(len(items) - 1)
                n.add("scores", first[-1])
                n.add("items", len(items))

            def attend1(self, s):
                n, e = self.n, self.e

                def beside(j):
                    gv = gates[:, :, 256:512]
                    if j == 1:
                        self.power()
                        f = rstd[:, 32:32 + 4 * TT].rearrange("p (t h) -> p t h", t=TT).unsqueeze(3).broadcast_to([P, TT, 4, DH])
                        self.order(nc.vector.tensor_tensor(heads_of(gv), heads_of(gv), f, ALU.mult))
                    if j == 2:
                        nc.vector.tensor_tensor(gv, gv, gains1[:, 2 * DH:].unsqueeze(1).broadcast_to([P, TT, 256]),
                                                ALU.mult).then_inc(gates_ready, 1)
                    if j == DFT_OUT + 1:
                        self.mix_out(bank[3][:], 4)
                    if j == SPATIAL:
                        e.wait_ge(spatial, n("gmlp", 1))
                        for h in range(4):
                            u = gates[:, :, h * DH:(h + 1) * DH]
                            ins = nc.vector.scalar_tensor_tensor(u, tiles(bank[3][:, h * P:(h + 1) * P], TT), b_sp[:, h:h + 1], u,
                                                                 ALU.add, ALU.mult)
                        ins.then_inc(gates_ready, 1)
                    if j == GATE_OUT + 1:
                        self.mix_out(bank[3][:], 6)
                self.attention(items1(s), probs1, 3, beside)
                n.add("fourier", 1)
                n.add("gmlp", 1)
                n.add("turned", 1)

            def params2(self, l):
                super().params2(l)
                n, e = self.n, self.e
                e.wait_ge(params2_in, 96 * DEPTH)
                lv = lam_in[:, l].rearrange("p (a b d) -> p a b d", a=2, b=2)
                self.order(nc.vector.tensor_tensor(lv[:, :, 0, :], lv[:, :, 0, :], lv[:, :, 1, :], ALU.mult))
                nc.vector.tensor_reduce(lam[:, l, 0:2], lv[:, :, 0, :], AX.X, ALU.add).then_inc(lam_sums, 1)
                e.wait_ge(lam_exp, l + 1)
                init = 0.8 - 0.6 * float(np.exp(-0.3 * l))
                self.order(nc.vector.tensor_tensor(lam[:, l, 4:5], lam[:, l, 2:3], lam[:, l, 3:4], ALU.subtract))
                self.order(nc.vector.tensor_scalar(lam[:, l, 4:5], lam[:, l, 4:5], init, None, ALU.add))
                self.order(nc.vector.tensor_scalar(sub_g[:, l], sub_g[:, l], 1.0 - init, None, ALU.mult))

            def attend2(self, l):
                n, e = self.n, self.e

                def norm_rows(t, part):
                    x = tiles(diff_rows[:, t, :], 4)
                    v = variance[:, 8 * t:8 * t + 4]
                    if part == 0:
                        e.wait_ge(diff_squares, TT * l + t + 1)
                        nc.vector.tensor_scalar(v, v, 1.0 / (2 * DH), EPS, ALU.mult, ALU.add).then_inc(var_ready, 1)
                        return
                    self.power()
                    for h in range(4):
                        ins = nc.vector.scalar_tensor_tensor(x[:, h], x[:, h], rstd[:, 8 * t + h:8 * t + h + 1], sub_g[:, l],
                                                             ALU.mult, ALU.mult)
                    ins.then_inc(rows_ready, 1)

                def beside(j):
                    if j < TOPK // 8:
                        self.search(1)
                    for t in range(TT):
                        for part in range(2):
                            if j == DIFF_NORM + 4 * t + 1 + part:
                                norm_rows(t, part)
                self.attention(items2(), probs2, 4, beside, l)
                n.add("rows", TT)
                for t in range(TT):
                    self.mix_out(bank[4 + t][:], 2 + 2 * t)

        class Tensor(Phases):
            def three(self, o, w, x, first):
                for i, (a, b) in enumerate(((0, 0), (0, 1), (1, 0))):
                    ins = nc.tensor.matmul(o, w[a], x[b], start=first and i == 0, stop=True, skip_group_check=True)
                return ins

            def stream(self, count, multiply, free=None, extra=None, tail=0, after=None):
                n, e = self.n, self.e

                def body(j, at):
                    if free is not None and (j >= 4 or n.it is not None):
                        e.wait_ge(free[0], n(free[1], -3))
                    for h in range(2):
                        e.wait_ge(lo_ready, n("halves", h + 1))
                        slot = (2 * n.static("chunks") + h) % SPLIT
                        multiply(j, at, h, w_hi[:, slot, :], w_lo[:, slot, :]).then_inc(multiplied, 1)
                    n.add("chunks", 1)
                    n.add("halves", 2)
                    if free is not None:
                        n.add(free[1], 1)
                    if after:
                        after(j, at)

                per = dict(chunks=1, halves=2, **(extra or {}))
                if free is not None:
                    per[free[1]] = 1
                run_chunks(e, n, count, per, body, tail, 4 if free is not None else 1)

            def load(self):
                n, e = self.n, self.e
                e.wait_ge(inputs_in, 32)
                e.wait_ge(consts_in, 16)
                e.wait_ge(preset, 2)
                for k in range(KT):
                    for t in range(2 * TT):
                        ins = nc.tensor.transpose(bank[k][:, t * P:(t + 1) * P], rows_in[:, t, k * P:(k + 1) * P], ident)
                    ins.then_inc(turned, 1)
                n.add("turned", 8)
                e.wait_ge(turned_out, 8)
                e.wait_ge(cond_ready, 1)

            def ada(self, l):
                n, e = self.n, self.e

                def multiply(j, at, h, hi, lo):
                    for k in range(4):
                        for i, w in enumerate((hi, lo)):
                            ins = nc.tensor.matmul(bank[j % 4][:, 0:CW], cond[:, 4 * h + k, :], tiles(w, 4)[:, k, :],
                                                   start=h == 0 and k == 0 and i == 0, stop=True, skip_group_check=True)
                    return ins

                def turn_rows(slot, lag, copied):
                    e.wait_ge(drained_act, n("drained_act", -lag))
                    if copied is not None:
                        e.wait_ge(mod_out, copied)
                    for i in range(2):
                        ins = nc.tensor.matmul(bank[4 + slot % 2][:, 2 * i:2 * i + 2], mod_rows[:, slot, i * P:(i + 1) * P],
                                               sel[0:4, :], start=True, stop=True, skip_group_check=True)
                    ins.then_inc(mod_turned, 1)

                def after(j, at):
                    if j >= 2:
                        turn_rows((j - 2) % 4, 2, n("adas", -3) if j >= 4 else None)
                    n.add("adas", 1)
                    if j in (ADA_NORM + 2, ADA_NORM + 7):
                        self.sum_up(bank[6])
                self.stream(24, multiply, (drained_act, "drained_act"), dict(adas=1), 24 - ADA_NORM, after)
                turn_rows(22 % 4, 1, n("adas", -3))
                turn_rows(23 % 4, 0, n("adas", -2))
                e.wait_ge(params_in, params_until("bias", l))
                nc.tensor.transpose(bank[3][:, 0:6 * KT], bias_rows[:], ident[0:6 * KT, 0:6 * KT]).then_inc(bias_turned, 1)

            def up(self, kind, count, w):
                n, e = self.n, self.e

                def multiply(j, at, h, hi, lo):
                    for k in range(4):
                        if j == 0:
                            e.wait_ge(norm_lo, KT * (n("norm") - 1) + 4 * h + k + 1)
                        x = [a[:, 4 * h + k, :] for a in (act_hi, act_lo)]
                        for t in range(2):
                            ins = self.three(tiles(bank[j % 4][:], 2)[:, t, :], [tiles(v, 4)[:, k, t * P:(t + 1) * P] for v in (hi, lo)],
                                             x, h == 0 and k == 0 and t == 0)
                    return ins
                self.stream(count, multiply, (drained_act, "drained_act") if kind == "relu2" else (gated, "gated"))
                n.add("hidden", count)

            def down(self, kind, count, w, s, gate, norm_next):
                n, e = self.n, self.e
                src = (act_hi, act_lo) if kind == "mix" else (hid_hi, hid_lo)
                last_hidden = KT if gate is None else KT // 2

                def multiply(j, at, h, hi, lo):
                    if j == 0 and kind == "mix":
                        e.wait_ge(mix_lo, n("mix", h - 1))
                    c = j - (count - WIDE)
                    if kind == "hidden" and h == 0 and j == 0:
                        e.wait_ge(hidden, n("hidden", 1 - last_hidden))
                    if kind == "hidden" and h == 0 and c == 0:
                        e.wait_ge(hidden, n("hidden"))
                    if c < 0:
                        x = [a[:, bass.ds(at * 2 + h, 1), :] for a in src]
                        for d in range(KT):
                            ins = self.three(tiles(bank[4 + d // 2][:], 2)[:, d % 2:d % 2 + 1, :], [v[:, d * P:(d + 1) * P] for v in (hi, lo)],
                                             x, j == 0 and h == 0 and d % 2 == 0)
                        return ins
                    for k in range(4):
                        if kind == "mix" and gate is not None and j == 0 and k == 2:
                            e.wait_ge(mix_lo, n("mix"))
                        x = [a[:, 2 * count - KT + 4 * h + k, :] for a in src]
                        for t in range(2):
                            ins = self.three(tiles(bank[4 + c][:], 2)[:, t, :], [tiles(v, 4)[:, k, t * P:(t + 1) * P] for v in (hi, lo)],
                                             x, count == WIDE and h == 0 and k == 0 and t == 0)
                    return ins
                self.stream(count, multiply, tail=WIDE)
                n.add("residual", KT)

            def sum_up(self, b):
                n, e = self.n, self.e
                for i, k in enumerate((0, KT - 2, KT - 1)):
                    if i == 0:
                        e.wait_ge(folded, 3 * (n("sum") + 1))
                    else:
                        e.wait_ge(squares, 5 * n("sum") + 3 + i)
                    for t in range(TT):
                        ins = nc.tensor.matmul(b[:, t:t + 1], wide[:, k, t * P:(t + 1) * P], ones[:, 0:1],
                                               start=i == 0 and t == 0, stop=True, skip_group_check=True)
                ins.then_inc(sums, 1)
                n.add("sum", 1)

            def norm(self, s, b, which, summed, l):
                n, e = self.n, self.e
                if summed:
                    self.sum_up(bank[0])
                e.wait_ge(rstd_diag, n("norm", 1))
                nc.tensor.matmul(bank[1][:, 0:NT], ones[:], diag[:].rearrange("p t n -> p (t n)"), start=True, stop=True).then_inc(rstd_wide, 1)
                n.add("norm", 1)

            def turn(self, b, srcs, wait=True):
                n, e = self.n, self.e
                if wait:
                    e.wait_ge(turned_out, n("turned", -1))
                for i, x in enumerate(srcs):
                    ins = nc.tensor.transpose(b[:, i * P:(i + 1) * P], x, ident)
                ins.then_inc(turned, 1)
                n.add("turned", 1)

            def rows(self, plan, w, l):
                n, e = self.n, self.e
                roped = [c["heads"] for c in plan if "heads" in c]

                def multiply(j, at, h, hi, lo):
                    wd = plan[j]["wd"]
                    for k in range(4):
                        if j == 0:
                            e.wait_ge(norm_lo, KT * (n("norm") - 1) + 4 * h + k + 1)
                        for t in range(TT):
                            x = [a[:, 4 * h + k, t * P:(t + 1) * P] for a in (act_hi, act_lo)]
                            ins = self.three(tiles(bank[j % 4][:], TT)[:, t, 0:wd], x,
                                             [tiles(v, 4)[:, k, 0:wd] for v in (hi, lo)], h == 0 and k == 0 and t == 0)
                    return ins

                def after(j, at):
                    if 0 <= j - 2 < len(roped):
                        e.wait_ge(rows_ready, n("rows", 1))
                        n.add("rows", 1)
                        self.turn(bank[4 + (j - 2) % 2], roped[j - 2]["turn"])
                    if roped[0]["block"] == 2 and INDEX_AT <= j < INDEX_AT + 8:
                        for i in range(2 * (j - INDEX_AT), 2 * (j - INDEX_AT) + 2):
                            t, h = divmod(i, IH)
                            wd = (t + 1) * P
                            if i == 0:
                                e.wait_ge(turned_out, n("turned") - (j - 1) + 3)
                            if i >= 2:
                                e.wait_ge(logit_relu, n("logits", -1))
                            nc.tensor.matmul(bank[6 + i % 2][:, 0:wd], pair("iq", h, t * P, wd),
                                             pairs_t[DH * (h % 2):DH * (h % 2) + DH, PAIR["ik"], 0:wd], start=True, stop=True).then_inc(logit_full, 1)
                            n.add("logits", 1)

                self.stream(len(plan), multiply, (drained_act, "drained_act"), tail=len(plan), after=after)
                for j in range(len(plan), len(roped) + 2):
                    after(j, j)

            def attention(self, items, probs, probs_t, ring=4, beside={}):
                n, e = self.n, self.e
                s0, i0 = n.static("scores"), n.static("items")
                first = [0]
                for it in items:
                    first.append(first[-1] + len(it["scores"]))

                slots = probs.shape[1]

                def score_(j):
                    if j >= len(items):
                        return
                    for i, (q, k, m) in enumerate(items[j]["scores"]):
                        s = first[j] + i
                        width = items[j]["keys"] * P
                        if s >= ring:
                            e.wait_ge(exped, s0 + s - ring + 1)
                        if j == 16 + i and len(items) > 16:
                            e.wait_ge(seen_ready, TT * (n("index") + 1))
                        o = bank[s % ring][:, 0:width]
                        ins = nc.tensor.matmul(o, q, k, start=True, stop=m is None)
                        if m is not None:
                            ins = nc.tensor.matmul(bank[s % ring][:, width - m.shape[-1]:width], ident_b[:], m, start=False, stop=True)
                        ins.then_inc(scored, 1)

                def values(j):
                    if j < 0:
                        return
                    it = items[j]
                    e.wait_ge(prob_t, i0 + j + 1)
                    if len(items) > 16 and j == 12:
                        e.wait_ge(mix_lo, n("mix", 1))
                    if len(items) > 16 and j == 16:
                        e.wait_ge(diff_drained, TT * n("index") + 1)
                    for k, v in enumerate(it["v"]):
                        pt = probs_t[:, j % 3, k, :]
                        a, b = (pt, v) if it.get("diff") else (v, pt)
                        ins = nc.tensor.matmul(it["o"], a, b, start=k == 0, stop=k == it["keys"] - 1)
                    ins.then_inc(mixed, 1)
                score_(0)
                score_(1)
                for j, it in enumerate(items):
                    score_(j + 2)
                    values(j - 2)
                    if j in beside:
                        beside[j]()
                    e.wait_ge(prob_ready, i0 + j + 1)
                    if j >= 2:
                        e.wait_ge(prob_t, i0 + j - 1)
                    s = first[j]
                    for k in range(it["keys"]):
                        ins = nc.tensor.transpose(bank[4 + j % 2][:, k * P:(k + 1) * P], probs[:, s % slots, k * P:(k + 1) * P], ident)
                    ins.then_inc(prob_turned, 1)
                values(len(items) - 2)
                values(len(items) - 1)
                n.add("scores", first[-1])
                n.add("items", len(items))

            def attend1(self, s):
                self.e.wait_ge(turned_out, self.n("turned"))
                self.e.wait_ge(v_kept, self.n("heads", 1))
                self.n.add("heads", 1)
                n, e = self.n, self.e

                def spectrum(i):
                    if i == 0:
                        e.wait_ge(drained_act, n("drained_act"))
                    else:
                        e.wait_ge(dft_out, 2 * n("fourier") + 1)
                    for t in range(TT):
                        ins = nc.tensor.matmul(bank[3][:], proj1[:, t, F1 + i * P:F1 + (i + 1) * P], dft_n[:, t, :],
                                               start=t == 0, stop=t == TT - 1)
                    ins.then_inc(dft_full, 1)

                def fourier():
                    e.wait_ge(dft_out, 2 * n("fourier") + 2)
                    for i in range(2):
                        o = bank[3][:, i * NT:(i + 1) * NT]
                        nc.tensor.matmul(o, cols["dft_c"], four[:, i, 0:NT], start=True, stop=False)
                        ins = nc.tensor.matmul(o, cols["dft_s"], four[:, i, NT:2 * NT], start=False, stop=True)
                    ins.then_inc(mix_full, 1)

                def turn_w():
                    e.wait_ge(mix_lo, n("mix", 1))
                    self.turn(bank[3], [w_sp[:, h, :] for h in range(4)])

                def gate():
                    e.wait_ge(turned_out, n("turned"))
                    e.wait_ge(gates_ready, 2 * n("gmlp") + 1)
                    for h in range(4):
                        ins = nc.tensor.matmul(bank[3][:, h * P:(h + 1) * P], w_sp_t[:, h, :],
                                               gates[:, :, 256 + h * DH:256 + (h + 1) * DH], start=True, stop=True)
                    ins.then_inc(spatial, 1)

                def turn_gated():
                    e.wait_ge(gates_ready, 2 * n("gmlp") + 2)
                    for i in range(2):
                        for t in range(TT):
                            ins = nc.tensor.transpose(bank[3][:, (2 * i + t) * P:(2 * i + t + 1) * P], gates[:, t, i * P:(i + 1) * P], ident)
                    ins.then_inc(mix_full, 1)
                self.attention(items1(s), probs1, probs_t1, 3, {
                    DFT0: lambda: spectrum(0), DFT1: lambda: spectrum(1), DFT_OUT: fourier,
                    TURN_W: turn_w, SPATIAL: gate, GATE_OUT: turn_gated})
                n.add("fourier", 1)
                n.add("gmlp", 1)
                n.add("mix", 4)

            def attend2(self, l):
                n, e = self.n, self.e
                e.wait_ge(turned_out, n("turned"))
                e.wait_ge(drained_act, n("drained_act"))
                self.attention(items2(), probs2, probs_t2)
                n.add("index", 1)
                e.wait_ge(prob_t, n("items"))
                for t in range(TT):
                    e.wait_ge(rows_ready, n("rows", TT))
                    for j in range(2):
                        for q in range(TT):
                            h = 2 * t + j
                            ins = nc.tensor.transpose(bank[4 + t][:, (2 * j + q) * P:(2 * j + q + 1) * P],
                                                      diff_rows[:, q, h * P:(h + 1) * P], ident)
                    ins.then_inc(mix_full, 1)
                n.add("rows", TT)
                n.add("mix", 4)

            def finish(self):
                n, e = self.n, self.e
                for i in range(2):
                    e.wait_ge(residual_new, n("residual", 4 * (i - 1)))
                    for t in range(TT):
                        for k in range(4):
                            ins = nc.tensor.transpose(bank[i + 2 * t][:, k * P:(k + 1) * P],
                                                      residual[:, 4 * i + k, t * P:(t + 1) * P], ident)
                        ins.then_inc(turned, 1)
                        n.add("turned", 1)

        counter = Phases(None)
        program(counter)
        TOTAL[0] = counter.n.static("chunks")

        @block.sync
        def _(eng):
            program(Sync(eng))

        @block.gpsimd
        def _(eng):
            program(Pool(eng))

        @block.scalar
        def _(eng):
            program(Scalar(eng))

        @block.vector
        def _(eng):
            program(Vector(eng))

        @block.tensor
        def _(eng):
            program(Tensor(eng))


def kernel(**inputs):
    import numpy as _np
    import concourse.bacc as _bacc
    from concourse import mybir as _mybir
    from concourse.bass_utils import run_bass_kernel_spmd as _run

    nc = _bacc.Bacc("TRN2", target_bir_lowering=False, num_devices=1)
    arrays, aps = {}, {}
    for name, a in inputs.items():
        a = _np.ascontiguousarray(a)
        arrays[f"in_{name}"] = a
        aps[name] = nc.dram_tensor(f"in_{name}", a.shape, _mybir.dt.from_np(a.dtype), kind="ExternalInput").ap()
    arrays["consts"] = constant_table()
    consts = nc.dram_tensor("consts", arrays["consts"].shape, F32, kind="ExternalInput").ap()
    out = nc.dram_tensor("out", (1, NT, D), F32, kind="ExternalOutput").ap()
    build(nc, aps, consts, out)
    return _run(nc, [arrays], core_ids=[0]).results[0]["out"]
```
